# Optimizing a Trainium2 kernel written in Bass

```python
import jax, jax.numpy as jnp
from jax import lax
import numpy as np

D_MODEL = 1024
BATCH = 1
SEQ = 256
DEPTH = 2

CHUNK = 64
N_META = 16
N_PAD = CHUNK - N_META
N_MIXERS = 2
RMS_EPS = 1e-6
L2_EPS = 1e-6

GDN_QK_HEADS = 8
GDN_V_HEADS = 16
GDN_HEAD_DIM = 128
GDN_CONV = 4
GDN_KEY_DIM = GDN_QK_HEADS * GDN_HEAD_DIM
GDN_VAL_DIM = GDN_V_HEADS * GDN_HEAD_DIM
GDN_QKV_DIM = 2 * GDN_KEY_DIM + GDN_VAL_DIM
GDN_IN = GDN_QKV_DIM + GDN_VAL_DIM + 2 * GDN_V_HEADS

ML_HEADS = 4
ML_QK_DIM = 128
ML_V_DIM = 256
ML_GATE_CAP = 15.0
ML_QK_TOT = ML_HEADS * ML_QK_DIM
ML_V_TOT = ML_HEADS * ML_V_DIM
ML_IN = 2 * ML_QK_TOT + 2 * ML_V_TOT + 2 * ML_HEADS

FFN_DIM = 2816
FFN_CONV = 3

N_GDN_LAYERS = (DEPTH + 1) // 2
N_ML_LAYERS = DEPTH // 2


def rms_norm(x, w):
    xf = x.astype(jnp.float32)
    y = xf * lax.rsqrt(jnp.mean(xf * xf, -1, keepdims=True) + RMS_EPS)
    return (y * w.astype(jnp.float32)).astype(x.dtype)

def l2_normalize(x):
    return x * lax.rsqrt(jnp.sum(x * x, -1, keepdims=True) + L2_EPS)

def causal_depthwise_conv(x, w):
    K, C = w.shape
    return lax.conv_general_dilated(x, w[:, None, :].astype(x.dtype), window_strides=(1,),
                                    padding=[(K - 1, 0)], dimension_numbers=('NWC', 'WIO', 'NWC'),
                                    feature_group_count=C)

def to_chunks(t):
    B, L, H = t.shape[:3]
    t = t.reshape((B, L // CHUNK, CHUNK, H) + t.shape[3:])
    return jnp.moveaxis(t, 3, 1)

def from_chunks(t):
    B, H, nc, C, d = t.shape
    return jnp.moveaxis(t, 1, 3).reshape(B, nc * C, H, d)

def gated_deltanet(h, valid, w_in, conv_w, a_log, dt_bias, norm_w, w_out):
    f32 = jnp.float32
    B, L, _ = h.shape
    proj = h @ w_in
    o1 = GDN_QKV_DIM
    o2 = o1 + GDN_VAL_DIM
    o3 = o2 + GDN_V_HEADS
    qkv = jax.nn.silu(causal_depthwise_conv(proj[..., :o1], conv_w)).astype(f32)
    z = proj[..., o1:o2].astype(f32).reshape(B, L, GDN_V_HEADS, GDN_HEAD_DIM)
    beta = jax.nn.sigmoid(proj[..., o2:o3].astype(f32))
    g = -jnp.exp(a_log.astype(f32)) * jax.nn.softplus(proj[..., o3:].astype(f32) + dt_bias.astype(f32))

    rep = GDN_V_HEADS // GDN_QK_HEADS
    mask = valid[None, :, None, None]
    q = qkv[..., :GDN_KEY_DIM].reshape(B, L, GDN_QK_HEADS, GDN_HEAD_DIM)
    k = qkv[..., GDN_KEY_DIM:2 * GDN_KEY_DIM].reshape(B, L, GDN_QK_HEADS, GDN_HEAD_DIM)
    v = qkv[..., 2 * GDN_KEY_DIM:].reshape(B, L, GDN_V_HEADS, GDN_HEAD_DIM) * mask
    q = jnp.repeat(l2_normalize(q), rep, axis=2) * (GDN_HEAD_DIM ** -0.5)
    k = jnp.repeat(l2_normalize(k), rep, axis=2) * mask

    qc, kc, vc = to_chunks(q), to_chunks(k), to_chunks(v)
    bc, gc = to_chunks(beta), to_chunks(g)
    G = jnp.cumsum(gc, -1)
    incl = jnp.tri(CHUNK, dtype=bool)
    strict = jnp.tri(CHUNK, k=-1, dtype=f32)
    decay = jnp.exp(jnp.where(incl, G[..., :, None] - G[..., None, :], -jnp.inf))
    kb = kc * bc[..., None]
    a_mat = jnp.eye(CHUNK, dtype=f32) + jnp.einsum('bhnid,bhnjd->bhnij', kb, kc) * decay * strict
    rhs = jnp.concatenate([vc * bc[..., None], kb * jnp.exp(G)[..., None]], -1)
    sol = lax.linalg.triangular_solve(a_mat, rhs, left_side=True, lower=True)
    u, w = sol[..., :GDN_HEAD_DIM], sol[..., GDN_HEAD_DIM:]
    attn = jnp.einsum('bhnid,bhnjd->bhnij', qc, kc) * decay
    qd = qc * jnp.exp(G)[..., None]
    kt = kc * jnp.exp(G[..., -1:] - G)[..., None]
    gt = jnp.exp(G[..., -1])

    def step(S, xs):
        u_c, w_c, qd_c, att_c, kt_c, gt_c = xs
        v_new = u_c - jnp.einsum('bhck,bhkv->bhcv', w_c, S)
        o_c = jnp.einsum('bhck,bhkv->bhcv', qd_c, S) + jnp.einsum('bhij,bhjv->bhiv', att_c, v_new)
        S = S * gt_c[..., None, None] + jnp.einsum('bhck,bhcv->bhkv', kt_c, v_new)
        return S, o_c

    xs = tuple(jnp.moveaxis(t, 2, 0) for t in (u, w, qd, attn, kt, gt))
    S0 = jnp.zeros((B, GDN_V_HEADS, GDN_HEAD_DIM, GDN_HEAD_DIM), f32)
    _, o = lax.scan(step, S0, xs)
    o = from_chunks(jnp.moveaxis(o, 0, 2))
    o = rms_norm(o, norm_w) * jax.nn.silu(z)
    return o.reshape(B, L, GDN_VAL_DIM).astype(h.dtype) @ w_out

def mlstm(h, valid, w_in, gate_b, norm_w, w_out):
    f32 = jnp.float32
    B, L, _ = h.shape
    proj = h @ w_in
    o1 = ML_QK_TOT
    o2 = 2 * ML_QK_TOT
    o3 = o2 + ML_V_TOT
    o4 = o3 + ML_V_TOT
    mask = valid[None, :, None, None]
    q = proj[..., :o1].astype(f32).reshape(B, L, ML_HEADS, ML_QK_DIM) * (ML_QK_DIM ** -0.5)
    k = proj[..., o1:o2].astype(f32).reshape(B, L, ML_HEADS, ML_QK_DIM) * mask
    v = proj[..., o2:o3].astype(f32).reshape(B, L, ML_HEADS, ML_V_DIM) * mask
    o_gate = jax.nn.sigmoid(proj[..., o3:o4].astype(f32)).reshape(B, L, ML_HEADS, ML_V_DIM)
    gates = proj[..., o4:].astype(f32) + gate_b.astype(f32)
    gates = ML_GATE_CAP * jnp.tanh(gates / ML_GATE_CAP)
    log_i = gates[..., :ML_HEADS]
    log_f = jax.nn.log_sigmoid(gates[..., ML_HEADS:])

    qc, kc, vc = to_chunks(q), to_chunks(k), to_chunks(v)
    lic, lfc = to_chunks(log_i), to_chunks(log_f)
    b = jnp.cumsum(lfc, -1)
    b_last = b[..., -1]
    a = b_last[..., None] - b + lic

    def step(carry, xs):
        Cs, ns, ms = carry
        k_c, v_c, a_c, bl_c = xs
        m_new = jnp.maximum(bl_c + ms, jnp.max(a_c, -1))
        dec = jnp.exp(bl_c + ms - m_new)
        kw = k_c * jnp.exp(a_c - m_new[..., None])[..., None]
        C_new = dec[..., None, None] * Cs + jnp.einsum('bhck,bhcv->bhkv', kw, v_c)
        n_new = dec[..., None] * ns + jnp.sum(kw, -2)
        return (C_new, n_new, m_new), (Cs, ns, ms)

    xs = tuple(jnp.moveaxis(t, 2, 0) for t in (kc, vc, a, b_last))
    init = (jnp.zeros((B, ML_HEADS, ML_QK_DIM, ML_V_DIM), f32),
            jnp.zeros((B, ML_HEADS, ML_QK_DIM), f32),
            jnp.zeros((B, ML_HEADS), f32))
    _, (C_st, n_st, m_st) = lax.scan(step, init, xs)
    C_st = jnp.moveaxis(C_st, 0, 2)
    n_st = jnp.moveaxis(n_st, 0, 2)
    m_st = jnp.moveaxis(m_st, 0, 2)

    incl = jnp.tri(CHUNK, dtype=bool)
    D = jnp.where(incl, b[..., :, None] - b[..., None, :] + lic[..., None, :], -jnp.inf)
    inter = b + m_st[..., None]
    m_t = jnp.maximum(jnp.max(D, -1), inter)
    wD = jnp.exp(D - m_t[..., None]) * jnp.einsum('bhnid,bhnjd->bhnij', qc, kc)
    sc = jnp.exp(inter - m_t)
    num = sc[..., None] * jnp.einsum('bhnck,bhnkv->bhncv', qc, C_st) + jnp.einsum('bhnij,bhnjv->bhniv', wD, vc)
    den = sc * jnp.einsum('bhnck,bhnk->bhnc', qc, n_st) + jnp.sum(wD, -1)
    hh = num / jnp.maximum(jnp.abs(den), jnp.exp(-m_t))[..., None]
    hh = from_chunks(hh)
    hh = rms_norm(hh, norm_w.reshape(ML_HEADS, ML_V_DIM)) * o_gate
    return hh.reshape(B, L, ML_V_TOT).astype(h.dtype) @ w_out

def conv_ffn(h, w_up, conv_w, conv_b, w_down):
    u = causal_depthwise_conv(h @ w_up, conv_w) + conv_b
    gate, up = u[..., :FFN_DIM], u[..., FFN_DIM:]
    return (jax.nn.silu(gate) * up) @ w_down

def first_inputs(seed: int = 0) -> dict:
    key = jax.random.key(seed)
    ks = jax.random.split(key, 20)
    f32 = jnp.float32
    nrm = lambda k, shape, s: jax.random.normal(k, shape, f32) * s
    x = nrm(ks[0], (BATCH, SEQ, D_MODEL), 1.0)
    meta_tokens = nrm(ks[1], (N_META, D_MODEL), 1.0)
    norm_w = 1.0 + nrm(ks[2], (DEPTH, 4, D_MODEL), 0.05)
    gdn_w_in = nrm(ks[3], (N_GDN_LAYERS, D_MODEL, GDN_IN), D_MODEL ** -0.5)
    gdn_conv_w = nrm(ks[4], (N_GDN_LAYERS, GDN_CONV, GDN_QKV_DIM), GDN_CONV ** -0.5)
    gdn_a_log = jnp.log(jax.random.uniform(ks[5], (N_GDN_LAYERS, GDN_V_HEADS), f32, 1.0, 16.0))
    dt = jnp.exp(jax.random.uniform(ks[6], (N_GDN_LAYERS, GDN_V_HEADS), f32, np.log(1e-3), np.log(1e-1)))
    gdn_dt_bias = dt + jnp.log(-jnp.expm1(-dt))
    gdn_norm_w = 1.0 + nrm(ks[7], (N_GDN_LAYERS, GDN_HEAD_DIM), 0.05)
    gdn_w_out = nrm(ks[8], (N_GDN_LAYERS, GDN_VAL_DIM, D_MODEL), GDN_VAL_DIM ** -0.5)
    ml_w_in = nrm(ks[9], (N_ML_LAYERS, D_MODEL, ML_IN), D_MODEL ** -0.5)
    ig_b = nrm(ks[10], (N_ML_LAYERS, ML_HEADS), 0.1)
    fg_b = jnp.linspace(3.0, 6.0, ML_HEADS, dtype=f32)[None] + nrm(ks[11], (N_ML_LAYERS, ML_HEADS), 0.1)
    ml_gate_b = jnp.concatenate([ig_b, fg_b], -1)
    ml_norm_w = 1.0 + nrm(ks[12], (N_ML_LAYERS, ML_V_TOT), 0.05)
    ml_w_out = nrm(ks[13], (N_ML_LAYERS, ML_V_TOT, D_MODEL), ML_V_TOT ** -0.5)
    ffn_w_up = nrm(ks[14], (DEPTH, D_MODEL, 2 * FFN_DIM), D_MODEL ** -0.5)
    ffn_conv_w = nrm(ks[15], (DEPTH, FFN_CONV, 2 * FFN_DIM), FFN_CONV ** -0.5)
    ffn_conv_b = nrm(ks[16], (DEPTH, 2 * FFN_DIM), 0.01)
    ffn_w_down = nrm(ks[17], (DEPTH, FFN_DIM, D_MODEL), FFN_DIM ** -0.5)
    return {"x": x, "meta_tokens": meta_tokens, "norm_w": norm_w,
            "gdn_w_in": gdn_w_in, "gdn_conv_w": gdn_conv_w, "gdn_a_log": gdn_a_log,
            "gdn_dt_bias": gdn_dt_bias, "gdn_norm_w": gdn_norm_w, "gdn_w_out": gdn_w_out,
            "ml_w_in": ml_w_in, "ml_gate_b": ml_gate_b, "ml_norm_w": ml_norm_w, "ml_w_out": ml_w_out,
            "ffn_w_up": ffn_w_up, "ffn_conv_w": ffn_conv_w, "ffn_conv_b": ffn_conv_b, "ffn_w_down": ffn_w_down}

def first_block(x, meta_tokens, norm_w, gdn_w_in, gdn_conv_w, gdn_a_log, gdn_dt_bias, gdn_norm_w, gdn_w_out,
              ml_w_in, ml_gate_b, ml_norm_w, ml_w_out, ffn_w_up, ffn_conv_w, ffn_conv_b, ffn_w_down):
    B, S, D = x.shape
    pad = jnp.zeros((B, N_PAD, D), x.dtype)
    meta = jnp.broadcast_to(meta_tokens[None].astype(x.dtype), (B, N_META, D))
    hs = jnp.concatenate([pad, meta, x], 1)
    L = hs.shape[1]
    valid = (jnp.arange(L) >= N_PAD).astype(jnp.float32)
    keep = valid.astype(x.dtype)[None, :, None]
    for i in range(DEPTH):
        j = i // N_MIXERS
        a_in = rms_norm(hs, norm_w[i, 0])
        if i % N_MIXERS == 0:
            mix = gated_deltanet(a_in, valid, gdn_w_in[j], gdn_conv_w[j], gdn_a_log[j], gdn_dt_bias[j],
                                 gdn_norm_w[j], gdn_w_out[j])
        else:
            mix = mlstm(a_in, valid, ml_w_in[j], ml_gate_b[j], ml_norm_w[j], ml_w_out[j])
        hs = hs + keep * rms_norm(mix, norm_w[i, 1])
        f = conv_ffn(rms_norm(hs, norm_w[i, 2]), ffn_w_up[i], ffn_conv_w[i], ffn_conv_b[i], ffn_w_down[i])
        hs = hs + keep * rms_norm(f, norm_w[i, 3])
    return hs[:, N_PAD + N_META:]


CONV_WIDTH = 512
CONV_K = 3
SWA_HEADS = 8
SWA_KV_HEADS = 2
SWA_HEAD_DIM = 64
WINDOW = 128
SWA_BLOCK = 128
GLA_HEADS = 4
GLA_DK = 64
GLA_DV = 128
GLA_GATE_RANK = 16
GLA_GATE_TAU = 16.0
GLA_CHUNK = 64
MLA_HEADS = 4
MLA_Q_RANK = 256
MLA_KV_RANK = 128
MLA_NOPE = 64
MLA_ROPE = 32
MLA_V = 128
MLA_BLOCK = 128
ROPE_THETA = 10000.0
D_FF = ((-(-8 * D_MODEL // 3) + 255) // 256) * 256
ALPHA = (2.0 * DEPTH) ** 0.25
BETA = (8.0 * DEPTH) ** -0.25
LN_EPS = 1e-5

N_EVEN = (DEPTH + 1) // 2
N_ODD = DEPTH // 2

EVEN_SPLITS = [CONV_WIDTH, CONV_WIDTH, CONV_WIDTH,
               SWA_HEADS * SWA_HEAD_DIM, SWA_KV_HEADS * SWA_HEAD_DIM, SWA_KV_HEADS * SWA_HEAD_DIM]
EVEN_IN = sum(EVEN_SPLITS)
EVEN_MIX = CONV_WIDTH + SWA_HEADS * SWA_HEAD_DIM
ODD_SPLITS = [GLA_HEADS * GLA_DK, GLA_HEADS * GLA_DK, GLA_HEADS * GLA_DV, GLA_GATE_RANK,
              GLA_HEADS * GLA_DV, MLA_Q_RANK, MLA_KV_RANK, MLA_ROPE]
ODD_IN = sum(ODD_SPLITS)
ODD_MIX = GLA_HEADS * GLA_DV + MLA_HEADS * MLA_V


def split_cols(u, sizes):
    return jnp.split(u, np.cumsum(sizes)[:-1].tolist(), axis=-1)

def layer_norm(x, g, b):
    xf = x.astype(jnp.float32)
    mu = xf.mean(-1, keepdims=True)
    var = jnp.mean(jnp.square(xf - mu), -1, keepdims=True)
    return ((xf - mu) * lax.rsqrt(var + LN_EPS) * g.astype(jnp.float32) + b.astype(jnp.float32)).astype(x.dtype)

def rms_norm_2(x, g):
    xf = x.astype(jnp.float32)
    ms = jnp.mean(jnp.square(xf), -1, keepdims=True)
    return (xf * lax.rsqrt(ms + RMS_EPS) * g.astype(jnp.float32)).astype(x.dtype)

def apply_rope(t, cos, sin):
    t1, t2 = jnp.split(t, 2, axis=-1)
    return jnp.concatenate([t1 * cos - t2 * sin, t2 * cos + t1 * sin], axis=-1)

def short_conv_mixer(b_gate, c_gate, h, conv_w):
    S = h.shape[1]
    z = c_gate * h
    zp = jnp.pad(z, ((0, 0), (CONV_K - 1, 0), (0, 0)))
    y = zp[:, 0:S] * conv_w[0]
    for j in range(1, CONV_K):
        y = y + zp[:, j:j + S] * conv_w[j]
    return b_gate * y

def swa_sink_attention(q, k, v, sinks):
    B_, S, _ = q.shape
    nb = S // SWA_BLOCK
    G = SWA_HEADS // SWA_KV_HEADS
    q = q.reshape(B_, nb, SWA_BLOCK, SWA_KV_HEADS, G, SWA_HEAD_DIM)
    k = k.reshape(B_, nb, SWA_BLOCK, SWA_KV_HEADS, SWA_HEAD_DIM)
    v = v.reshape(B_, nb, SWA_BLOCK, SWA_KV_HEADS, SWA_HEAD_DIM)
    pad = ((0, 0), (1, 0), (0, 0), (0, 0), (0, 0))
    kk = jnp.concatenate([jnp.pad(k, pad)[:, :-1], k], axis=2)
    vv = jnp.concatenate([jnp.pad(v, pad)[:, :-1], v], axis=2)
    s = jnp.einsum('bnqhgd,bnkhd->bnhgqk', q, kk).astype(jnp.float32) * (SWA_HEAD_DIM ** -0.5)
    qi = jnp.arange(SWA_BLOCK)[:, None]
    kj = jnp.arange(2 * SWA_BLOCK)[None, :] - SWA_BLOCK
    diff = qi - kj
    band = (diff >= 0) & (diff < WINDOW)
    valid = (jnp.arange(nb)[:, None, None] > 0) | (kj[None] >= 0)
    mask = band[None] & valid
    s = jnp.where(mask[None, :, None, None], s, -jnp.inf)
    sink = sinks.astype(jnp.float32).reshape(SWA_KV_HEADS, G)[None, None, :, :, None, None]
    m = jnp.maximum(s.max(-1, keepdims=True), sink)
    p = jnp.exp(s - m)
    p = p / (p.sum(-1, keepdims=True) + jnp.exp(sink - m))
    o = jnp.einsum('bnhgqk,bnkhd->bnqhgd', p.astype(v.dtype), vv)
    return o.reshape(B_, S, SWA_HEADS * SWA_HEAD_DIM)

def gla_mixer(q, k, v, g_low, r, w_gate, b_gate, g_norm):
    B_, S, _ = q.shape
    H, C = GLA_HEADS, GLA_CHUNK
    nc = S // C
    log_a = jax.nn.log_sigmoid((g_low @ w_gate + b_gate).astype(jnp.float32)) / GLA_GATE_TAU

    def to_chunks(t, d):
        return t.astype(jnp.float32).reshape(B_, nc, C, H, d).transpose(1, 0, 3, 2, 4)

    qc = to_chunks(q, GLA_DK) * (GLA_DK ** -0.5)
    kc = to_chunks(k, GLA_DK)
    vc = to_chunks(v, GLA_DV)
    gc = to_chunks(log_a, GLA_DK)
    causal = jnp.tril(jnp.ones((C, C), bool))[:, :, None]

    def step(state, inp):
        qb, kb, vb, gb = inp
        b = jnp.cumsum(gb, axis=2)
        o_inter = jnp.einsum('bhtd,bhdv->bhtv', qb * jnp.exp(b), state)
        diff = b[:, :, :, None, :] - b[:, :, None, :, :]
        decay = jnp.exp(jnp.where(causal, diff, -jnp.inf))
        attn = jnp.einsum('bhtd,bhsd,bhtsd->bhts', qb, kb, decay)
        o = o_inter + jnp.einsum('bhts,bhsv->bhtv', attn, vb)
        b_last = b[:, :, -1:, :]
        k_dec = kb * jnp.exp(b_last - b)
        state = jnp.exp(b_last[:, :, 0, :])[..., None] * state + jnp.einsum('bhsd,bhsv->bhdv', k_dec, vb)
        return state, o

    s0 = jnp.zeros((B_, H, GLA_DK, GLA_DV), jnp.float32)
    _, o = lax.scan(step, s0, (qc, kc, vc, gc))
    o = o.transpose(1, 0, 3, 2, 4).reshape(B_, S, H, GLA_DV)
    o = rms_norm_2(o, g_norm).reshape(B_, S, H * GLA_DV)
    return (o * jax.nn.silu(r.astype(jnp.float32))).astype(q.dtype)

def mla_mixer(c_q, c_kv, k_r, g_qn, w_uq, g_kvn, w_ukv, cos, sin):
    B_, S, _ = c_q.shape
    H = MLA_HEADS
    q = (rms_norm_2(c_q, g_qn) @ w_uq).reshape(B_, S, H, MLA_NOPE + MLA_ROPE)
    q_nope = q[..., :MLA_NOPE]
    q_rope = apply_rope(q[..., MLA_NOPE:], cos[:, None, :], sin[:, None, :])
    kv = (rms_norm_2(c_kv, g_kvn) @ w_ukv).reshape(B_, S, H, MLA_NOPE + MLA_V)
    k_nope, v = kv[..., :MLA_NOPE], kv[..., MLA_NOPE:]
    k_rope = apply_rope(k_r, cos, sin)
    scale = (MLA_NOPE + MLA_ROPE) ** -0.5
    nb = S // MLA_BLOCK
    qn_b = q_nope.reshape(B_, nb, MLA_BLOCK, H, MLA_NOPE).transpose(1, 0, 2, 3, 4)
    qr_b = q_rope.reshape(B_, nb, MLA_BLOCK, H, MLA_ROPE).transpose(1, 0, 2, 3, 4)
    kpos = jnp.arange(S)

    def attend(args):
        qn, qr, i = args
        s = (jnp.einsum('bqhd,bkhd->bhqk', qn, k_nope) +
             jnp.einsum('bqhr,bkr->bhqk', qr, k_rope)).astype(jnp.float32) * scale
        qpos = i * MLA_BLOCK + jnp.arange(MLA_BLOCK)
        s = jnp.where(kpos[None, :] <= qpos[:, None], s, -jnp.inf)
        p = jax.nn.softmax(s, axis=-1)
        return jnp.einsum('bhqk,bkhv->bqhv', p.astype(v.dtype), v)

    o = lax.map(attend, (qn_b, qr_b, jnp.arange(nb)))
    return o.transpose(1, 0, 2, 3, 4).reshape(B_, S, H * MLA_V)

def swiglu(x, w_gate, w_up, w_down):
    return (jax.nn.silu(x @ w_gate) * (x @ w_up)) @ w_down

def second_inputs(seed: int = 0) -> dict:
    key = jax.random.key(seed)
    ks = iter(jax.random.split(key, 32))
    nrm = lambda shape, s: jax.random.normal(next(ks), shape, jnp.float32) * s
    D = D_MODEL
    return {
        "x": nrm((BATCH, SEQ, D), 1.0),
        "ev_w_in": nrm((N_EVEN, D, EVEN_IN), D ** -0.5),
        "ev_conv_w": nrm((N_EVEN, CONV_K, CONV_WIDTH), CONV_K ** -0.5),
        "ev_sinks": nrm((N_EVEN, SWA_HEADS), 0.5),
        "ev_w_out": nrm((N_EVEN, EVEN_MIX, D), BETA * EVEN_MIX ** -0.5),
        "od_w_in": nrm((N_ODD, D, ODD_IN), D ** -0.5),
        "od_gla_w_gate": nrm((N_ODD, GLA_GATE_RANK, GLA_HEADS * GLA_DK), GLA_GATE_RANK ** -0.5),
        "od_gla_b_gate": nrm((N_ODD, GLA_HEADS * GLA_DK), 0.1),
        "od_gla_norm_g": 1.0 + nrm((N_ODD, GLA_DV), 0.02),
        "od_mla_q_norm_g": 1.0 + nrm((N_ODD, MLA_Q_RANK), 0.02),
        "od_mla_w_uq": nrm((N_ODD, MLA_Q_RANK, MLA_HEADS * (MLA_NOPE + MLA_ROPE)), MLA_Q_RANK ** -0.5),
        "od_mla_kv_norm_g": 1.0 + nrm((N_ODD, MLA_KV_RANK), 0.02),
        "od_mla_w_ukv": nrm((N_ODD, MLA_KV_RANK, MLA_HEADS * (MLA_NOPE + MLA_V)), MLA_KV_RANK ** -0.5),
        "od_w_out": nrm((N_ODD, ODD_MIX, D), BETA * ODD_MIX ** -0.5),
        "ffn_w_gate": nrm((DEPTH, D, D_FF), D ** -0.5),
        "ffn_w_up": nrm((DEPTH, D, D_FF), D ** -0.5),
        "ffn_w_down": nrm((DEPTH, D_FF, D), BETA * D_FF ** -0.5),
        "ln_mix_g": 1.0 + nrm((DEPTH, D), 0.02),
        "ln_mix_b": nrm((DEPTH, D), 0.02),
        "ln_ffn_g": 1.0 + nrm((DEPTH, D), 0.02),
        "ln_ffn_b": nrm((DEPTH, D), 0.02),
    }

def second_block(x, ev_w_in, ev_conv_w, ev_sinks, ev_w_out, od_w_in, od_gla_w_gate, od_gla_b_gate,
              od_gla_norm_g, od_mla_q_norm_g, od_mla_w_uq, od_mla_kv_norm_g, od_mla_w_ukv, od_w_out,
              ffn_w_gate, ffn_w_up, ffn_w_down, ln_mix_g, ln_mix_b, ln_ffn_g, ln_ffn_b):
    S = x.shape[1]
    pos = jnp.arange(S, dtype=jnp.float32)
    inv_freq = ROPE_THETA ** (-jnp.arange(0, MLA_ROPE, 2, dtype=jnp.float32) / MLA_ROPE)
    ang = pos[:, None] * inv_freq[None, :]
    cos, sin = jnp.cos(ang).astype(x.dtype), jnp.sin(ang).astype(x.dtype)

    for layer in range(DEPTH):
        i = layer // 2
        if layer % 2 == 0:
            u = x @ ev_w_in[i]
            b_g, c_g, h, q, k, v = split_cols(u, EVEN_SPLITS)
            ya = short_conv_mixer(b_g, c_g, h, ev_conv_w[i])
            yb = swa_sink_attention(q, k, v, ev_sinks[i])
            y = jnp.concatenate([ya, yb], axis=-1) @ ev_w_out[i]
        else:
            u = x @ od_w_in[i]
            gq, gk, gv, g_low, gr, c_q, c_kv, k_r = split_cols(u, ODD_SPLITS)
            yc = gla_mixer(gq, gk, gv, g_low, gr, od_gla_w_gate[i], od_gla_b_gate[i], od_gla_norm_g[i])
            yd = mla_mixer(c_q, c_kv, k_r, od_mla_q_norm_g[i], od_mla_w_uq[i],
                           od_mla_kv_norm_g[i], od_mla_w_ukv[i], cos, sin)
            y = jnp.concatenate([yc, yd], axis=-1) @ od_w_out[i]
        x = layer_norm(ALPHA * x + y, ln_mix_g[layer], ln_mix_b[layer])
        x = layer_norm(ALPHA * x + swiglu(x, ffn_w_gate[layer], ffn_w_up[layer], ffn_w_down[layer]),
                       ln_ffn_g[layer], ln_ffn_b[layer])
    return x


def setup_inputs(seed=0):
    out = dict(first_inputs(seed))
    for name, value in second_inputs(seed + 1).items():
        if name != "x":
            out[name + "_2"] = value
    return out


def reference(
    x, meta_tokens, norm_w, gdn_w_in, gdn_conv_w, gdn_a_log, gdn_dt_bias, gdn_norm_w, gdn_w_out,
    ml_w_in, ml_gate_b, ml_norm_w, ml_w_out, ffn_w_up, ffn_conv_w, ffn_conv_b, ffn_w_down,
    ev_w_in_2, ev_conv_w_2, ev_sinks_2, ev_w_out_2, od_w_in_2, od_gla_w_gate_2, od_gla_b_gate_2,
    od_gla_norm_g_2, od_mla_q_norm_g_2, od_mla_w_uq_2, od_mla_kv_norm_g_2, od_mla_w_ukv_2,
    od_w_out_2, ffn_w_gate_2, ffn_w_up_2, ffn_w_down_2, ln_mix_g_2, ln_mix_b_2, ln_ffn_g_2,
    ln_ffn_b_2,
):
    x = first_block(
        x, meta_tokens, norm_w, gdn_w_in, gdn_conv_w, gdn_a_log, gdn_dt_bias, gdn_norm_w,
        gdn_w_out, ml_w_in, ml_gate_b, ml_norm_w, ml_w_out, ffn_w_up, ffn_conv_w, ffn_conv_b,
        ffn_w_down,
    )
    return second_block(
        x, ev_w_in_2, ev_conv_w_2, ev_sinks_2, ev_w_out_2, od_w_in_2, od_gla_w_gate_2,
        od_gla_b_gate_2, od_gla_norm_g_2, od_mla_q_norm_g_2, od_mla_w_uq_2, od_mla_kv_norm_g_2,
        od_mla_w_ukv_2, od_w_out_2, ffn_w_gate_2, ffn_w_up_2, ffn_w_down_2, ln_mix_g_2,
        ln_mix_b_2, ln_ffn_g_2, ln_ffn_b_2,
    )


_drawn_inputs = setup_inputs


def setup_inputs(seed=0):
    import zlib

    import numpy as np

    out = dict(_drawn_inputs(seed))
    spreads = {}
    factors = {'ev_sinks_2': 8.0,
     'od_gla_w_gate_2': 3.784,
     'od_gla_b_gate_2': 8.0,
     'od_gla_norm_g_2': 8.0,
     'od_mla_q_norm_g_2': 8.0,
     'od_mla_kv_norm_g_2': 8.0}
    for name, (base, spread) in spreads.items():
        noise = np.random.default_rng([zlib.crc32(name.encode()), seed]).standard_normal(out[name].shape)
        drawn = base * np.exp(spread * noise) if base else spread * noise
        out[name] = __import__('jax').numpy.asarray(drawn.astype(out[name].dtype))
    for name, factor in factors.items():
        out[name] = (out[name] * factor).astype(out[name].dtype)
    return out
```

```python
import math
from contextlib import ExitStack

import numpy as np

import concourse.bass as bass
from concourse import mybir
from concourse.alu_op_type import AluOpType as ALU

F32 = mybir.dt.float32
F32R = mybir.dt.float32r
ACT = mybir.ActivationFunctionType
AX = mybir.AxisListType.X

P = 128
D = 1024
KC = D // P
N_META, SEQ = 16, 256
T1 = N_META + SEQ
T2 = SEQ
RMS_EPS = L2_EPS = 1e-6
LN_EPS = 1e-5

GK, GV, GD = 8, 16, 128
CH = 68
NCH = T1 // CH
LEVELS = [1 << s for s in range(7)]
MH, MV = 4, 256
GATE_CAP = 15.0
FF = 2816
FC = FF // P
ALPHA = 4.0 ** 0.25
NEG = -1.0e30
WORK = 6720

SLOTS = 4
AHEAD = 3
BLOCK = 8 * P


class Steps:

    def __init__(self, sem, table, key):
        self.sem, self.seen, self.key = sem, 0, key
        self.table = table.setdefault(key, {})
        self.loop = None

    def mark(self, name):
        self.seen += 1
        if self.loop:
            self.table[name] = (self.loop[0], self.seen, None, self.loop[1])
        else:
            self.table[name] = (0, self.seen, 0, 1)
        return self.sem, 1

    def repeat(self, times):
        return _Repeat(self, times)

    def at(self, name, i=None):
        if name not in self.table:
            return self.sem, 1
        base, seen, per, times = self.table[name]
        per = self.table[("per", base)] if per is None and ("per", base) in self.table else (per or 0)
        if i is None:
            return self.sem, base + (times - 1) * per + seen
        return self.sem, i * per + (base + seen)

    def before(self, i):
        base = self.table.get("loop_base", 0)
        return self.sem, i * self.table.get(("per", base), 0) + base


class _Repeat:
    def __init__(self, steps, times):
        self.s, self.times = steps, times

    def __enter__(self):
        s = self.s
        self.base = s.seen
        s.table["loop_base"] = self.base
        s.loop, s.seen = (self.base, self.times), 0
        return self

    def __exit__(self, *_):
        s = self.s
        s.table[("per", self.base)] = s.seen
        s.seen, s.loop = self.base + self.times * s.seen, None


def vec_tiles(n):
    return n // P


PARAMS = [
    ("norm_w", 8 * KC), ("gdn_conv", 32 * 4), ("gdn_norm", 1), ("ml_norm", 8),
    ("ffn0", 44 * 4), ("ffn1", 44 * 4), ("ev_conv", 4 * 3), ("gla_b", 2), ("gla_norm", 1),
    ("mla_qn", 2), ("mla_kvn", 1), ("ln_mix", 2 * 2 * KC), ("ln_ffn", 2 * 2 * KC), ("sinks", 8),
    ("gdn_a_log", 1), ("gdn_dt", 1), ("ml_ib", 1), ("ml_fb", 1),
    ("gdn_gates", KC * 32), ("ml_gates", KC * 8), ("g_low", KC * 16), ("gla_w", 256),
]
AT, _n = {}, 0
for _name, _cols in PARAMS:
    AT[_name] = (_n, _n + _cols)
    _n += _cols
NPARAM = _n

CONSTS = [
    ("ident", 128), ("ones", 128), ("upto", 128), ("neg_chunk", CH), ("levels", len(LEVELS) * CH),
    ("swa_mask", 256), ("mla_mask", 256), ("cos", T2), ("sin", T2),
]
CAT, _n = {}, 0
for _name, _cols in CONSTS:
    CAT[_name] = (_n, _n + _cols)
    _n += _cols
NCONST = _n

PHASES = [("gdn_in", "tiles", 48), ("gdn_out", "wide", 16), ("up0", "tiles", 44), ("down0", "wide", 22),
          ("ml_in", "tiles", 24), ("ml_out", "wide", 8), ("up1", "tiles", 44), ("down1", "wide", 22),
          ("ev_in", "tiles", 18), ("ev_out", "wide", 8), ("up2", "tiles", 44), ("down2", "wide", 22),
          ("od_in", "tiles", 17), ("od_out", "wide", 8), ("up3", "tiles", 44), ("down3", "wide", 22)]
FIRST_BLOCK, _n = {}, 0
for _name, _kind, _count in PHASES:
    FIRST_BLOCK[_name] = _n
    _n += _count
NBLOCKS = _n
COUNT = {n: c for n, _, c in PHASES}


def constants():
    c = np.zeros((P, NCONST), np.float32)
    r, q = np.arange(P)[:, None], np.arange(P)[None]
    put = lambda name, a: c[:a.shape[0], CAT[name][0]:CAT[name][0] + a.shape[1]].__setitem__(slice(None), a)
    put("ident", np.eye(P, dtype=np.float32))
    put("ones", np.ones((P, P), np.float32))
    put("upto", (r <= q).astype(np.float32))
    put("neg_chunk", np.where(r <= q, 0, NEG).astype(np.float32)[:CH, :CH])
    i, j = np.arange(CH)[:, None], np.arange(CH)[None]
    put("levels", np.concatenate([((i // (2 * s) == j // (2 * s)) & (i // s % 2 == 1) & (j // s % 2 == 0))
                                  .astype(np.float32) for s in LEVELS], 1))
    same = np.where(q <= r, 0, NEG).astype(np.float32)
    put("swa_mask", np.concatenate([np.where(q > r, 0, NEG).astype(np.float32), same], 1))
    put("mla_mask", np.concatenate([0 * same, same], 1))
    freq = 10000.0 ** (-np.arange(0, 32, 2, dtype=np.float32) / 32)
    ang = (np.arange(T2, dtype=np.float32)[:, None] * freq[None]).T
    cos, sin = np.ones((96, T2), np.float32), np.zeros((96, T2), np.float32)
    cos[64:80] = cos[80:96] = np.cos(ang)
    sin[64:80], sin[80:96] = -np.sin(ang), np.sin(ang)
    put("cos", cos)
    put("sin", sin)
    return c


def tile_blocks(w):
    n = w.shape[1] // P
    return w.reshape(KC, P, n, P).transpose(2, 1, 0, 3).reshape(n, P, BLOCK)


def wide_blocks(w):
    return w.reshape(-1, P, BLOCK)


SWAP = np.r_[16:32, 0:16]


def lay_out(a):
    f = FF
    stream, cols = [], {}
    gw = a["gdn_w_in"][0]
    stream += [tile_blocks(gw[:, :6144]), wide_blocks(a["gdn_w_out"][0])]
    mw = a["ml_w_in"][0]

    def ffn(gate, up, down):
        both = np.stack([gate.reshape(D, FC, P), up.reshape(D, FC, P)], 2).reshape(D, 2 * f)
        return [tile_blocks(both), wide_blocks(down)]

    ev, od = a["ev_w_in_2"][0], a["od_w_in_2"][0]
    heads = np.arange(1536, 2048).reshape(8, 64)
    order = np.concatenate([np.r_[heads[t], heads[t + 4]] for t in range(4)])
    evw = np.concatenate([ev[:, :1536], ev[:, order], ev[:, 2048:]], 1)
    evo = a["ev_w_out_2"][0]
    evo = np.concatenate([evo[:512], evo[order - 1024]], 0)
    kr = od[:, 1936:1968]
    odw = np.concatenate([od[:, :1024], od[:, 1040:1936]] + [kr] * 4 + [kr[:, SWAP]] * 4, 1)
    u = a["ffn_w_up"]
    stream += ffn(u[0, :, :f], u[0, :, f:], a["ffn_w_down"][0])
    stream += [tile_blocks(mw[:, :3072]), wide_blocks(a["ml_w_out"][0])]
    stream += ffn(u[1, :, :f], u[1, :, f:], a["ffn_w_down"][1])
    stream += [tile_blocks(evw), wide_blocks(evo)]
    g2, u2, d2 = a["ffn_w_gate_2"], a["ffn_w_up_2"], a["ffn_w_down_2"]
    stream += ffn(g2[0], u2[0], d2[0])
    stream += [tile_blocks(odw), wide_blocks(a["od_w_out_2"][0])]
    stream += ffn(g2[1], u2[1], d2[1])
    stream = np.concatenate(stream, 0)
    assert stream.shape == (NBLOCKS, P, BLOCK)

    params = np.zeros((P, NPARAM), np.float32)

    def put(name, v):
        params[:v.shape[0], AT[name][0]:AT[name][1]] = v

    def per_tile(v):
        return v.reshape(v.shape[0], -1, P).transpose(2, 1, 0).reshape(P, -1)

    def rows(v):
        return v.reshape(-1, P).T

    put("norm_w", rows(a["norm_w"].reshape(8, D)))
    put("gdn_conv", per_tile(a["gdn_conv_w"][0]))
    put("gdn_norm", a["gdn_norm_w"][0][:, None])
    put("ml_norm", rows(a["ml_norm_w"]))
    for n in range(2):
        cw = np.concatenate([a["ffn_conv_w"][n], a["ffn_conv_b"][n][None]], 0)
        both = np.stack([cw[:, :f].reshape(4, FC, P), cw[:, f:].reshape(4, FC, P)], 2).reshape(4, 2 * f)
        put(f"ffn{n}", per_tile(both))
    put("ev_conv", per_tile(a["ev_conv_w_2"][0]))
    put("gla_b", rows(a["od_gla_b_gate_2"]))
    put("gla_norm", a["od_gla_norm_g_2"][0][:, None])
    put("mla_qn", rows(a["od_mla_q_norm_g_2"]))
    put("mla_kvn", rows(a["od_mla_kv_norm_g_2"]))
    for name in ("ln_mix", "ln_ffn"):
        put(name, rows(np.stack([a[name + "_g_2"], a[name + "_b_2"]], 1).reshape(4, D)))
    put("sinks", np.broadcast_to(a["ev_sinks_2"], (P, 8)))
    put("gdn_a_log", a["gdn_a_log"][0][:, None])
    put("gdn_dt", a["gdn_dt_bias"][0][:, None])
    put("ml_ib", a["ml_gate_b"][0, :4][:, None])
    put("ml_fb", a["ml_gate_b"][0, 4:][:, None])
    put("gdn_gates", gw[:, 6144:].reshape(KC, P, 32).transpose(1, 0, 2).reshape(P, -1))
    put("ml_gates", mw[:, 3072:].reshape(KC, P, 8).transpose(1, 0, 2).reshape(P, -1))
    put("g_low", od[:, 1024:1040].reshape(KC, P, 16).transpose(1, 0, 2).reshape(P, -1))
    put("gla_w", a["od_gla_w_gate_2"][0])

    uq = a["od_mla_w_uq_2"][0]
    swapped = uq.reshape(256, 4, 96)[:, :, np.r_[0:64, 64 + SWAP]].reshape(256, 384)
    ukv = a["od_mla_w_ukv_2"][0].reshape(P, 4, 192)
    mla = np.concatenate([uq.reshape(2, P, 384).transpose(1, 0, 2).reshape(P, -1),
                          swapped.reshape(2, P, 384).transpose(1, 0, 2).reshape(P, -1),
                          ukv[:, :, :64].reshape(P, 256), ukv[:, :, 64:].reshape(P, 512)], 1)
    hs = np.concatenate([a["meta_tokens"], a["x"][0]], 0).T.reshape(KC, P, T1).transpose(1, 0, 2)
    return {name: np.ascontiguousarray(v) for name, v in dict(
        stream=stream, params=params, consts=constants(), mla=mla, hs=hs.reshape(P, -1)).items()}


SHAPES = dict(stream=(NBLOCKS, P, BLOCK), params=(P, NPARAM), consts=(P, NCONST), mla=(P, 2304),
              hs=(P, KC * T1))


def build(nc, stream, params, consts, mla, hs_in, out, table):
    ctx = ExitStack()

    def sb(name, shape):
        return ctx.enter_context(nc.sbuf_tensor(name, shape, F32))

    def sem(name):
        return ctx.enter_context(nc.semaphore(name))

    def shared(name, shape, other, other_shape):
        with nc.sbuf_tensor(name, shape, F32) as first:
            pass
        return first, ctx.enter_context(nc.sbuf_tensor(other, other_shape, F32R))

    raw = sb("raw", [P, SLOTS, BLOCK])
    whi = ctx.enter_context(nc.sbuf_tensor("whi", [P, SLOTS, BLOCK], F32R))
    wlo = ctx.enter_context(nc.sbuf_tensor("wlo", [P, SLOTS, BLOCK], F32R))
    par = sb("par", [P, NPARAM])
    con = sb("con", [P, NCONST])
    hs = sb("hs_sb", [P, KC, T1])
    xf, xs = shared("xf", [P, 2 * KC, T1], "xs", [P, 2 * KC, T1])
    y = sb("y", [P, KC, T1])
    sq = sb("sq", [P, KC, T1])
    rs = sb("rs", [P, 2, T1])
    big, hf = shared("big", [P, 48, T1], "hf", [P, 2 * FC, T1])
    mix = sb("mix", [P, KC, T1])
    cv = sb("cv", [P, 8, T1])
    work = sb("work", [P, WORK])
    bank = [ctx.enter_context(nc.psum_tensor(f"bank{i}", [P, 512], F32)) for i in range(8)]

    def pv(name, k=0, n=1, rows=P):
        lo = AT[name][0] + k
        return par[0:rows, lo:lo + n]

    def cn(name, rows=P, lo=0, cols=None):
        a, b = CAT[name]
        return con[0:rows, a + lo:a + lo + cols if cols else b]

    ones, ident = cn("ones"), cn("ident")

    loaded = sem("loaded")
    hs_loaded = sem("hs_loaded")
    mla_loaded = sem("mla_loaded")
    block_loaded = [sem(f"block_loaded{s}") for s in range(SLOTS)]
    hi_split = sem("hi_split")
    block_split = sem("block_split")
    block_used = sem("block_used")
    bank_free = sem("bank_free")
    conv_taken = sem("conv_taken")
    stored = sem("stored")

    steps = {}

    def S(phase, engine):
        key = f"{phase}_{engine}"
        if key not in steps:
            steps[key] = Steps(sem(key), table, key)
        return steps[key]

    def sp_stream(sp):
        sp.dma_start(hs[:, :, :], hs_in.rearrange("p (c t) -> p c t", t=T1)).then_inc(hs_loaded, 16)
        sp.dma_start(con[:, :], consts).then_inc(loaded, 16)
        sp.dma_start(par[:, :], params).then_inc(loaded, 16)
        for s in range(SLOTS):
            sp.dma_start(raw[:, s, :], stream[s]).then_inc(block_loaded[s], 16)
        rounds = NBLOCKS // SLOTS
        with sp.Fori(0, rounds - 1) as r:
            for s in range(SLOTS):
                sp.wait_ge(block_split, r * SLOTS + (s + 1))
                sp.dma_start(raw[:, s, :], stream[(r + 1) * SLOTS + s]).then_inc(block_loaded[s], 16)
        for n in range(rounds * SLOTS, NBLOCKS):
            sp.wait_ge(block_split, n - SLOTS + 1)
            sp.dma_start(raw[:, n % SLOTS, :], stream[n]).then_inc(block_loaded[n % SLOTS], 16)

    def split_hi(act, n, i=0):
        s = n % SLOTS
        act.wait_ge(block_loaded[s], i * (16 * 8 // SLOTS) + 16 * (n // SLOTS + 1))
        if n >= SLOTS:
            act.wait_ge(block_used, i * 8 + (n - SLOTS + 1))
        nc.scalar.activation(whi[:, s, :], raw[:, s, :], ACT.Copy).then_inc(hi_split, 1)

    def split_lo(dve, n, i=0):
        s = n % SLOTS
        dve.wait_ge(hi_split, i * 8 + (n + 1))
        nc.vector.tensor_tensor(wlo[:, s, :], raw[:, s, :], whi[:, s, :].bitcast(F32), ALU.subtract).then_inc(block_split, 1)

    def split_all(engine, split, phase, lo=0):
        b0 = FIRST_BLOCK[phase] + AHEAD + lo
        n = min(COUNT[phase] - lo, NBLOCKS - b0)
        if n >= 16:
            with engine.Fori(0, n // 8) as i:
                for j in range(8):
                    split(engine, b0 + j, i)
        for j in range(n // 8 * 8 if n >= 16 else 0, n):
            split(engine, b0 + j)

    def three(out_, slot, c, hi, lo, start, stop):
        w = slice(c * P, (c + 1) * P)
        nc.tensor.matmul(out_, whi[:, slot, w], hi, start=start, stop=False)
        nc.tensor.matmul(out_, whi[:, slot, w], lo, start=False, stop=False)
        return nc.tensor.matmul(out_, wlo[:, slot, w], hi, start=False, stop=stop)

    def pe_tiles(pe, phase, g0):
        b0, n = FIRST_BLOCK[phase], COUNT[phase]
        T = T1 if b0 < FIRST_BLOCK["ev_in"] else T2

        def tile(j, i=0):
            g = g0 + j
            pe.wait_ge(block_split, i * 8 + (b0 + j + 1))
            pe.wait_ge(bank_free, i * 8 + (g + 1))
            for k in range(KC):
                last = three(rhs_out(g, phase), (b0 + j) % SLOTS, k, xs[:, k, 0:T], xs[:, KC + k, 0:T], k == 0, k == KC - 1)
            last.then_inc(block_used, 1)

        with pe.Fori(0, n // 8) as i:
            for j in range(8):
                tile(j, i)
        for j in range(n // 8 * 8, n):
            tile(j)

    def rhs_out(g, phase):
        return bank[g % 8][:, 0:T1 if FIRST_BLOCK[phase] < FIRST_BLOCK["ev_in"] else T2]

    def pe_wide(pe, phase, g0, ready):
        b0, n = FIRST_BLOCK[phase], COUNT[phase]
        T = T1 if b0 < FIRST_BLOCK["ev_in"] else T2
        pe.wait_ge(bank_free, g0 + 8)

        def rows(k, i=None):
            at = k if i is None else i * 8 + k
            lo = n + k if i is None else i * 8 + (n + k)
            pe.wait_ge(block_split, (0 if i is None else i * 8) + (b0 + k + 1))
            ready(pe, k, i)
            for m in range(8):
                last = three(rhs_out(g0 + m, phase), (b0 + k) % SLOTS, m, hf[:, at, 0:T], hf[:, lo, 0:T], k == 0, k == n - 1)
            last.then_inc(block_used, 1)

        if n == 22:
            rows(0)
            with pe.Fori(0, 2) as i:
                for k in range(1, 9):
                    rows(k, i)
            for k in range(17, 22):
                rows(k)
        else:
            for k in range(n):
                rows(k)

    NORM = {}

    def pe_sum(pe, name, g, src, engine, T, n=KC, sums="norm"):
        pe.wait_ge(bank_free, g + 1)
        for m in range(n):
            pe.wait_ge(*S("norm", engine).at(f"{name}_{m}"))
            last = nc.tensor.matmul(bank[g % 8][:, 0:T], ones, src(m), start=(m == 0), stop=(m == n - 1))
        last.then_inc(*S("norm", "pe").mark(name))

    def act_scale(act, name, g, dst, T, count, eps, ready):
        act.wait_ge(*S("norm", "pe").at(name))
        nc.scalar.activation(dst, bank[g % 8][:, 0:T], ACT.Ln, bias=eps, scale=1.0 / count).then_inc(bank_free, 1)
        act.wait_ge(bank_free, 8 + g + 1)
        nc.scalar.activation(dst, dst, ACT.Exp, scale=-0.5).then_inc(*S("norm", "act").mark(f"{name}_scale"))

    def pre_pe(pe, name, g):
        pe_sum(pe, name, g, lambda m: sq[:, m, :], "act", T1)

    def pre_act(act, name, g, ready):
        for m in range(KC):
            ready(act, m)
            nc.scalar.activation(sq[:, m, :], hs[:, m, :], ACT.Square).then_inc(*S("norm", "act").mark(f"{name}_{m}"))
        act_scale(act, name, g, rs[:, 0, :], T1, D, eps_1, None)
        pre_act_hi(act, name)

    def pre_dve(dve, name, row):
        st, a_ = S("norm", "dve"), S("norm", "act")
        dve.wait_ge(*a_.at(f"{name}_scale"))
        for m in range(KC):
            nc.vector.scalar_tensor_tensor(y[:, m, :], hs[:, m, :], pv("norm_w", row * KC + m), rs[:, 0, :],
                                           ALU.mult, ALU.mult).then_inc(*st.mark(f"{name}_x{m}"))
        for m in range(KC):
            dve.wait_ge(*a_.at(f"{name}_hi{m}"))
            nc.vector.tensor_tensor(xs[:, KC + m, :], y[:, m, :], xs[:, m, :].bitcast(F32), ALU.subtract
                                    ).then_inc(*st.mark(f"{name}_lo{m}"))

    def pre_act_hi(act, name):
        for m in range(KC):
            act.wait_ge(*S("norm", "dve").at(f"{name}_x{m}"))
            nc.scalar.activation(xs[:, m, :], y[:, m, :], ACT.Copy).then_inc(*S("norm", "act").mark(f"{name}_hi{m}"))

    def mix_act(act, name, src, n, ready):
        ready(act)
        for k in range(n):
            nc.scalar.activation(hf[:, k, 0:src(k).shape[1]], src(k), ACT.Copy).then_inc(*S("norm", "act").mark(f"{name}_hi{k}"))

    def mix_dve(dve, name, src, n, ready):
        ready(dve)
        for k in range(n):
            T = src(k).shape[1]
            dve.wait_ge(*S("norm", "act").at(f"{name}_hi{k}"))
            nc.vector.tensor_tensor(hf[:, n + k, 0:T], src(k), hf[:, k, 0:T].bitcast(F32), ALU.subtract
                                    ).then_inc(*S("norm", "dve").mark(f"{name}_lo{k}"))

    def post_pe(pe, name, g):
        pe_sum(pe, name, g, lambda m: sq[:, m, :], "act", T1)

    def post_act(act, name, g):
        for m in range(KC):
            act.wait_ge(bank_free, 8 + g - 8 + m + 1)
            nc.scalar.activation(sq[:, m, :], y[:, m, :], ACT.Square).then_inc(*S("norm", "act").mark(f"{name}_{m}"))
        act_scale(act, name, g, rs[:, 1, :], T1, D, eps_1, None)

    def post_dve(dve, name, g, row, last_block):
        for m in range(KC):
            if m == 0:
                dve.wait_ge(block_used, last_block)
            nc.vector.tensor_copy(y[:, m, :], bank[(g - 8 + m) % 8][:, 0:T1]).then_inc(bank_free, 1)
        dve.wait_ge(*S("norm", "act").at(f"{name}_scale"))
        for m in range(KC):
            nc.vector.scalar_tensor_tensor(y[:, m, :], y[:, m, :], pv("norm_w", row * KC + m), rs[:, 1, :],
                                           ALU.mult, ALU.mult).then_inc(*S("norm", "dve").mark(f"{name}_y{m}"))
        for m in range(KC):
            dve.wait_ge(*S("norm", "dve").at(f"{name}_y{m}"))
            nc.vector.tensor_tensor(hs[:, m, :], hs[:, m, :], y[:, m, :], ALU.add
                                    ).then_inc(*S("norm", "dve").mark(f"{name}_h{m}"))

    def conv_first(act, steps_, tag, tiles, taps, bias):
        for a, (bk, slot, w) in enumerate(tiles):
            args = dict(scale=w[:, taps - 1:taps])
            if bias:
                args["bias"] = w[:, taps:taps + 1]
            nc.scalar.activation(cv[:, slot, :], bk[:, 0:T1], ACT.Identity, **args).then_inc(*steps_.mark(f"{tag}{a}"))

    def conv_rest(dve, steps_, first, tag, tiles, i, taps):
        for tap in range(1, taps):
            for a, (bk, slot, w) in enumerate(tiles):
                o = cv[:, slot, :]
                dve.wait_ge(*(first.at(f"{tag}{a}", i) if tap == 1 else steps_.at(f"{tag}_{tap - 1}{a}", i)))
                ins = nc.vector.scalar_tensor_tensor(o[:, tap:T1], bk[:, 0:T1 - tap], w[:, taps - 1 - tap:taps - tap],
                                                     o[:, tap:T1], ALU.mult, ALU.add)
                if tap == taps - 1 and a == 1:
                    ins.then_inc(bank_free, 2)
                else:
                    ins.then_inc(*steps_.mark(f"{tag}_{tap}{a}"))

    CONV0, _c = {}, 0
    for name, n in (("gdn_in", 32), ("up0", 44), ("up1", 44), ("up2", 44), ("up3", 44)):
        CONV0[name] = _c
        _c += n

    def pairs(engine, pair, steps_=None):
        with ExitStack() as loop:
            i = loop.enter_context(engine.Fori(0, 5))
            if steps_:
                loop.enter_context(steps_.repeat(5))
            for j in range(4):
                pair(j, i, 0)
        for j in range(2):
            pair(j, None, 40)

    def ffn_tiles(f, g0, j, i, base):
        t = 2 * j + base
        if f < 2:
            lo = AT[f"ffn{f}"][0]
            W = par[:, lo:lo + 176].rearrange("p (t k) -> p t k", k=4)
            w = [W[:, i * 8 + (t + a) if i is not None else t + a, :] for a in range(2)]
        else:
            w = [None] * 2
        return [(bank[(g0 + t + a) % 8], 2 * j + a, w[a]) for a in range(2)]

    def ffn_act(act, f, g0):
        st, b0, c0 = S("ffn", "act"), FIRST_BLOCK[f"up{f}"], CONV0[f"up{f}"]

        def pair(j, i, base):
            t, ii = base + 2 * j, 0 if i is None else i
            tiles = ffn_tiles(f, g0, j, i, base)
            act.wait_ge(block_used, ii * 8 + (b0 + t + 2))
            act.wait_ge(conv_taken, ii * 8 + (c0 + t + 2))
            if f < 2:
                conv_first(act, st, f"f{f}_{base}_{j}", tiles, 3, True)
                split_hi(act, b0 + t + AHEAD, ii)
                split_hi(act, b0 + t + AHEAD + 1, ii)
                act.wait_ge(bank_free, ii * 8 + (8 + g0 + t + 2))
                o = cv[:, 2 * j, :]
                nc.scalar.activation(o, o, ACT.Silu).then_inc(*st.mark(f"silu{f}_{base}_{j}"))
            else:
                nc.scalar.activation(cv[:, 2 * j, 0:T2], tiles[0][0][:, 0:T2], ACT.Silu).then_inc(*st.mark(f"silu{f}_{base}_{j}"))
                split_hi(act, b0 + t + AHEAD, ii)
                split_hi(act, b0 + t + AHEAD + 1, ii)

        pairs(act, pair, st)

    def ffn_dve(dve, f, g0):
        st, b0 = S("ffn", "dve"), FIRST_BLOCK[f"up{f}"]

        def pair(j, i, base):
            t, ii = base + 2 * j, 0 if i is None else i
            tiles = ffn_tiles(f, g0, j, i, base)
            if f < 2:
                conv_rest(dve, st, S("ffn", "act"), f"f{f}_{base}_{j}", tiles, i, 3)
            else:
                dve.wait_ge(*S("ffn", "act").at(f"silu{f}_{base}_{j}", i))
                nc.vector.tensor_tensor(cv[:, 2 * j + 1, 0:T2], cv[:, 2 * j, 0:T2], tiles[1][0][:, 0:T2], ALU.mult).then_inc(bank_free, 2)
            split_lo(dve, b0 + t + AHEAD, ii)
            split_lo(dve, b0 + t + AHEAD + 1, ii)

        pairs(dve, pair, st)

    def ffn_pool(pool, f, g0):
        st, T = S("ffn", "pool"), T1 if f < 2 else T2

        def pair(j, i, base):
            ii = 0 if i is None else i
            k = base // 2 + j
            h = cv[:, 2 * j + 1, 0:T]
            hi = hf[:, k if i is None else i * 4 + k, 0:T]
            lo = hf[:, FC + k if i is None else i * 4 + (FC + k), 0:T]
            if f < 2:
                pool.wait_ge(*S("ffn", "act").at(f"silu{f}_{base}_{j}", i))
                nc.gpsimd.tensor_tensor(h, cv[:, 2 * j, 0:T], h, ALU.mult).then_inc(*st.mark(f"h{f}_{base}_{j}"))
                pool.wait_ge(*st.at(f"h{f}_{base}_{j}", i))
            else:
                pool.wait_ge(bank_free, ii * 8 + (8 + g0 + base + 2 * j + 2))
            nc.gpsimd.tensor_copy(hi, h).then_inc(*st.mark(f"hi{f}_{base}_{j}"))
            pool.wait_ge(*st.at(f"hi{f}_{base}_{j}", i))
            nc.gpsimd.tensor_tensor(lo, h, hi.bitcast(F32), ALU.subtract).then_inc(conv_taken, 2)

        pairs(pool, pair, st)

    def ffn_ready(f):
        def ready(pe, k, i):
            c = 8 + CONV0[f"up{f}"] + 2 * (k + 1)
            pe.wait_ge(conv_taken, c if i is None else i * 16 + c)
        return ready

    G, _g = {}, 0
    for name, n in (("pre0", 1), ("gdn_g", 2), ("gdn_in", 48), ("gdn_out", 8), ("post0", 1), ("pre1", 1), ("up0", 44), ("down0", 8),
                    ("post1", 1), ("pre2", 1), ("ml_g", 2), ("ml_in", 24), ("ml_out", 8), ("post2", 1), ("pre3", 1), ("up1", 44),
                    ("down1", 8), ("post3", 1),
                    ("ev_in", 18), ("ev_out", 8), ("lm0", 1), ("lv0", 1), ("up2", 44), ("down2", 8), ("lm1", 1), ("lv1", 1),
                    ("od_g", 1), ("od_in", 17), ("od_out", 8), ("lm2", 1), ("lv2", 1), ("up3", 44), ("down3", 8), ("lm3", 1), ("lv3", 1)):
        G[name] = _g
        _g += n

    def used_after(phase):
        return FIRST_BLOCK[phase] + COUNT[phase]

    ch = lambda ap: ap.rearrange("p (c t) -> p c t", c=NCH)
    H = [[buf[:, s, :] for s in range(KC)] for buf in (y, sq)]
    TT, UU, X1 = ([xf[:, a * 4 + s, :] for a in range(2)] for s in range(3))
    qn, kn, kk, kq = (cv[:, s, :] for s in range(4))
    vst = [cv[:, 4, :], cv[:, 5, :]]
    qss, kss = cv[:, 6, :], cv[:, 7, :]
    wk = lambda lo, n: work[:, lo:lo + n]
    ktok = wk(0, 512).rearrange("p (c d) -> p c d", c=NCH)
    vtok = [wk(512 + a * 512, 512).rearrange("p (c d) -> p c d", c=NCH) for a in range(2)]
    vnew = [wk(1536 + a * 128, 128) for a in range(2)]
    vdec = [wk(1792 + a * 128, 128) for a in range(2)]
    state = [wk(2048 + a * 128, 128) for a in range(2)]
    tok = lambda n: wk(2304 + n * 64, 64)[0:CH].rearrange("p (c h) -> p c h", c=NCH)
    g_tok, b_tok, G_tok, nbe_tok, el_tok = (tok(n) for n in range(5))
    row = lambda n: wk(2624 + n * T1, T1)[0:GV]
    b_row, u_row, t_row, G_row, ea = row(0), row(1), row(2), row(3), row(4)
    BR = row(5)
    head = lambda ap, h: ap.rearrange("p c (h o) -> p c h o", o=1)[:, :, h, :]
    EYE = cn("ident").rearrange("p (n o) -> p n o", o=1)

    def gates_pe(pe, name, g, cols, base, width, T, rhs):
        w = pv(base, 0, KC * width).rearrange("p (k n) -> p k n", k=KC)
        for n, (lo, m) in enumerate(cols):
            pe.wait_ge(bank_free, g + n + 1)
            for k in range(KC):
                last = nc.tensor.matmul(bank[(g + n) % 8][0:m, 0:T], w[:, k, lo:lo + m], rhs(k), start=(k == 0), stop=(k == KC - 1))
            last.then_inc(*S("gates", "pe").mark(f"{name}{n}"))

    def gdn_gates_act(act):
        g = G["gdn_g"]
        act.wait_ge(*S("gates", "pe").at("gdn0"))
        nc.scalar.activation(b_row, bank[g % 8][0:GV, 0:T1], ACT.Sigmoid).then_inc(bank_free, 1)
        act.wait_ge(*S("gates", "pe").at("gdn1"))
        nc.scalar.activation(u_row, bank[(g + 1) % 8][0:GV, 0:T1], ACT.Identity, bias=pv("gdn_dt", rows=GV)).then_inc(bank_free, 1)

    def gdn_in_tiles(j, i):
        lo = AT["gdn_conv"][0]
        W = par[:, lo:lo + 128].rearrange("p (t k) -> p t k", k=4)
        return [(bank[(G["gdn_in"] + 2 * j + a) % 8], 2 * j + a, W[:, i * 8 + (2 * j + a), :]) for a in range(2)]

    def gdn_in_dve(dve):
        st, g0, b0 = S("gin", "dve"), G["gdn_in"], FIRST_BLOCK["gdn_in"]
        dve.wait_ge(bank_free, 8 + g0)
        with dve.Fori(0, 4) as i, st.repeat(4):
            for j in range(4):
                conv_rest(dve, st, S("gin", "act"), f"c{j}", gdn_in_tiles(j, i), i, 4)
                split_lo(dve, b0 + 2 * j + AHEAD, i)
                split_lo(dve, b0 + 2 * j + AHEAD + 1, i)
        split_all(dve, split_lo, "gdn_in", 32)

    def gdn_in_act(act):
        st, g0, b0, c0 = S("gin", "act"), G["gdn_in"], FIRST_BLOCK["gdn_in"], CONV0["gdn_in"]
        with act.Fori(0, 4) as i, st.repeat(4):
            for j in range(4):
                act.wait_ge(block_used, i * 8 + (b0 + 2 * j + 2))
                act.wait_ge(conv_taken, i * 8 + (c0 + 2 * j + 2))
                conv_first(act, st, f"c{j}", gdn_in_tiles(j, i), 4, False)
                split_hi(act, b0 + 2 * j + AHEAD, i)
                split_hi(act, b0 + 2 * j + AHEAD + 1, i)
                act.wait_ge(bank_free, i * 8 + (8 + g0 + 2 * j + 2))
                for a in range(2):
                    nc.scalar.activation(big[:, i * 8 + (2 * j + a), :], cv[:, 2 * j + a, :], ACT.Silu).then_inc(conv_taken, 1)
        with act.Fori(0, 2) as i:
            for j in range(8):
                act.wait_ge(block_used, i * 8 + (b0 + 32 + j + 1))
                nc.scalar.activation(big[:, i * 8 + (32 + j), :], bank[(g0 + 32 + j) % 8][:, 0:T1], ACT.Silu).then_inc(bank_free, 1)
                split_hi(act, b0 + 32 + j + AHEAD, i)

    def gdn_pe(pe):
        m, v, a_ = S("gdn", "pe"), S("gdn", "dve"), S("gdn", "act")
        pl = S("gdn", "pool")
        mm = nc.tensor.matmul
        pe.wait_ge(bank_free, 8 + G["gdn_out"])
        pe.wait_ge(*v.at("g_row"))
        for c in range(NCH):
            nc.tensor.transpose(bank[0][0:CH, c * 16:c * 16 + 16], ch(t_row)[:, c, :], ident[0:16, 0:16])
        for c in range(NCH):
            last = nc.tensor.transpose(bank[1][0:CH, c * 16:c * 16 + 16], ch(b_row)[:, c, :], ident[0:16, 0:16])
        last.then_inc(*m.mark("to_tok"))
        pe.wait_ge(*v.at("g_tok"))
        upto = cn("upto")[0:CH, 0:CH]
        for c in range(NCH):
            mm(bank[2][0:16, c * CH:(c + 1) * CH], g_tok[:, c, :], upto, start=True, stop=True)
        for c in range(NCH):
            mm(bank[3][0:CH, c * 16:c * 16 + 16], upto, g_tok[:, c, :], start=True, stop=True)
        for c in range(NCH):
            last = mm(bank[4][0:CH, c * 16:c * 16 + 16], ones[0:CH, 0:CH], g_tok[:, c, :], start=True, stop=True)
        last.then_inc(*m.mark("sums"))

        sl = lambda ap, c: ap[0:CH, c * CH:(c + 1) * CH]
        full = lambda ap, c: ap[:, c * CH:(c + 1) * CH]
        with pe.Fori(0, GK) as i, m.repeat(GK):
            pe.wait_ge(*v.at("squares", i))
            mm(bank[0][:, 0:T1], ones, qss, start=True, stop=True)
            mm(bank[1][:, 0:T1], ones, kss, start=True, stop=True).then_inc(*m.mark("norms"))
            pe.wait_ge(*v.at("kn", i))
            for c in range(NCH):
                mm(sl(bank[2], c), full(kn, c), full(kn, c), start=True, stop=True)
            last = None
            for c in range(NCH):
                last = mm(sl(bank[3], c), full(kn, c), full(qn, c), start=True, stop=True)
            last.then_inc(*m.mark("kk"))
            for c in range(NCH):
                last = nc.tensor.transpose(bank[4][0:CH, c * P:(c + 1) * P], full(kn, c), ident)
            last.then_inc(*m.mark("ktok"))
            pe.wait_ge(*a_.at("vst", i))
            for a in range(2):
                for c in range(NCH):
                    last = nc.tensor.transpose(bank[5 + a][0:CH, c * P:(c + 1) * P], full(vst[a], c), ident)
                last.then_inc(*m.mark(f"vtok{a}"))
            for a, (bg, bb) in enumerate(((0, 1), (7, 2))):
                pe.wait_ge(*v.at(f"sel{a}", i))
                if a == 0:
                    pe.wait_ge(*a_.at("rk", i))
                else:
                    pe.wait_ge(*a_.at("kk", i))
                mm(bank[bg][:, 0:T1], ones[0:16, :], H[a][0][0:16, :], start=True, stop=True)
                mm(bank[bb][:, 0:T1], ones[0:16, :], H[a][1][0:16, :], start=True, stop=True).then_inc(*m.mark(f"rows{a}"))
            B3 = ((3, 4, 5), (6, 7, 0))
            for l in range(len(LEVELS)):
                for a in range(2):
                    b1, b2, b3 = B3[a]
                    if l == 0:
                        pe.wait_ge(*v.at(f"A{a}", i))
                        pe.wait_ge(*a_.at(f"EG{a}", i))
                        pe.wait_ge(*a_.at(f"vtok{a}", i))
                        pe.wait_ge(*a_.at("kq", i))
                    else:
                        pe.wait_ge(*v.at(f"U{a}_{l - 1}", i))
                    for c in range(NCH):
                        last = mm(sl(bank[b1], c), sl(H[a][4], c), ident[0:CH, 0:CH] if l == 0 else sl(TT[a], c), start=True, stop=True)
                    last.then_inc(*m.mark(f"X{a}_{l}"))
                for a in range(2):
                    b1, b2, b3 = B3[a]
                    pe.wait_ge(*v.at(f"X{a}_{l}", i))
                    if l == 0 and a == 1:
                        pe.wait_ge(*a_.at("EG0", i))
                    if 0 < l < len(LEVELS) - 1:
                        for c in range(NCH):
                            last = mm(sl(bank[b2], c), sl(UU[a], c), sl(X1[a], c), start=True, stop=True)
                    for c in range(NCH):
                        last = mm(sl(bank[b3], c), sl(X1[a], c), ident[0:CH, 0:CH] if l == 0 else sl(UU[a], c), start=True, stop=True)
                    last.then_inc(*m.mark(f"Y{a}_{l}"))
            for a in range(2):
                pe.wait_ge(*v.at(f"U2{a}", i))
                for c in range(NCH):
                    last = mm(full(bank[1 + a], c), ktok[0:CH, c, :], sl(H[a][1], c), start=True, stop=True)
                last.then_inc(*m.mark(f"w{a}"))
            B4 = ((3, 4, 5), (6, 7, 0))
            for c in range(NCH):
                for a in range(2):
                    bv, bo, bs = B4[a]
                    if c == 0:
                        pe.wait_ge(*a_.at(f"w{a}", i))
                        pe.wait_ge(*v.at(f"U1{a}", i))
                    if c > 0:
                        pe.wait_ge(*v.at(f"S{a}_{c - 1}", i))
                        mm(bank[bo][:, c * CH:(c + 1) * CH], state[a], full(H[a][6], c), start=True, stop=False)
                    last = mm(bank[bv][0:CH, 0:P], sl(H[a][0], c), vtok[a][0:CH, c, :], start=True, stop=(c == 0))
                    if c > 0:
                        last = mm(bank[bv][0:CH, 0:P], full(H[a][7], c), state[a], start=False, stop=True)
                    last.then_inc(*m.mark(f"v{a}_{c}"))
                for a in range(2):
                    bv, bo, bs = B4[a]
                    pe.wait_ge(*a_.at(f"v{a}_{c}", i))
                    if c == 0:
                        pe.wait_ge(*pl.at(f"qd{a}", i))
                    mm(bank[bo][:, c * CH:(c + 1) * CH], vnew[a][0:CH], sl(H[a][5], c), start=(c == 0), stop=True).then_inc(*m.mark(f"o{a}_{c}"))
                    if c < NCH - 1:
                        pe.wait_ge(*pl.at(f"d{a}_{c}", i))
                        mm(bank[bs][:, 0:P], ktok[0:CH, c, :], vdec[a][0:CH], start=True, stop=True).then_inc(*m.mark(f"s{a}_{c}"))
            for a in range(2):
                pe.wait_ge(*a_.at(f"osq{a}", i))
                mm(bank[1 + a][:, 0:T1], ones, H[a][3], start=True, stop=True).then_inc(*m.mark(f"on{a}"))
            pe.wait_ge(*v.at("o1", i))

    def gdn_act(act):
        m, v, a_, pl = S("gdn", "pe"), S("gdn", "dve"), S("gdn", "act"), S("gdn", "pool")
        A = nc.scalar.activation
        act.wait_ge(bank_free, 8 + G["gdn_g"] + 2)
        A(t_row, u_row, ACT.Abs).then_inc(*a_.mark("abs"))
        act.wait_ge(*a_.at("abs"))
        A(t_row, t_row, ACT.Exp, scale=-1.0).then_inc(*a_.mark("e"))
        A(ea[:, 0:1], pv("gdn_a_log", rows=GV), ACT.Exp).then_inc(*a_.mark("ea"))
        act.wait_ge(*a_.at("e"))
        A(t_row, t_row, ACT.Ln, bias=1.0).then_inc(*a_.mark("softplus"))
        act.wait_ge(*m.at("to_tok"))
        A(g_tok.rearrange("p c h -> p (c h)"), bank[0][0:CH, 0:64], ACT.Copy).then_inc(*a_.mark("g_tok"))
        A(b_tok.rearrange("p c h -> p (c h)"), bank[1][0:CH, 0:64], ACT.Copy).then_inc(*a_.mark("b_tok"))
        act.wait_ge(*v.at("G_tok"))
        act.wait_ge(*v.at("el_tok"))
        flat = lambda ap: ap.rearrange("p c h -> p (c h)")
        A(flat(nbe_tok), flat(G_tok), ACT.Exp).then_inc(*a_.mark("eG"))
        A(flat(el_tok), flat(el_tok), ACT.Exp).then_inc(*a_.mark("el"))
        with act.Fori(0, GK) as i, a_.repeat(GK):
            for a in range(2):
                last = A(vst[a], big[:, 2 * i + (16 + a), :], ACT.Copy)
            last.then_inc(*a_.mark("vst"))
            act.wait_ge(*m.at("norms", i))
            A(qss, bank[0][:, 0:T1], ACT.Ln, scale=float(GD), bias=eps_q).then_inc(*a_.mark("lq"))
            A(kss, bank[1][:, 0:T1], ACT.Ln, bias=eps_1).then_inc(*a_.mark("lk"))
            act.wait_ge(*a_.at("lq", i))
            A(qss, qss, ACT.Exp, scale=-0.5).then_inc(*a_.mark("rq"))
            act.wait_ge(*a_.at("lk", i))
            A(kss, kss, ACT.Exp, scale=-0.5).then_inc(*a_.mark("rk"))
            act.wait_ge(*m.at("kk", i))
            A(kk[0:CH], bank[2][0:CH, 0:T1], ACT.Copy).then_inc(*a_.mark("kk"))
            A(kq[0:CH], bank[3][0:CH, 0:T1], ACT.Copy).then_inc(*a_.mark("kq"))
            act.wait_ge(*m.at("ktok", i))
            A(wk(0, 512)[0:CH], bank[4][0:CH, :], ACT.Copy).then_inc(*a_.mark("ktok"))
            for a in range(2):
                act.wait_ge(*m.at(f"vtok{a}", i))
                A(wk(512 + a * 512, 512)[0:CH], bank[5 + a][0:CH, :], ACT.Copy).then_inc(*a_.mark(f"vtok{a}"))
            for a in range(2):
                act.wait_ge(*v.at(f"Z{a}", i))
                A(H[a][3][0:CH], H[a][3][0:CH], ACT.Exp).then_inc(*a_.mark(f"D{a}"))
                act.wait_ge(*m.at(f"rows{a}", i))
                A(H[a][2], bank[(0, 7)[a]][:, 0:T1], ACT.Exp).then_inc(*a_.mark(f"EG{a}"))
            for a in range(2):
                act.wait_ge(*m.at(f"w{a}", i))
                A(H[a][7], bank[1 + a][:, 0:T1], ACT.Copy).then_inc(*a_.mark(f"w{a}"))
            for c in range(NCH):
                for a in range(2):
                    act.wait_ge(*m.at(f"v{a}_{c}", i))
                    if c > 0:
                        act.wait_ge(*pl.at(f"d{a}_{c - 1}", i))
                    A(vnew[a][0:CH], bank[(3, 6)[a]][0:CH, 0:P], ACT.Copy).then_inc(*a_.mark(f"v{a}_{c}"))
            for a in range(2):
                act.wait_ge(*m.at(f"o{a}_{NCH - 1}", i))
                act.wait_ge(*v.at(f"att{a}", i))
                A(H[a][3], bank[(4, 7)[a]][:, 0:T1], ACT.Square).then_inc(*a_.mark(f"osq{a}"))
            for a in range(2):
                act.wait_ge(*m.at(f"on{a}", i))
                A(H[a][3], bank[1 + a][:, 0:T1], ACT.Ln, scale=1.0 / GD, bias=eps_1).then_inc(*a_.mark(f"ol{a}"))
                act.wait_ge(*a_.at(f"ol{a}", i))
                A(H[a][3], H[a][3], ACT.Exp, scale=-0.5).then_inc(*a_.mark(f"or{a}"))

    def gdn_dve(dve):
        m, v, a_, pl = S("gdn", "pe"), S("gdn", "dve"), S("gdn", "act"), S("gdn", "pool")
        tt, ts, stt = nc.vector.tensor_tensor, nc.vector.tensor_scalar, nc.vector.scalar_tensor_tensor
        flat = lambda ap: ap.rearrange("p c h -> p (c h)")
        over_i = lambda ap: ap.unsqueeze(2).to_broadcast([CH, NCH, CH])
        over_c = lambda ap: ap.unsqueeze(1).to_broadcast([CH, NCH, CH])
        sq3 = lambda ap: ch(ap[0:CH])
        dve.wait_ge(*a_.at("softplus"))
        stt(t_row, u_row, 0.0, t_row, ALU.max, ALU.add).then_inc(*v.mark("sp"))
        dve.wait_ge(*v.at("sp"))
        ts(t_row, t_row, ea[:, 0:1], -1.0, ALU.mult, ALU.mult).then_inc(*v.mark("g_row"))
        dve.wait_ge(*a_.at("b_tok"))
        nc.vector.tensor_copy(ea[:, 1:2], ea[:, 0:1]).then_inc(*v.mark("g_tok"))
        dve.wait_ge(*m.at("sums"))
        nc.vector.tensor_copy(G_row, bank[2][0:16, 0:T1]).then_inc(*v.mark("G_row"))
        nc.vector.tensor_copy(flat(G_tok), bank[3][0:CH, 0:64]).then_inc(*v.mark("G_tok"))
        dve.wait_ge(*v.at("G_tok"))
        tt(flat(el_tok), bank[4][0:CH, 0:64], flat(G_tok), ALU.subtract).then_inc(*v.mark("el_tok"))
        dve.wait_ge(*a_.at("eG"))
        stt(flat(nbe_tok), flat(nbe_tok), -1.0, flat(b_tok), ALU.mult, ALU.mult).then_inc(*v.mark("nbe"))
        with dve.Fori(0, GK) as i, v.repeat(GK):
            dve.wait_ge(bank_free, 8 + G["gdn_out"])
            tt(qss, big[:, i, :], big[:, i, :], ALU.mult).then_inc(*v.mark("sq_q"))
            tt(kss, big[:, i + 8, :], big[:, i + 8, :], ALU.mult).then_inc(*v.mark("squares"))
            for a in range(2):
                ts(H[a][0][0:16], G_row, EYE[0:16, 2 * i + a, :], None, ALU.mult).then_inc(*v.mark(f"selG{a}"))
                ts(H[a][1][0:16], b_row, EYE[0:16, 2 * i + a, :], None, ALU.mult).then_inc(*v.mark(f"sel{a}"))
            dve.wait_ge(*a_.at("rk", i))
            tt(qn, big[:, i, :], qss, ALU.mult).then_inc(*v.mark("qn"))
            tt(kn, big[:, i + 8, :], kss, ALU.mult).then_inc(*v.mark("kn"))
            for a in range(2):
                dve.wait_ge(*m.at(f"rows{a}", i))
                Z = sq3(H[a][3])
                tt(Z, ch(bank[(0, 7)[a]][0:CH, 0:T1]), over_i(head(G_tok, 2 * i + a).squeeze(2)), ALU.subtract).then_inc(*v.mark(f"z{a}"))
                dve.wait_ge(*v.at(f"z{a}", i))
                tt(Z, Z, over_c(cn("neg_chunk", CH)), ALU.add).then_inc(*v.mark(f"Z{a}"))
            for a in range(2):
                dve.wait_ge(*a_.at(f"D{a}", i))
                dve.wait_ge(*a_.at("kq", i))
                A_T = H[a][4][0:CH]
                tt(A_T, H[a][3][0:CH], kk[0:CH], ALU.mult).then_inc(*v.mark(f"a{a}"))
                tt(H[a][5][0:CH], H[a][3][0:CH], kq[0:CH], ALU.mult).then_inc(*v.mark(f"att{a}"))
                dve.wait_ge(*v.at(f"a{a}", i))
                tt(A_T, A_T, bank[1 + a][0:CH, 0:T1], ALU.mult).then_inc(*v.mark(f"A{a}"))
            for l in range(len(LEVELS)):
                level = over_c(cn("levels", CH, l * CH, CH))
                last_level = l == len(LEVELS) - 1
                for a in range(2):
                    dve.wait_ge(*m.at(f"X{a}_{l}", i))
                    tt(sq3(X1[a]), ch(bank[(3, 6)[a]][0:CH, 0:T1]), level, ALU.mult).then_inc(*v.mark(f"X{a}_{l}"))
                    if l == 0:
                        dve.wait_ge(*v.at(f"X{a}_0", i))
                        tt(sq3(TT[a]), over_c(ident[0:CH, 0:CH]), sq3(X1[a]), ALU.subtract).then_inc(*v.mark(f"T{a}_0"))
                for a in range(2):
                    dve.wait_ge(*m.at(f"Y{a}_{l}", i))
                    if l > 0:
                        dve.wait_ge(*v.at(f"T{a}_{l - 1}", i))
                        if not last_level:
                            tt(TT[a][0:CH], TT[a][0:CH], bank[(4, 7)[a]][0:CH, 0:T1], ALU.subtract).then_inc(*v.mark(f"T{a}_{l}"))
                        tt(UU[a][0:CH], UU[a][0:CH], bank[(5, 0)[a]][0:CH, 0:T1], ALU.subtract).then_inc(*v.mark(f"U{a}_{l}"))
                    else:
                        tt(sq3(UU[a]), over_c(ident[0:CH, 0:CH]), ch(bank[(5, 0)[a]][0:CH, 0:T1]), ALU.subtract).then_inc(*v.mark(f"U{a}_0"))
            for a in range(2):
                dve.wait_ge(*v.at(f"U{a}_{len(LEVELS) - 1}", i))
                tt(sq3(H[a][1]), sq3(UU[a]), over_i(head(nbe_tok, 2 * i + a).squeeze(2)), ALU.mult).then_inc(*v.mark(f"U2{a}"))
                tt(sq3(H[a][0]), sq3(UU[a]), over_i(head(b_tok, 2 * i + a).squeeze(2)), ALU.mult).then_inc(*v.mark(f"U1{a}"))
            for c in range(NCH - 1):
                for a in range(2):
                    dve.wait_ge(*m.at(f"s{a}_{c}", i))
                    if c == 0:
                        nc.vector.tensor_copy(state[a], bank[(5, 0)[a]][:, 0:P]).then_inc(*v.mark(f"S{a}_0"))
                    else:
                        dve.wait_ge(*v.at(f"S{a}_{c - 1}", i))
                        stt(state[a], state[a], H[a][2][:, c * CH + CH - 1:c * CH + CH], bank[(5, 0)[a]][:, 0:P], ALU.mult, ALU.add
                            ).then_inc(*v.mark(f"S{a}_{c}"))
            for a in range(2):
                h = 2 * i + a
                dve.wait_ge(*a_.at(f"or{a}", i))
                tt(H[a][7], bank[(4, 7)[a]][:, 0:T1], H[a][3], ALU.mult).then_inc(*v.mark(f"on{a}"))
                dve.wait_ge(*v.at(f"on{a}", i))
                stt(big[:, h + 32, :], H[a][7], pv("gdn_norm"), big[:, h + 32, :], ALU.mult, ALU.mult).then_inc(*v.mark(f"o{a}"))

    def gdn_pool(pool):
        m, v, a_, pl = S("gdn", "pe"), S("gdn", "dve"), S("gdn", "act"), S("gdn", "pool")
        with pool.Fori(0, GK) as i, pl.repeat(GK):
            for a in range(2):
                pool.wait_ge(*a_.at(f"EG{a}", i))
                nc.gpsimd.tensor_tensor(H[a][6], qn, H[a][2], ALU.mult).then_inc(*pl.mark(f"qd{a}"))
            for c in range(NCH - 1):
                for a in range(2):
                    pool.wait_ge(*a_.at(f"v{a}_{c}", i))
                    nc.gpsimd.tensor_tensor(vdec[a][0:CH], vnew[a][0:CH],
                                            head(el_tok, 2 * i + a)[:, c, :].to_broadcast([CH, P]), ALU.mult).then_inc(*pl.mark(f"d{a}_{c}"))

    JB = ((0, 128), (128, 128), (256, 16))
    OFF = (0, T1, T1 + 144)
    r4 = lambda n: work[0:MH, n * T1:(n + 1) * T1]
    f_row, i_row, s_row, t4_row, bsum_row, cmax_row, m_row, c_row = (r4(n) for n in range(8))
    c_tok = work[:, 2180:2192]
    zbuf, pbuf = work[:, 2200:2632], work[:, 2640:3072]
    em, rden = work[:, 3080:3352], work[:, 3360:3632]
    vt = work[:, 3640:4408].rearrange("p (b d) -> p b d", b=3)
    hh = [work[:, 4420 + s * T1:4420 + (s + 1) * T1] for s in range(4)]
    cB = lambda b: work[0:JB[b][1], 2180 + 4 * b:2184 + 4 * b]

    def ml_gates_act(act):
        g, s = G["ml_g"], S("ml", "act")
        A = nc.scalar.activation
        act.wait_ge(*S("norm", "dve").at("post1_h7"))
        act.wait_ge(*S("gates", "pe").at("ml0"))
        A(i_row, bank[g % 8][0:MH, 0:T1], ACT.Identity, bias=pv("ml_ib", rows=MH)).then_inc(bank_free, 1)
        act.wait_ge(*S("gates", "pe").at("ml1"))
        A(f_row, bank[(g + 1) % 8][0:MH, 0:T1], ACT.Identity, bias=pv("ml_fb", rows=MH)).then_inc(bank_free, 1)
        act.wait_ge(bank_free, 8 + g + 2)
        A(i_row, i_row, ACT.Tanh, scale=1.0 / GATE_CAP).then_inc(*s.mark("i"))
        A(f_row, f_row, ACT.Tanh, scale=1.0 / GATE_CAP).then_inc(*s.mark("tf"))
        act.wait_ge(*s.at("tf"))
        A(s_row, f_row, ACT.Abs).then_inc(*s.mark("af"))
        act.wait_ge(*s.at("af"))
        A(s_row, s_row, ACT.Exp, scale=-GATE_CAP).then_inc(*s.mark("ef"))
        act.wait_ge(*s.at("ef"))
        A(s_row, s_row, ACT.Ln, bias=1.0).then_inc(*s.mark("lf"))

    def scan(dve, s, tag, src, other, op, T):
        step, n = 1, 0
        while step < T:
            if n:
                dve.wait_ge(*s.at(f"{tag}{n - 1}"))
            nc.vector.tensor_tensor(other[..., step:T], src[..., step:T], src[..., 0:T - step], op).then_inc(*s.mark(f"{tag}{n}a"))
            nc.vector.tensor_copy(other[..., 0:step], src[..., 0:step]).then_inc(*s.mark(f"{tag}{n}"))
            src, other = other, src
            step, n = step * 2, n + 1
        dve.wait_ge(*s.at(f"{tag}{n - 1}"))
        return src

    def ml_gates_dve(dve):
        s, a_ = S("ml", "dve"), S("ml", "act")
        ts, stt, tt = nc.vector.tensor_scalar, nc.vector.scalar_tensor_tensor, nc.vector.tensor_tensor
        dve.wait_ge(*a_.at("lf"))
        ts(f_row, f_row, GATE_CAP, 0.0, ALU.mult, ALU.min).then_inc(*s.mark("minf"))
        dve.wait_ge(*s.at("minf"))
        tt(f_row, f_row, s_row, ALU.subtract).then_inc(*s.mark("logf"))
        dve.wait_ge(*s.at("logf"))
        b = scan(dve, s, "b", f_row, t4_row, ALU.add, T1)
        stt(c_row, i_row, GATE_CAP, b, ALU.mult, ALU.subtract).then_inc(*s.mark("c"))
        nc.vector.tensor_copy(bsum_row, b).then_inc(*s.mark("bsum"))
        dve.wait_ge(*s.at("bsum"))
        nc.vector.tensor_copy(f_row, c_row).then_inc(*s.mark("c2"))
        dve.wait_ge(*s.at("c2"))
        mx = scan(dve, s, "m", f_row, t4_row, ALU.max, T1)
        nc.vector.tensor_copy(cmax_row, mx).then_inc(*s.mark("cmax"))
        tt(m_row, mx, bsum_row, ALU.add).then_inc(*s.mark("m"))

    def ml_in_act(act):
        g0, b0 = G["ml_in"], FIRST_BLOCK["ml_in"]
        for turn in range(2):
            with act.Fori(0, (2, 1)[turn]) as i:
                for j in range(8):
                    act.wait_ge(block_used, i * 8 + (b0 + 16 * turn + j + 1))
                    nc.scalar.activation(big[:, i * 8 + (16 * turn + j), :], bank[(g0 + j) % 8][:, 0:T1],
                                         (ACT.Copy, ACT.Sigmoid)[turn]).then_inc(bank_free, 1)
                    split_hi(act, b0 + 16 * turn + j + AHEAD, i)

    def ml_pe(pe):
        m, v, a_, pl = S("ml", "pe"), S("ml", "dve"), S("ml", "act"), S("ml", "pool")
        mm = nc.tensor.matmul
        pe.wait_ge(bank_free, 8 + G["ml_out"])
        pe.wait_ge(*v.at("m"))
        for b, (lo, n) in enumerate(JB):
            last = nc.tensor.transpose(bank[0][0:n, 4 * b:4 * b + 4], c_row[:, lo:lo + n], ident[0:MH, 0:MH])
        last.then_inc(*m.mark("ctok"))
        for h in range(MH):
            if h:
                pe.wait_ge(*v.at(f"P{h - 1}"))
                pe.wait_ge(*a_.at(f"em{h - 1}"))
            else:
                pe.wait_ge(*v.at("ctok"))
            sel = ident[0:MH, h:h + 1].to_broadcast([MH, P])
            mm(bank[0][:, 0:T1], sel, cmax_row, start=True, stop=True)
            mm(bank[1][:, 0:T1], sel, m_row, start=True, stop=True).then_inc(*m.mark(f"rows{h}"))
            for b, (lo, n) in enumerate(JB):
                last = mm(bank[2][0:n, OFF[b]:OFF[b] + T1 - lo], big[:, 4 + h, lo:lo + n], big[:, h, lo:T1], start=True, stop=True)
            last.then_inc(*m.mark(f"S{h}"))
            if h:
                pe.wait_ge(*a_.at(f"vt{h - 1}1"))
            for d in range(2):
                for b, (lo, n) in enumerate(JB):
                    last = nc.tensor.transpose(bank[(3, 7)[d]][0:n, b * P:(b + 1) * P], big[:, 8 + 2 * h + d, lo:lo + n], ident)
                last.then_inc(*m.mark(f"vt{h}{d}"))
            pe.wait_ge(*pl.at(f"P{h}"))
            pe.wait_ge(*a_.at(f"vt{h}1"))
            if h:
                pe.wait_ge(*v.at(f"y{h - 1}1"))
            for d in range(3):
                for b, (lo, n) in enumerate(JB):
                    w = ones[0:n, :] if d == 2 else work[0:n, 3640 + b * 256 + d * P:3640 + b * 256 + (d + 1) * P]
                    last = mm(bank[4 + d][:, lo:T1], w, pbuf[0:n, OFF[b]:OFF[b] + T1 - lo], start=(b == 0), stop=(b == 2))
                last.then_inc(*m.mark(f"n{h}{d}"))
            for d in range(2):
                pe.wait_ge(*a_.at(f"sq{h}{d}"))
                last = mm(bank[3][:, 0:T1], ones, hh[2 + d], start=(d == 0), stop=(d == 1))
            last.then_inc(*m.mark(f"ss{h}"))
            if h + 1 < MH:
                pe.wait_ge(*a_.at(f"ln{h}"))

    def ml_act(act):
        m, v, a_, pl = S("ml", "pe"), S("ml", "dve"), S("ml", "act"), S("ml", "pool")
        A = nc.scalar.activation
        for h in range(MH):
            act.wait_ge(*m.at(f"rows{h}"))
            if h:
                act.wait_ge(*v.at(f"den{h - 1}"))
            A(em, bank[1][:, 0:T1], ACT.Exp, scale=-1.0).then_inc(*a_.mark(f"em{h}"))
            act.wait_ge(*v.at(f"Z{h}"))
            A(zbuf[:, 0:416], zbuf[:, 0:416], ACT.Exp, scale=-1.0).then_inc(*a_.mark(f"Ea{h}"))
            A(zbuf[0:16, 416:432], zbuf[0:16, 416:432], ACT.Exp, scale=-1.0).then_inc(*a_.mark(f"E{h}"))
            for d in range(2):
                act.wait_ge(*m.at(f"vt{h}{d}"))
                if h:
                    act.wait_ge(*m.at(f"n{h - 1}2"))
                bk = bank[(3, 7)[d]]
                A(vt[:, 0:2, d * P:(d + 1) * P], bk[:, 0:256].rearrange("p (b d) -> p b d", b=2), ACT.Copy).then_inc(*a_.mark(f"vta{h}{d}"))
                A(vt[0:16, 2, d * P:(d + 1) * P], bk[0:16, 256:384], ACT.Copy).then_inc(*a_.mark(f"vt{h}{d}"))
            act.wait_ge(*m.at(f"n{h}2"))
            if h:
                act.wait_ge(*v.at(f"o{h - 1}1"))
            A(rden, bank[6][:, 0:T1], ACT.Abs).then_inc(*a_.mark(f"ab{h}"))
            for d in range(2):
                act.wait_ge(*v.at(f"y{h}{d}"))
                if h:
                    act.wait_ge(*m.at(f"ss{h - 1}"))
                A(hh[2 + d], hh[d], ACT.Square).then_inc(*a_.mark(f"sq{h}{d}"))
            act.wait_ge(*m.at(f"ss{h}"))
            A(rden, bank[3][:, 0:T1], ACT.Ln, bias=eps_1, scale=1.0 / MV).then_inc(*a_.mark(f"ln{h}"))
            act.wait_ge(*a_.at(f"ln{h}"))
            A(rden, rden, ACT.Exp, scale=-0.5).then_inc(*a_.mark(f"rs{h}"))

    def ml_dve(dve):
        m, v, a_, pl = S("ml", "pe"), S("ml", "dve"), S("ml", "act"), S("ml", "pool")
        ts, stt, tt = nc.vector.tensor_scalar, nc.vector.scalar_tensor_tensor, nc.vector.tensor_tensor
        dve.wait_ge(*m.at("ctok"))
        nc.vector.tensor_copy(c_tok[:, 0:8], bank[0][:, 0:8]).then_inc(*v.mark("ctoka"))
        nc.vector.tensor_copy(c_tok[0:16, 8:12], bank[0][0:16, 8:12]).then_inc(*v.mark("ctok"))
        dve.wait_ge(*v.at("ctok"))
        for h in range(MH):
            dve.wait_ge(*m.at(f"rows{h}"))
            if h:
                dve.wait_ge(*v.at(f"P{h - 1}"))
            for b, (lo, n) in enumerate(JB):
                ts(zbuf[0:n, OFF[b]:OFF[b] + T1 - lo], bank[0][0:n, lo:T1], work[0:n, 2180 + 4 * b + h:2181 + 4 * b + h], 0.0,
                   ALU.subtract, ALU.max).then_inc(*v.mark(f"Z{h}" if b == 2 else f"Z{h}{b}"))
            dve.wait_ge(*a_.at(f"E{h}"))
            dve.wait_ge(*m.at(f"S{h}"))
            if h:
                dve.wait_ge(*m.at(f"n{h - 1}2"))
            tt(pbuf[:, 0:416], zbuf[:, 0:416], bank[2][:, 0:416], ALU.mult).then_inc(*v.mark(f"Pa{h}"))
            tt(pbuf[0:16, 416:432], zbuf[0:16, 416:432], bank[2][0:16, 416:432], ALU.mult).then_inc(*v.mark(f"P{h}"))
            dve.wait_ge(*a_.at(f"ab{h}"))
            tt(rden, rden, em, ALU.max).then_inc(*v.mark(f"den{h}"))
            dve.wait_ge(*v.at(f"den{h}"))
            nc.vector.reciprocal(rden, rden).then_inc(*v.mark(f"r{h}"))
            dve.wait_ge(*v.at(f"r{h}"))
            for d in range(2):
                tt(hh[d], bank[4 + d][:, 0:T1], rden, ALU.mult).then_inc(*v.mark(f"y{h}{d}"))
            dve.wait_ge(*a_.at(f"rs{h}"))
            for d in range(2):
                stt(hh[d], hh[d], pv("ml_norm", 2 * h + d), rden, ALU.mult, ALU.mult).then_inc(*v.mark(f"w{h}{d}"))
            for d in range(2):
                dve.wait_ge(*v.at(f"w{h}{d}"))
                tt(mix[:, 2 * h + d, :], hh[d], big[:, 16 + 2 * h + d, :], ALU.mult).then_inc(*v.mark(f"o{h}{d}"))

    def ml_pool(pool):
        v, pl = S("ml", "dve"), S("ml", "pool")
        for h in range(MH):
            pool.wait_ge(*v.at(f"P{h}"))
            for b, (lo, n) in enumerate(JB):
                o = pbuf[0:n, OFF[b]:OFF[b] + n]
                nc.gpsimd.tensor_tensor(o, o, cn("upto")[0:n, 0:n], ALU.mult).then_inc(*pl.mark(f"P{h}" if b == 2 else f"P{h}{b}"))

    X = lambda k: hs[:, k, N_META:T1]
    yt, sqt = (lambda m: y[:, m, 0:T2]), (lambda m: sq[:, m, 0:T2])

    def ln_pe(pe, n):
        name, g = f"ln{n}", G[f"lm{n}"]
        pe.wait_ge(bank_free, g + 1)
        for m in range(KC):
            pe.wait_ge(bank_free, 8 + g - 8 + m + 1)
            last = nc.tensor.matmul(bank[g % 8][:, 0:T2], ones, yt(m), start=(m == 0), stop=(m == KC - 1))
        last.then_inc(*S("norm", "pe").mark(name + "m"))
        pe_sum(pe, name + "v", g + 1, sqt, "act", T2)

    def ln_act(act, n, which, layer):
        name, g = f"ln{n}", G[f"lm{n}"]
        for m in range(KC):
            act.wait_ge(*S("norm", "dve").at(f"{name}_c{m}"))
            nc.scalar.activation(sqt(m), yt(m), ACT.Square).then_inc(*S("norm", "act").mark(f"{name}v_{m}"))
        act.wait_ge(bank_free, 8 + g + 1)
        act_scale(act, name + "v", g + 1, rs[:, 0, 0:T2], T2, D, eps_ln, None)
        for m in range(KC):
            act.wait_ge(*S("norm", "dve").at(f"{name}_g{m}"))
            nc.scalar.activation(X(m), yt(m), ACT.Identity, bias=pv(which, (2 * layer + 1) * KC + m)
                                 ).then_inc(*S("norm", "act").mark(f"{name}_x{m}"))
        if n < 3:
            x_act(act, name)

    def x_act(act, name):
        for m in range(KC):
            if name != "b2":
                act.wait_ge(*S("norm", "act").at(f"{name}_x{m}"))
            nc.scalar.activation(xs[:, m, 0:T2], X(m), ACT.Copy).then_inc(*S("norm", "act").mark(f"{name}_hi{m}"))

    def x_dve(dve, name):
        for m in range(KC):
            dve.wait_ge(*S("norm", "act").at(f"{name}_hi{m}"))
            nc.vector.tensor_tensor(xs[:, KC + m, 0:T2], X(m), xs[:, m, 0:T2].bitcast(F32), ALU.subtract
                                    ).then_inc(*S("norm", "dve").mark(f"{name}_lo{m}"))

    def ln_dve(dve, n, which, layer, last_block):
        name, g = f"ln{n}", G[f"lm{n}"]
        st = S("norm", "dve")
        stt = nc.vector.scalar_tensor_tensor
        dve.wait_ge(block_used, last_block)
        for m in range(KC):
            stt(yt(m), X(m), ALPHA, bank[(g - 8 + m) % 8][:, 0:T2], ALU.mult, ALU.add).then_inc(bank_free, 1)
        dve.wait_ge(*S("norm", "pe").at(name + "m"))
        for m in range(KC):
            stt(yt(m), bank[g % 8][:, 0:T2], -1.0 / D, yt(m), ALU.mult, ALU.add).then_inc(*st.mark(f"{name}_c{m}"))
        dve.wait_ge(*st.at(f"{name}_c7"))
        nc.vector.memset(rs[:, 1, 0:1], 0.0).then_inc(bank_free, 1)
        dve.wait_ge(*S("norm", "act").at(f"{name}v_scale"))
        for m in range(KC):
            stt(yt(m), yt(m), pv(which, 2 * layer * KC + m), rs[:, 0, 0:T2], ALU.mult, ALU.mult).then_inc(*st.mark(f"{name}_g{m}"))
        if n < 3:
            x_dve(dve, name)

    def in_act(act, phase, kinds):
        g0, b0 = G[phase], FIRST_BLOCK[phase]
        for t, (fn, scale) in enumerate(kinds):
            act.wait_ge(block_used, b0 + t + 1)
            nc.scalar.activation(big[:, t, 0:T2], bank[(g0 + t) % 8][:, 0:T2], fn, scale=scale).then_inc(bank_free, 1)
            split_hi(act, b0 + t + AHEAD)

    QB = 2
    probs = work[:, 0:2048]
    ptr = work[:, 2048:4096]
    st8 = lambda k: work[:, 4096 + 8 * k:4104 + 8 * k]
    qrot = [work[0:96, 4160 + h * T2:4160 + (h + 1) * T2] for h in range(4)]
    krot = [work[0:96, 5184 + h * T2:5184 + (h + 1) * T2] for h in range(4)]
    spare = big[:, 18:24, :].rearrange("p a b -> p (a b)")
    vmla = spare[:, 0:1024].rearrange("p (b d) -> p b d", b=2)
    vswa = spare[:, 1024:1280].rearrange("p (b d) -> p b d", b=2)
    krr, tmp96 = work[0:96, 6208:6464], work[0:96, 6464:6720]

    def attn_pe(pe, ph, units, vtok, width, slots):
        m, v, a_ = S(ph, "pe"), S(ph, "dve"), S(ph, "act")
        mm = nc.tensor.matmul
        U = len(units)
        for n in range(QB):
            W = 128 * (n + 1)
            per = 512 // W
            if n:
                pe.wait_ge(*a_.at("out0"))
            for u, (q, k) in enumerate(units):
                b, o = u // per, (u % per) * W
                last = mm(bank[b][:, o:o + W], q[:, n * 128:(n + 1) * 128], k[:, 0:W], start=True, stop=True)
            last.then_inc(*m.mark(f"s{n}"))
            pe.wait_ge(*v.at(f"p{n}"))
            for j in range(n + 1):
                for u in range(U):
                    t = j * U + u
                    last = nc.tensor.transpose(bank[t // 4][:, (t % 4) * 128:(t % 4 + 1) * 128],
                                               probs[:, u * W + j * 128:u * W + (j + 1) * 128], ident)
                    if t % 4 == 3:
                        last.then_inc(*m.mark(f"t{n}_{t // 4}"))
            for t in range((n + 1) * U // 4):
                pe.wait_ge(*a_.at(f"t{n}_{t}"))
            for u in range(U):
                for j in range(n + 1):
                    o, w = vtok(u, j)
                    t = j * U + u
                    last = mm(o, w, ptr[:, t * 128:(t + 1) * 128], start=(j == 0), stop=(j == n))
            last.then_inc(*m.mark(f"o{n}"))

    def attn_act(act, ph, U, sink, slot):
        m, v, a_ = S(ph, "pe"), S(ph, "dve"), S(ph, "act")
        A = nc.scalar.activation
        for n in range(QB):
            W = 128 * (n + 1)
            act.wait_ge(*v.at(f"e{n}"))
            A(probs[:, 0:U * W], probs[:, 0:U * W], ACT.Exp).then_inc(*a_.mark(f"e{n}"))
            if sink:
                A(st8(2), st8(2), ACT.Exp).then_inc(*a_.mark(f"es{n}"))
            for t in range((n + 1) * U // 4):
                act.wait_ge(*m.at(f"t{n}_{t}"))
                A(ptr[:, t * 512:(t + 1) * 512], bank[t][:, :], ACT.Copy).then_inc(*a_.mark(f"t{n}_{t}"))
            act.wait_ge(*m.at(f"o{n}"))
            A(mix[:, slot:slot + 4, n * 128:(n + 1) * 128], bank[7][:, :].rearrange("p (t i) -> p t i", t=4), ACT.Copy
              ).then_inc(*a_.mark(f"out{n}"))

    def attn_dve(dve, ph, U, scale, mask, sink):
        m, v, a_ = S(ph, "pe"), S(ph, "dve"), S(ph, "act")
        ts, stt, tt = nc.vector.tensor_scalar, nc.vector.scalar_tensor_tensor, nc.vector.tensor_tensor
        for n in range(QB):
            W = 128 * (n + 1)
            per = 512 // W
            pr = probs[:, 0:U * W].rearrange("p (u w) -> p u w", u=U)
            mk = (mask if n else mask[:, 128:256]).unsqueeze(1).to_broadcast([P, per, W])
            dve.wait_ge(*m.at(f"s{n}"))
            for b in range(U // per):
                stt(pr[:, b * per:(b + 1) * per, :], bank[b][:, :].rearrange("p (u w) -> p u w", u=per), scale, mk,
                    ALU.mult, ALU.add).then_inc(*v.mark(f"s{n}_{b}"))
            dve.wait_ge(*v.at(f"s{n}_{U // per - 1}"))
            mx, ng, es, sm = (st8(k)[:, 0:U] for k in range(4))
            nc.vector.reduce_max(mx, pr, axis=AX).then_inc(*v.mark(f"mx{n}"))
            dve.wait_ge(*v.at(f"mx{n}"))
            if sink:
                tt(mx, mx, pv("sinks", 0, 8), ALU.max).then_inc(*v.mark(f"ms{n}"))
                dve.wait_ge(*v.at(f"ms{n}"))
                tt(es, pv("sinks", 0, 8), mx, ALU.subtract).then_inc(*v.mark(f"es{n}"))
            tt(pr, pr, mx.unsqueeze(2).to_broadcast([P, U, W]), ALU.subtract).then_inc(*v.mark(f"e{n}"))
            dve.wait_ge(*a_.at(f"e{n}"))
            nc.vector.reduce_sum(sm, pr, axis=AX).then_inc(*v.mark(f"sm{n}"))
            dve.wait_ge(*v.at(f"sm{n}"))
            if sink:
                dve.wait_ge(*a_.at(f"es{n}"))
                tt(sm, sm, es, ALU.add).then_inc(*v.mark(f"sd{n}"))
                dve.wait_ge(*v.at(f"sd{n}"))
            nc.vector.reciprocal(ng, sm).then_inc(*v.mark(f"r{n}"))
            dve.wait_ge(*v.at(f"r{n}"))
            tt(pr, pr, ng.unsqueeze(2).to_broadcast([P, U, W]), ALU.mult).then_inc(*v.mark(f"p{n}"))

    def swa_units():
        return [(big[64 * a:64 * a + 64, 12 + t, 0:T2], big[64 * a:64 * a + 64, 16, 0:T2]) for a in range(2) for t in range(4)]

    def swa_v(u, j):
        a, t = divmod(u, 4)
        return bank[7][64 * a:64 * a + 64, t * 128:(t + 1) * 128], vswa[:, j, 64 * a:64 * a + 64]

    def even_pe(pe):
        m, a_ = S("swa", "pe"), S("swa", "act")
        pe.wait_ge(bank_free, 8 + G["ev_out"])
        for j in range(2):
            last = nc.tensor.transpose(bank[6][:, j * 128:(j + 1) * 128], big[:, 17, j * 128:(j + 1) * 128], ident)
        last.then_inc(*m.mark("vt"))
        attn_pe(pe, "swa", swa_units(), swa_v, 64, 4)

    def even_act(act):
        act.wait_ge(*S("swa", "pe").at("vt"))
        nc.scalar.activation(vswa, bank[6][:, 0:256].rearrange("p (b d) -> p b d", b=2), ACT.Copy).then_inc(*S("swa", "act").mark("vt"))
        attn_act(act, "swa", 8, True, 4)

    def even_pool(pool):
        pl = S("swa", "pool")
        pool.wait_ge(bank_free, 8 + G["ev_out"])
        for t in range(4):
            nc.gpsimd.tensor_tensor(cv[:, t, 0:T2], big[:, 4 + t, 0:T2], big[:, 8 + t, 0:T2], ALU.mult).then_inc(*pl.mark(f"z{t}"))
        for t in range(4):
            pool.wait_ge(*S("swa", "dve").at(f"z{t}_2"))
            nc.gpsimd.tensor_tensor(mix[:, t, 0:T2], cv[:, 4 + t, 0:T2], big[:, t, 0:T2], ALU.mult).then_inc(*pl.mark(f"y{t}"))

    def even_dve(dve):
        v, pl = S("swa", "dve"), S("swa", "pool")
        attn_dve(dve, "swa", 8, 64 ** -0.5, cn("swa_mask"), True)
        for tap in range(3):
            for t in range(4):
                w = pv("ev_conv", 3 * t + 2 - tap)
                o, z = cv[:, 4 + t, 0:T2], cv[:, t, 0:T2]
                if tap == 0:
                    dve.wait_ge(*pl.at(f"z{t}"))
                    nc.vector.tensor_scalar(o, z, w, None, ALU.mult).then_inc(*v.mark(f"z{t}_0"))
                else:
                    dve.wait_ge(*v.at(f"z{t}_{tap - 1}"))
                    nc.vector.scalar_tensor_tensor(o[:, tap:], z[:, 0:T2 - tap], w, o[:, tap:], ALU.mult, ALU.add
                                                   ).then_inc(*v.mark(f"z{t}_{tap}"))

    GR, NG = 16, T2 // 16
    LA, LB, RR = (xf[:, 2 * s:2 * s + 2, 0:T2] for s in range(3))
    QG = xf[:, 6:8, 0:T2]
    KG = [y[:, 2 * s:2 * s + 2, 0:T2] for s in range(4)]
    last_tiles = big[:, 33:48, :].rearrange("p a b -> p (a b)")
    gp = [last_tiles[:, h * 384:384 + h * 384] for h in range(4)]
    vg = last_tiles[:, 1536:2560].rearrange("p (b d) -> p b d", b=2)
    go = [sq[:, h, 0:T2] for h in range(4)]
    gs = [sq[:, 4 + h, 0:T2] for h in range(4)]
    glow = cv[0:16, 0, 0:T2]

    def odd_pe(pe):
        m, v, a_, pl = S("gla", "pe"), S("gla", "dve"), S("gla", "act"), S("gla", "pool")
        mm = nc.tensor.matmul
        pe.wait_ge(bank_free, 8 + G["od_out"])
        pe.wait_ge(*a_.at("glow"))
        for t in range(2):
            last = mm(bank[0][:, t * T2:(t + 1) * T2], pv("gla_w", 128 * t, 128, 16), glow, start=True, stop=True)
        last.then_inc(*m.mark("gate"))
        for h in range(4):
            for j in range(2):
                last = nc.tensor.transpose(bank[1 + j][:, h * 128:(h + 1) * 128], big[:, 4 + h, j * 128:(j + 1) * 128], ident)
        last.then_inc(*m.mark("vt"))
        mla_pe(pe)
        pe.wait_ge(*S("mla", "act").at("out1"))
        pe.wait_ge(*v.at("qg"))
        for g in range(NG):
            pe.wait_ge(*pl.at(f"k{g}"))
            for h in range(4):
                t, a = divmod(h, 2)
                rows = slice(64 * a, 64 * a + 64)
                for j in range(1 if g < 8 else 2):
                    o = (0 if j == 0 else 128) + 16 * g
                    last = mm(bank[3 + h][:, o:o + 16], KG[g % 4][rows, t, j * 128:(j + 1) * 128], QG[rows, t, 16 * g:16 * g + 16],
                              start=True, stop=True)
            last.then_inc(*m.mark(f"s{g}"))
        for h in range(4):
            pe.wait_ge(*v.at(f"p{h}"))
            b = (0, 1, 2, 7)[h]
            mm(bank[b][:, 0:T2], vg[:, 0, h * 128:(h + 1) * 128], gp[h][:, 0:T2], start=True, stop=False)
            mm(bank[b][:, 128:T2], vg[:, 1, h * 128:(h + 1) * 128], gp[h][:, T2:T2 + 128], start=False, stop=True
               ).then_inc(*m.mark(f"o{h}"))
        for h in range(4):
            pe.wait_ge(*a_.at(f"sq{h}"))
            mm(bank[3 + h][:, 0:T2], ones, gs[h], start=True, stop=True).then_inc(*m.mark(f"ss{h}"))

    def odd_gate_act(act):
        act.wait_ge(*S("gates", "pe").at("od0"))
        nc.scalar.activation(glow, bank[G["od_g"] % 8][0:16, 0:T2], ACT.Copy).then_inc(bank_free, 1)

    def odd_act(act):
        m, v, a_, pl = S("gla", "pe"), S("gla", "dve"), S("gla", "act"), S("gla", "pool")
        A = nc.scalar.activation
        act.wait_ge(bank_free, 8 + G["od_g"] + 1)
        A(rs[:, 1, 0:1], eps_1, ACT.Copy).then_inc(*a_.mark("glow"))
        act.wait_ge(*m.at("gate"))
        for t in range(2):
            A(LA[:, t, :], bank[0][:, t * T2:(t + 1) * T2], ACT.Identity, bias=pv("gla_b", t)).then_inc(*a_.mark(f"x{t}"))
        act.wait_ge(*a_.at("x1"))
        A(LB, LA, ACT.Abs).then_inc(*a_.mark("abs"))
        act.wait_ge(*a_.at("abs"))
        A(LB, LB, ACT.Exp, scale=-1.0).then_inc(*a_.mark("e"))
        act.wait_ge(*a_.at("e"))
        A(LB, LB, ACT.Ln, bias=1.0).then_inc(*a_.mark("ln"))
        act.wait_ge(*m.at("vt"))
        for j in range(2):
            A(vg[:, j, :], bank[1 + j][:, :], ACT.Copy).then_inc(*a_.mark(f"vt{j}"))
        mla_act(act)
        act.wait_ge(*v.at("dq"))
        A(QG, QG, ACT.Exp).then_inc(*a_.mark("qg"))
        for g in range(NG):
            W = 128 if g < 8 else 256
            act.wait_ge(*v.at(f"k{g}"))
            A(KG[g % 4][:, :, 0:W], KG[g % 4][:, :, 0:W], ACT.Exp, scale=-1.0).then_inc(*a_.mark(f"k{g}"))
        for h in range(4):
            act.wait_ge(*m.at(f"o{h}"))
            A(gs[h], bank[(0, 1, 2, 7)[h]][:, 0:T2], ACT.Square).then_inc(*a_.mark(f"sq{h}"))
        for h in range(4):
            act.wait_ge(*m.at(f"ss{h}"))
            A(gs[h], bank[3 + h][:, 0:T2], ACT.Ln, scale=1.0 / 128, bias=eps_1).then_inc(*a_.mark(f"l{h}"))
        for h in range(4):
            act.wait_ge(*a_.at(f"l{h}"))
            A(gs[h], gs[h], ACT.Exp, scale=-0.5).then_inc(*a_.mark(f"r{h}"))

    def odd_dve(dve):
        m, v, a_, pl = S("gla", "pe"), S("gla", "dve"), S("gla", "act"), S("gla", "pool")
        ts, stt, tt = nc.vector.tensor_scalar, nc.vector.scalar_tensor_tensor, nc.vector.tensor_tensor
        dve.wait_ge(*a_.at("ln"))
        ts(LA, LA, 0.0, 1.0 / 16, ALU.min, ALU.mult).then_inc(*v.mark("min"))
        dve.wait_ge(*v.at("min"))
        stt(LA, LB, -1.0 / 16, LA, ALU.mult, ALU.add).then_inc(*v.mark("la"))
        dve.wait_ge(*v.at("la"))
        b = scan(dve, v, "b", LA, LB, ALU.add, T2)
        groups = lambda ap: ap.rearrange("p t (g k) -> p t g k", k=GR)
        r = RR[:, :, 0:NG]
        nc.vector.memset(r[:, :, 0:1], 0.0).then_inc(*v.mark("r0"))
        nc.vector.tensor_copy(r[:, :, 1:NG], groups(b)[:, :, 0:NG - 1, GR - 1]).then_inc(*v.mark("r"))
        dve.wait_ge(*v.at("r"))
        tt(groups(QG), groups(b), r.unsqueeze(3).to_broadcast([P, 2, NG, GR]), ALU.subtract).then_inc(*v.mark("dq"))
        mla_dve(dve)
        dve.wait_ge(*a_.at("qg"))
        tt(QG, QG, big[:, 0:2, 0:T2], ALU.mult).then_inc(*v.mark("qg"))
        for g in range(NG):
            W = 128 if g < 8 else 256
            if g >= 4:
                dve.wait_ge(*m.at(f"s{g - 4}"))
            for t in range(2):
                ts(KG[g % 4][:, t, 0:W], b[:, t, 0:W], RR[:, t, g:g + 1], -80.0, ALU.subtract, ALU.max
                   ).then_inc(*v.mark(f"k{g}" if t else f"k{g}a"))
        dve.wait_ge(*m.at(f"s{NG - 1}"))
        for h in range(4):
            tt(gp[h][:, 0:128], bank[3 + h][:, 0:128], cn("upto"), ALU.mult).then_inc(*v.mark(f"pa{h}"))
            nc.vector.tensor_copy(gp[h][:, 128:256], bank[3 + h][:, 128:256]).then_inc(*v.mark(f"pb{h}"))
            tt(gp[h][:, 256:384], bank[3 + h][:, 256:384], cn("upto"), ALU.mult).then_inc(*v.mark(f"p{h}"))
        for h in range(4):
            dve.wait_ge(*a_.at(f"r{h}"))
            tt(go[h], bank[(0, 1, 2, 7)[h]][:, 0:T2], gs[h], ALU.mult).then_inc(*v.mark(f"y{h}"))
        for h in range(4):
            dve.wait_ge(*v.at(f"y{h}"))
            stt(mix[:, h, 0:T2], go[h], pv("gla_norm"), big[:, 8 + h, 0:T2], ALU.mult, ALU.mult).then_inc(*v.mark(f"o{h}"))

    def odd_pool(pool):
        m, v, a_, pl = S("gla", "pe"), S("gla", "dve"), S("gla", "act"), S("gla", "pool")
        for g in range(NG):
            W = 128 if g < 8 else 256
            pool.wait_ge(*a_.at(f"k{g}"))
            nc.gpsimd.tensor_tensor(KG[g % 4][:, :, 0:W], KG[g % 4][:, :, 0:W], big[:, 2:4, 0:W], ALU.mult).then_inc(*pl.mark(f"k{g}"))

    cq = [cv[:, 1 + t, 0:T2] for t in range(2)]
    ckv = cv[:, 3, 0:T2]
    csq = [cv[:, 4 + t, 0:T2] for t in range(3)]
    crs = [cv[:, 7, 0:T2], rs[:, 1, 0:T2]]
    MLAW = big[:, 24:33, :].rearrange("p a b -> p (a b)")[:, 0:2304]

    def mla_pe(pe):
        m, v, a_ = S("mla", "pe"), S("mla", "dve"), S("mla", "act")
        mm = nc.tensor.matmul
        pe.wait_ge(*a_.at("sq"))
        for t in range(2):
            last = mm(bank[3][:, 0:T2], ones, csq[t], start=(t == 0), stop=(t == 1))
        last = mm(bank[4][:, 0:T2], ones, csq[2], start=True, stop=True)
        last.then_inc(*m.mark("ss"))
        pe.wait_ge(*v.at("ckv"))
        pe.wait_ge(mla_loaded, 16)
        B = (0, 5, 6, 7)
        for h in range(4):
            if h == 0:
                pe.wait_ge(*S("gla", "act").at("x1"))
            for s in range(2):
                for t in range(2):
                    last = mm(bank[B[h]][0:96, s * T2:(s + 1) * T2], MLAW[:, 768 * s + 384 * t + 96 * h:768 * s + 384 * t + 96 * h + 96],
                              cq[t], start=(t == 0), stop=(t == 1))
            last.then_inc(*m.mark(f"q{h}"))
        pe.wait_ge(*S("gla", "act").at("vt1"))
        for h in range(4):
            last = mm(bank[1 + h // 2][0:64, (h % 2) * T2:(h % 2 + 1) * T2], MLAW[:, 1536 + 64 * h:1600 + 64 * h], ckv, start=True, stop=True)
        last.then_inc(*m.mark("k"))
        pe.wait_ge(*a_.at("rkv"))
        for j in range(2):
            last = mm(bank[3 + j][:, :], ckv[:, j * 128:(j + 1) * 128], MLAW[:, 1792:2304], start=True, stop=True)
        last.then_inc(*m.mark("v"))
        pe.wait_ge(*v.at("q3"))
        pe.wait_ge(*a_.at("v1"))
        units = [(qrot[h], krot[h]) for h in range(4)]
        attn_pe(pe, "mla", units, lambda u, j: (bank[7][:, u * 128:(u + 1) * 128], vmla[:, j, u * 128:(u + 1) * 128]), 128, 4)

    def mla_act(act):
        m, v, a_ = S("mla", "pe"), S("mla", "dve"), S("mla", "act")
        A = nc.scalar.activation
        for t in range(3):
            last = A(csq[t], big[:, 12 + t, 0:T2], ACT.Square)
        last.then_inc(*a_.mark("sq"))
        act.wait_ge(*m.at("ss"))
        for n, name in enumerate(("q", "kv")):
            A(crs[n], bank[3 + n][:, 0:T2], ACT.Ln, scale=1.0 / (256, 128)[n], bias=eps_1).then_inc(*a_.mark(f"l{name}"))
        for n, name in enumerate(("q", "kv")):
            act.wait_ge(*a_.at(f"l{name}"))
            A(crs[n], crs[n], ACT.Exp, scale=-0.5).then_inc(*a_.mark(f"r{name}"))
        act.wait_ge(*m.at("k"))
        for h in range(4):
            A(krot[h][0:64], bank[1 + h // 2][0:64, (h % 2) * T2:(h % 2 + 1) * T2], ACT.Copy).then_inc(*a_.mark(f"k{h}"))
        act.wait_ge(*m.at("v"))
        for j in range(2):
            A(vmla[:, j, :], bank[3 + j][:, :], ACT.Copy).then_inc(*a_.mark(f"v{j}"))
        attn_act(act, "mla", 4, False, 4)

    def mla_dve(dve):
        m, v, a_ = S("mla", "pe"), S("mla", "dve"), S("mla", "act")
        ts, stt, tt = nc.vector.tensor_scalar, nc.vector.scalar_tensor_tensor, nc.vector.tensor_tensor
        dve.wait_ge(*a_.at("rkv"))
        for t in range(2):
            stt(cq[t], big[:, 12 + t, 0:T2], pv("mla_qn", t), crs[0], ALU.mult, ALU.mult).then_inc(*v.mark(f"cq{t}"))
        stt(ckv, big[:, 14, 0:T2], pv("mla_kvn"), crs[1], ALU.mult, ALU.mult).then_inc(*v.mark("ckv"))
        cos, sin = cn("cos", 96), cn("sin", 96)
        tt(krr[64:96], big[64:96, 15, 0:T2], cos[64:96], ALU.mult).then_inc(*v.mark("kr0"))
        tt(tmp96[64:96], big[64:96, 16, 0:T2], sin[64:96], ALU.mult).then_inc(*v.mark("kr1"))
        dve.wait_ge(*v.at("kr1"))
        for h in range(4):
            tt(krot[h][64:96], krr[64:96], tmp96[64:96], ALU.add).then_inc(*v.mark(f"kr{h + 2}"))
        for h in range(4):
            bk = bank[(0, 5, 6, 7)[h]]
            dve.wait_ge(*m.at(f"q{h}"))
            tt(qrot[h], bk[0:96, 0:T2], cos, ALU.mult).then_inc(*v.mark(f"qa{h}"))
            dve.wait_ge(*v.at(f"q{h - 1}" if h else "kr5"))
            tt(tmp96, bk[0:96, T2:2 * T2], sin, ALU.mult).then_inc(*v.mark(f"qb{h}"))
            dve.wait_ge(*v.at(f"qb{h}"))
            tt(qrot[h], qrot[h], tmp96, ALU.add).then_inc(*v.mark(f"q{h}"))
        attn_dve(dve, "mla", 4, 96 ** -0.5, cn("mla_mask"), False)
    con_eps = sb("con_eps", [P, 4])

    def sp_out(sp):
        o = out.rearrange("p (c t) -> p c t", t=T2)
        for m in range(KC):
            sp.wait_ge(*S("norm", "act").at(f"ln3_x{m}"))
            sp.dma_start(o[:, m, :], X(m)).then_inc(stored, 16)
        sp.wait_ge(stored, 16 * KC)

    eps_1 = con_eps[:, 0:1]
    eps_q = con_eps[:, 1:2]
    eps_ln = con_eps[:, 2:3]
    block = ctx.enter_context(nc.Block())
    xk = lambda k: y[:, k, :]

    def mix_ready(name):
        return lambda pe, k, i: pe.wait_ge(*S("norm", "dve").at(f"{name}_lo{k}"))

    def even_done(e):
        e.wait_ge(*S("swa", "pool").at("y3"))
        e.wait_ge(*S("swa", "act").at("out1"))

    def odd_done(e):
        e.wait_ge(*S("gla", "dve").at("o3"))
        e.wait_ge(*S("mla", "act").at("out1"))

    mix1 = lambda k: mix[:, k, :]
    mix2 = lambda k: mix[:, k, 0:T2]

    @block.sync
    def _(sp):
        sp_stream(sp)
        sp_out(sp)

    @block.gpsimd
    def _(pool):
        nc.gpsimd.memset(con_eps[:, 2:3], LN_EPS).then_inc(*S("init", "pool").mark("epsln"))
        nc.gpsimd.memset(con_eps[:, 0:1], RMS_EPS).then_inc(*S("init", "pool").mark("eps"))
        nc.gpsimd.memset(con_eps[:, 1:2], L2_EPS * GD).then_inc(*S("init", "pool").mark("epsq"))
        gdn_pool(pool)
        ffn_pool(pool, 0, G["up0"])
        ml_pool(pool)
        ffn_pool(pool, 1, G["up1"])
        even_pool(pool)
        ffn_pool(pool, 2, G["up2"])
        odd_pool(pool)
        ffn_pool(pool, 3, G["up3"])

    @block.scalar
    def _(act):
        act.wait_ge(hs_loaded, 16)
        act.wait_ge(loaded, 32)
        act.wait_ge(*S("init", "pool").at("epsq"))
        for n in range(AHEAD):
            split_hi(act, n)
        pre_act(act, "pre0", G["pre0"], lambda act, m: None)
        gdn_gates_act(act)
        gdn_in_act(act)
        gdn_act(act)
        mix_act(act, "gdn", lambda k: big[:, 32 + k, :], 16, lambda e: e.wait_ge(*S("gdn", "dve").at("o1")))
        split_all(act, split_hi, "gdn_out")
        post_act(act, "post0", G["post0"])
        pre_act(act, "pre1", G["pre1"], lambda act, m: act.wait_ge(*S("norm", "dve").at(f"post0_h{m}")))
        ffn_act(act, 0, G["up0"])
        split_all(act, split_hi, "down0")
        post_act(act, "post1", G["post1"])
        pre_act(act, "pre2", G["pre2"], lambda act, m: act.wait_ge(*S("norm", "dve").at(f"post1_h{m}")))
        ml_gates_act(act)
        ml_in_act(act)
        ml_act(act)
        mix_act(act, "ml", mix1, 8, lambda e: e.wait_ge(*S("ml", "dve").at("o31")))
        split_all(act, split_hi, "ml_out")
        post_act(act, "post2", G["post2"])
        pre_act(act, "pre3", G["pre3"], lambda act, m: act.wait_ge(*S("norm", "dve").at(f"post2_h{m}")))
        ffn_act(act, 1, G["up1"])
        split_all(act, split_hi, "down1")
        post_act(act, "post3", G["post3"])
        act.wait_ge(*S("norm", "dve").at("post3_h7"))
        x_act(act, "b2")
        in_act(act, "ev_in", [(ACT.Copy, 1.0)] * 18)
        even_act(act)
        mix_act(act, "ev", mix2, 8, even_done)
        split_all(act, split_hi, "ev_out")
        ln_act(act, 0, "ln_mix", 0)
        ffn_act(act, 2, G["up2"])
        split_all(act, split_hi, "down2")
        ln_act(act, 1, "ln_ffn", 0)
        act.wait_ge(block_used, used_after("down2"))
        act.dma_start(MLAW, mla).then_inc(mla_loaded, 16)
        odd_gate_act(act)
        in_act(act, "od_in", [(ACT.Copy, 0.125)] * 2 + [(ACT.Copy, 1.0)] * 6 + [(ACT.Silu, 1.0)] * 4 + [(ACT.Copy, 1.0)] * 5)
        odd_act(act)
        mix_act(act, "od", mix2, 8, odd_done)
        split_all(act, split_hi, "od_out")
        ln_act(act, 2, "ln_mix", 1)
        ffn_act(act, 3, G["up3"])
        split_all(act, split_hi, "down3")
        ln_act(act, 3, "ln_ffn", 1)

    @block.vector
    def _(dve):
        nc.vector.memset(rs[:, 0, 0:1], 0.0).then_inc(bank_free, 8)
        nc.vector.memset(rs[:, 1, 0:1], 0.0).then_inc(conv_taken, 8)
        dve.wait_ge(loaded, 32)
        for n in range(AHEAD):
            split_lo(dve, n)
        pre_dve(dve, "pre0", 0)
        gdn_in_dve(dve)
        gdn_dve(dve)
        mix_dve(dve, "gdn", lambda k: big[:, 32 + k, :], 16, lambda e: e.wait_ge(*S("gdn", "dve").at("o1")))
        split_all(dve, split_lo, "gdn_out")
        post_dve(dve, "post0", G["post0"], 1, used_after("gdn_out"))
        pre_dve(dve, "pre1", 2)
        ffn_dve(dve, 0, G["up0"])
        split_all(dve, split_lo, "down0")
        post_dve(dve, "post1", G["post1"], 3, used_after("down0"))
        pre_dve(dve, "pre2", 4)
        ml_gates_dve(dve)
        split_all(dve, split_lo, "ml_in")
        ml_dve(dve)
        mix_dve(dve, "ml", mix1, 8, lambda e: e.wait_ge(*S("ml", "dve").at("o31")))
        split_all(dve, split_lo, "ml_out")
        post_dve(dve, "post2", G["post2"], 5, used_after("ml_out"))
        pre_dve(dve, "pre3", 6)
        ffn_dve(dve, 1, G["up1"])
        split_all(dve, split_lo, "down1")
        post_dve(dve, "post3", G["post3"], 7, used_after("down1"))
        x_dve(dve, "b2")
        split_all(dve, split_lo, "ev_in")
        even_dve(dve)
        mix_dve(dve, "ev", mix2, 8, even_done)
        split_all(dve, split_lo, "ev_out")
        ln_dve(dve, 0, "ln_mix", 0, used_after("ev_out"))
        ffn_dve(dve, 2, G["up2"])
        split_all(dve, split_lo, "down2")
        ln_dve(dve, 1, "ln_ffn", 0, used_after("down2"))
        split_all(dve, split_lo, "od_in")
        odd_dve(dve)
        mix_dve(dve, "od", mix2, 8, odd_done)
        split_all(dve, split_lo, "od_out")
        ln_dve(dve, 2, "ln_mix", 1, used_after("od_out"))
        ffn_dve(dve, 3, G["up3"])
        split_all(dve, split_lo, "down3")
        ln_dve(dve, 3, "ln_ffn", 1, used_after("down3"))

    @block.tensor
    def _(pe):
        pe.wait_ge(loaded, 32)
        pre_pe(pe, "pre0", G["pre0"])
        pe.wait_ge(*S("norm", "dve").at("pre0_lo7"))
        gates_pe(pe, "gdn", G["gdn_g"], ((0, 16), (16, 16)), "gdn_gates", 32, T1, xk)
        pe_tiles(pe, "gdn_in", G["gdn_in"])
        gdn_pe(pe)
        pe_wide(pe, "gdn_out", G["gdn_out"], mix_ready("gdn"))
        post_pe(pe, "post0", G["post0"])
        pre_pe(pe, "pre1", G["pre1"])
        pe.wait_ge(*S("norm", "dve").at("pre1_lo7"))
        pe_tiles(pe, "up0", G["up0"])
        pe_wide(pe, "down0", G["down0"], ffn_ready(0))
        post_pe(pe, "post1", G["post1"])
        pre_pe(pe, "pre2", G["pre2"])
        pe.wait_ge(*S("norm", "dve").at("pre2_lo7"))
        gates_pe(pe, "ml", G["ml_g"], ((0, 4), (4, 4)), "ml_gates", 8, T1, xk)
        pe_tiles(pe, "ml_in", G["ml_in"])
        ml_pe(pe)
        pe_wide(pe, "ml_out", G["ml_out"], mix_ready("ml"))
        post_pe(pe, "post2", G["post2"])
        pre_pe(pe, "pre3", G["pre3"])
        pe.wait_ge(*S("norm", "dve").at("pre3_lo7"))
        pe_tiles(pe, "up1", G["up1"])
        pe_wide(pe, "down1", G["down1"], ffn_ready(1))
        post_pe(pe, "post3", G["post3"])
        pe.wait_ge(*S("norm", "dve").at("b2_lo7"))
        pe_tiles(pe, "ev_in", G["ev_in"])
        even_pe(pe)
        pe_wide(pe, "ev_out", G["ev_out"], mix_ready("ev"))
        ln_pe(pe, 0)
        pe.wait_ge(*S("norm", "dve").at("ln0_lo7"))
        pe_tiles(pe, "up2", G["up2"])
        pe_wide(pe, "down2", G["down2"], ffn_ready(2))
        ln_pe(pe, 1)
        pe.wait_ge(*S("norm", "dve").at("ln1_lo7"))
        gates_pe(pe, "od", G["od_g"], ((0, 16),), "g_low", 16, T2, X)
        pe_tiles(pe, "od_in", G["od_in"])
        odd_pe(pe)
        pe_wide(pe, "od_out", G["od_out"], mix_ready("od"))
        ln_pe(pe, 2)
        pe.wait_ge(*S("norm", "dve").at("ln2_lo7"))
        pe_tiles(pe, "up3", G["up3"])
        pe_wide(pe, "down3", G["down3"], ffn_ready(3))
        ln_pe(pe, 3)
    ctx.close()

INPUTS = ["stream", "params", "consts", "mla", "hs"]


def kernel(**inputs):
    import concourse.bacc as bacc
    from concourse.bass_utils import run_bass_kernel_spmd

    table = {}
    for _ in range(2):
        nc = bacc.Bacc("TRN2", target_bir_lowering=False, num_devices=1)
        aps = [nc.dram_tensor(name, SHAPES[name], F32, kind="ExternalInput").ap() for name in INPUTS]
        out = nc.dram_tensor("y_out", (P, KC * T2), F32, kind="ExternalOutput").ap()
        build(nc, *aps, out, table)
    arrays = lay_out({name: np.asarray(v) for name, v in inputs.items()})
    result = run_bass_kernel_spmd(nc, [arrays], core_ids=[0]).results[0]["y_out"]
    return np.ascontiguousarray(result.reshape(P, KC, T2).transpose(2, 1, 0).reshape(1, T2, D))
```

```python
import math
from contextlib import ExitStack

import numpy as np

import concourse.bass as bass
from concourse import mybir
from concourse.alu_op_type import AluOpType as ALU

F32 = mybir.dt.float32
F32R = mybir.dt.float32r
ACT = mybir.ActivationFunctionType
AX = mybir.AxisListType.X

P = 128
D = 1024
KC = D // P
N_META, SEQ = 16, 256
T1 = N_META + SEQ
T2 = SEQ
RMS_EPS = L2_EPS = 1e-6
LN_EPS = 1e-5

GK, GV, GD = 8, 16, 128
CHUNKS = ((0, T1 % P), (T1 % P, P), (T1 % P + P, P))
NCH, HEAD_T = len(CHUNKS), T1 % P
LEVELS = [1 << s for s in range(7)]
SHORT_LAST = HEAD_T.bit_length() - 2
LAST = len(LEVELS) - 1
MH, MV = 4, 256
LN_EXP = "natural_log_exp_and_others"
SILU = "silu_and_others"
GATE_CAP = 15.0
FF = 2816
FC = FF // P
ALPHA = 4.0 ** 0.25
NEG = -1.0e30
WORK = 6720

SLOTS = 4
AHEAD = 3
BLOCK = 8 * P


class Steps:

    def __init__(self, sem, table, key):
        self.sem, self.seen, self.key = sem, 0, key
        self.table = table.setdefault(key, {})
        self.loop = None

    def mark(self, name):
        self.seen += 1
        if self.loop:
            self.table[name] = (self.loop[0], self.seen, None, self.loop[1])
        else:
            self.table[name] = (0, self.seen, 0, 1)
        return self.sem, 1

    def repeat(self, times):
        return _Repeat(self, times)

    def at(self, name, i=None):
        if name not in self.table:
            return self.sem, 1
        base, seen, per, times = self.table[name]
        per = self.table[("per", base)] if per is None and ("per", base) in self.table else (per or 0)
        if i is None:
            return self.sem, base + (times - 1) * per + seen
        return self.sem, i * per + (base + seen)

    def before(self, i):
        base = self.table.get("loop_base", 0)
        return self.sem, i * self.table.get(("per", base), 0) + base


class _Repeat:
    def __init__(self, steps, times):
        self.s, self.times = steps, times

    def __enter__(self):
        s = self.s
        self.base = s.seen
        s.table["loop_base"] = self.base
        s.loop, s.seen = (self.base, self.times), 0
        return self

    def __exit__(self, *_):
        s = self.s
        s.table[("per", self.base)] = s.seen
        s.seen, s.loop = self.base + self.times * s.seen, None


def vec_tiles(n):
    return n // P


PARAMS = [
    ("norm_w", 8 * KC), ("gdn_conv", 32 * 4), ("gdn_norm", 1), ("ml_norm", 8),
    ("ffn0", 44 * 4), ("ffn1", 44 * 4), ("ev_conv", 4 * 3), ("gla_b", 2), ("gla_norm", 1),
    ("mla_qn", 2), ("mla_kvn", 1), ("ln_mix", 2 * 2 * KC), ("ln_ffn", 2 * 2 * KC), ("sinks", 8),
    ("gdn_a_log", 1), ("gdn_dt", 1), ("ml_ib", 1), ("ml_fb", 1),
    ("gdn_gates", KC * 32), ("ml_gates", KC * 8), ("g_low", KC * 16), ("gla_w", 256),
]
AT, _n = {}, 0
for _name, _cols in PARAMS:
    AT[_name] = (_n, _n + _cols)
    _n += _cols
NPARAM = _n

CONSTS = [
    ("ident", 128), ("ones", 128), ("upto", 128), ("neg_chunk", P), ("levels", len(LEVELS) * P), ("level0_t", P),
    ("swa_mask", 256), ("mla_mask", 256), ("cos", T2), ("sin", T2),
]
CAT, _n = {}, 0
for _name, _cols in CONSTS:
    CAT[_name] = (_n, _n + _cols)
    _n += _cols
NCONST = _n

PHASES = [("gdn_in", "tiles", 48), ("gdn_out", "wide", 16), ("up0", "tiles", 44), ("down0", "wide", 22),
          ("ml_in", "tiles", 24), ("ml_out", "wide", 8), ("up1", "tiles", 44), ("down1", "wide", 22),
          ("ev_in", "tiles", 18), ("ev_out", "wide", 8), ("up2", "tiles", 44), ("down2", "wide", 22),
          ("od_in", "tiles", 17), ("od_out", "wide", 8), ("up3", "tiles", 44), ("down3", "wide", 22)]
FIRST_BLOCK, _n = {}, 0
for _name, _kind, _count in PHASES:
    FIRST_BLOCK[_name] = _n
    _n += _count
NBLOCKS = _n
COUNT = {n: c for n, _, c in PHASES}


def constants():
    c = np.zeros((P, NCONST), np.float32)
    r, q = np.arange(P)[:, None], np.arange(P)[None]
    put = lambda name, a: c[:a.shape[0], CAT[name][0]:CAT[name][0] + a.shape[1]].__setitem__(slice(None), a)
    put("ident", np.eye(P, dtype=np.float32))
    put("ones", np.ones((P, P), np.float32))
    put("upto", (r <= q).astype(np.float32))
    put("neg_chunk", np.where(r <= q, 0, NEG).astype(np.float32))
    i, j = r, q
    put("levels", np.concatenate([((i // (2 * s) == j // (2 * s)) & (i // s % 2 == 1) & (j // s % 2 == 0))
                                  .astype(np.float32) for s in LEVELS], 1))
    put("level0_t", ((i % 2 == 0) & (j == i + 1)).astype(np.float32))
    same = np.where(q <= r, 0, NEG).astype(np.float32)
    put("swa_mask", np.concatenate([np.where(q > r, 0, NEG).astype(np.float32), same], 1))
    put("mla_mask", np.concatenate([0 * same, same], 1))
    freq = 10000.0 ** (-np.arange(0, 32, 2, dtype=np.float32) / 32)
    ang = (np.arange(T2, dtype=np.float32)[:, None] * freq[None]).T
    cos, sin = np.ones((96, T2), np.float32), np.zeros((96, T2), np.float32)
    cos[64:80] = cos[80:96] = np.cos(ang)
    sin[64:80], sin[80:96] = -np.sin(ang), np.sin(ang)
    put("cos", cos)
    put("sin", sin)
    return c


def tile_blocks(w):
    n = w.shape[1] // P
    return w.reshape(KC, P, n, P).transpose(2, 1, 0, 3).reshape(n, P, BLOCK)


def wide_blocks(w):
    return w.reshape(-1, P, BLOCK)


SWAP = np.r_[16:32, 0:16]


def lay_out(a):
    f = FF
    stream, cols = [], {}
    gw = a["gdn_w_in"][0]
    stream += [tile_blocks(gw[:, :6144]), wide_blocks(a["gdn_w_out"][0])]
    mw = a["ml_w_in"][0]

    def ffn(gate, up, down):
        both = np.stack([gate.reshape(D, FC, P), up.reshape(D, FC, P)], 2).reshape(D, 2 * f)
        return [tile_blocks(both), wide_blocks(down)]

    ev, od = a["ev_w_in_2"][0], a["od_w_in_2"][0]
    heads = np.arange(1536, 2048).reshape(8, 64)
    order = np.concatenate([np.r_[heads[t], heads[t + 4]] for t in range(4)])
    evw = np.concatenate([ev[:, :1536], ev[:, order], ev[:, 2048:]], 1)
    evo = a["ev_w_out_2"][0]
    evo = np.concatenate([evo[:512], evo[order - 1024]], 0)
    kr = od[:, 1936:1968]
    odw = np.concatenate([od[:, :1024], od[:, 1040:1936]] + [kr] * 4 + [kr[:, SWAP]] * 4, 1)
    u = a["ffn_w_up"]
    stream += ffn(u[0, :, :f], u[0, :, f:], a["ffn_w_down"][0])
    stream += [tile_blocks(mw[:, :3072]), wide_blocks(a["ml_w_out"][0])]
    stream += ffn(u[1, :, :f], u[1, :, f:], a["ffn_w_down"][1])
    stream += [tile_blocks(evw), wide_blocks(evo)]
    g2, u2, d2 = a["ffn_w_gate_2"], a["ffn_w_up_2"], a["ffn_w_down_2"]
    stream += ffn(g2[0], u2[0], d2[0])
    stream += [tile_blocks(odw), wide_blocks(a["od_w_out_2"][0])]
    stream += ffn(g2[1], u2[1], d2[1])
    stream = np.concatenate(stream, 0)
    assert stream.shape == (NBLOCKS, P, BLOCK)

    params = np.zeros((P, NPARAM), np.float32)

    def put(name, v):
        params[:v.shape[0], AT[name][0]:AT[name][1]] = v

    def per_tile(v):
        return v.reshape(v.shape[0], -1, P).transpose(2, 1, 0).reshape(P, -1)

    def rows(v):
        return v.reshape(-1, P).T

    put("norm_w", rows(a["norm_w"].reshape(8, D)))
    put("gdn_conv", per_tile(a["gdn_conv_w"][0]))
    put("gdn_norm", a["gdn_norm_w"][0][:, None])
    put("ml_norm", rows(a["ml_norm_w"]))
    for n in range(2):
        cw = np.concatenate([a["ffn_conv_w"][n], a["ffn_conv_b"][n][None]], 0)
        both = np.stack([cw[:, :f].reshape(4, FC, P), cw[:, f:].reshape(4, FC, P)], 2).reshape(4, 2 * f)
        put(f"ffn{n}", per_tile(both))
    put("ev_conv", per_tile(a["ev_conv_w_2"][0]))
    put("gla_b", rows(a["od_gla_b_gate_2"]))
    put("gla_norm", a["od_gla_norm_g_2"][0][:, None])
    put("mla_qn", rows(a["od_mla_q_norm_g_2"]))
    put("mla_kvn", rows(a["od_mla_kv_norm_g_2"]))
    for name in ("ln_mix", "ln_ffn"):
        put(name, rows(np.stack([a[name + "_g_2"], a[name + "_b_2"]], 1).reshape(4, D)))
    put("sinks", np.broadcast_to(a["ev_sinks_2"], (P, 8)))
    put("gdn_a_log", a["gdn_a_log"][0][:, None])
    put("gdn_dt", a["gdn_dt_bias"][0][:, None])
    put("ml_ib", a["ml_gate_b"][0, :4][:, None])
    put("ml_fb", a["ml_gate_b"][0, 4:][:, None])
    put("gdn_gates", gw[:, 6144:].reshape(KC, P, 32).transpose(1, 0, 2).reshape(P, -1))
    put("ml_gates", mw[:, 3072:].reshape(KC, P, 8).transpose(1, 0, 2).reshape(P, -1))
    put("g_low", od[:, 1024:1040].reshape(KC, P, 16).transpose(1, 0, 2).reshape(P, -1))
    put("gla_w", a["od_gla_w_gate_2"][0])

    uq = a["od_mla_w_uq_2"][0]
    swapped = uq.reshape(256, 4, 96)[:, :, np.r_[0:64, 64 + SWAP]].reshape(256, 384)
    ukv = a["od_mla_w_ukv_2"][0].reshape(P, 4, 192)
    mla = np.concatenate([uq.reshape(2, P, 384).transpose(1, 0, 2).reshape(P, -1),
                          swapped.reshape(2, P, 384).transpose(1, 0, 2).reshape(P, -1),
                          ukv[:, :, :64].reshape(P, 256), ukv[:, :, 64:].reshape(P, 512)], 1)
    hs = np.concatenate([a["meta_tokens"], a["x"][0]], 0).T.reshape(KC, P, T1).transpose(1, 0, 2)
    return {name: np.ascontiguousarray(v) for name, v in dict(
        stream=stream, params=params, consts=constants(), mla=mla, hs=hs.reshape(P, -1)).items()}


SHAPES = dict(stream=(NBLOCKS, P, BLOCK), params=(P, NPARAM), consts=(P, NCONST), mla=(P, 2304),
              hs=(P, KC * T1))


def build(nc, stream, params, consts, mla, hs_in, out, table):
    ctx = ExitStack()

    def sb(name, shape):
        return ctx.enter_context(nc.sbuf_tensor(name, shape, F32))

    def sem(name):
        return ctx.enter_context(nc.semaphore(name))

    def shared(name, shape, other, other_shape):
        with nc.sbuf_tensor(name, shape, F32) as first:
            pass
        return first, ctx.enter_context(nc.sbuf_tensor(other, other_shape, F32R))

    raw = sb("raw", [P, SLOTS, BLOCK])
    whi = ctx.enter_context(nc.sbuf_tensor("whi", [P, SLOTS, BLOCK], F32R))
    wlo = ctx.enter_context(nc.sbuf_tensor("wlo", [P, SLOTS, BLOCK], F32R))
    par = sb("par", [P, NPARAM])
    con = sb("con", [P, NCONST])
    hs = sb("hs_sb", [P, KC, T1])
    xf, xs = shared("xf", [P, 2 * KC, T1], "xs", [P, 2 * KC, T1])
    y = sb("y", [P, KC, T1])
    sq = sb("sq", [P, KC, T1])
    rs = sb("rs", [P, 2, T1])
    big, hf = shared("big", [P, 48, T1], "hf", [P, 48, T1])
    mix = sb("mix", [P, KC, T1])
    cv = sb("cv", [P, 8, T1])
    work = sb("work", [P, WORK])
    bank = [ctx.enter_context(nc.psum_tensor(f"bank{i}", [P, 512], F32)) for i in range(8)]

    def pv(name, k=0, n=1, rows=P):
        lo = AT[name][0] + k
        return par[0:rows, lo:lo + n]

    def cn(name, rows=P, lo=0, cols=None):
        a, b = CAT[name]
        return con[0:rows, a + lo:a + lo + cols if cols else b]

    ones, ident = cn("ones"), cn("ident")

    loaded = sem("loaded")
    hs_loaded = sem("hs_loaded")
    mla_loaded = sem("mla_loaded")
    block_loaded = [sem(f"block_loaded{s}") for s in range(SLOTS)]
    hi_split = sem("hi_split")
    block_split = sem("block_split")
    block_used = sem("block_used")
    bank_free = sem("bank_free")
    conv_taken = sem("conv_taken")
    stored = sem("stored")

    steps = {}

    def S(phase, engine):
        key = f"{phase}_{engine}"
        if key not in steps:
            steps[key] = Steps(sem(key), table, key)
        return steps[key]

    def sp_stream(sp):
        sp.dma_start(hs[:, :, :], hs_in.rearrange("p (c t) -> p c t", t=T1)).then_inc(hs_loaded, 16)
        sp.dma_start(con[:, :], consts).then_inc(loaded, 16)
        sp.dma_start(par[:, :], params).then_inc(loaded, 16)
        for s in range(SLOTS):
            sp.dma_start(raw[:, s, :], stream[s]).then_inc(block_loaded[s], 16)
        rounds = NBLOCKS // SLOTS
        with sp.Fori(0, rounds - 1) as r:
            for s in range(SLOTS):
                sp.wait_ge(block_split, r * SLOTS + (s + 1))
                sp.dma_start(raw[:, s, :], stream[(r + 1) * SLOTS + s]).then_inc(block_loaded[s], 16)
        for n in range(rounds * SLOTS, NBLOCKS):
            sp.wait_ge(block_split, n - SLOTS + 1)
            sp.dma_start(raw[:, n % SLOTS, :], stream[n]).then_inc(block_loaded[n % SLOTS], 16)

    def split_hi(act, n, i=0):
        s = n % SLOTS
        act.wait_ge(block_loaded[s], i * (16 * 8 // SLOTS) + 16 * (n // SLOTS + 1))
        if n >= SLOTS:
            act.wait_ge(block_used, i * 8 + (n - SLOTS + 1))
        nc.scalar.activation(whi[:, s, :], raw[:, s, :], ACT.Copy).then_inc(hi_split, 1)

    def split_lo(dve, n, i=0):
        s = n % SLOTS
        dve.wait_ge(hi_split, i * 8 + (n + 1))
        nc.vector.tensor_tensor(wlo[:, s, :], raw[:, s, :], whi[:, s, :].bitcast(F32), ALU.subtract).then_inc(block_split, 1)

    def split_all(engine, split, phase, lo=0):
        b0 = FIRST_BLOCK[phase] + AHEAD + lo
        n = min(COUNT[phase] - lo, NBLOCKS - b0)
        if n >= 16:
            with engine.Fori(0, n // 8) as i:
                for j in range(8):
                    split(engine, b0 + j, i)
        for j in range(n // 8 * 8 if n >= 16 else 0, n):
            split(engine, b0 + j)

    def three(out_, slot, c, hi, lo, start, stop):
        w = slice(c * P, (c + 1) * P)
        nc.tensor.matmul(out_, whi[:, slot, w], hi, start=start, stop=False)
        nc.tensor.matmul(out_, whi[:, slot, w], lo, start=False, stop=False)
        return nc.tensor.matmul(out_, wlo[:, slot, w], hi, start=False, stop=stop)

    def pe_tiles(pe, phase, g0):
        b0, n = FIRST_BLOCK[phase], COUNT[phase]
        T = T1 if b0 < FIRST_BLOCK["ev_in"] else T2

        def tile(j, i=0):
            g = g0 + j
            pe.wait_ge(block_split, i * 8 + (b0 + j + 1))
            pe.wait_ge(bank_free, i * 8 + (g + 1))
            for k in range(KC):
                last = three(rhs_out(g, phase), (b0 + j) % SLOTS, k, xs[:, k, 0:T], xs[:, KC + k, 0:T], k == 0, k == KC - 1)
            last.then_inc(block_used, 1)

        with pe.Fori(0, n // 8) as i:
            for j in range(8):
                tile(j, i)
        for j in range(n // 8 * 8, n):
            tile(j)

    def rhs_out(g, phase):
        return bank[g % 8][:, 0:T1 if FIRST_BLOCK[phase] < FIRST_BLOCK["ev_in"] else T2]

    def pe_wide(pe, phase, g0, ready):
        b0, n = FIRST_BLOCK[phase], COUNT[phase]
        T = T1 if b0 < FIRST_BLOCK["ev_in"] else T2
        pe.wait_ge(bank_free, g0 + 8)

        def rows(k, i=None):
            at = k if i is None else i * 8 + k
            lo = n + k if i is None else i * 8 + (n + k)
            pe.wait_ge(block_split, (0 if i is None else i * 8) + (b0 + k + 1))
            ready(pe, k, i)
            for m in range(8):
                last = three(rhs_out(g0 + m, phase), (b0 + k) % SLOTS, m, hf[:, at, 0:T], hf[:, lo, 0:T], k == 0, k == n - 1)
            last.then_inc(block_used, 1)

        if n == 22:
            rows(0)
            with pe.Fori(0, 2) as i:
                for k in range(1, 9):
                    rows(k, i)
            for k in range(17, 22):
                rows(k)
        else:
            for k in range(n):
                rows(k)

    NORM = {}

    def pe_sum(pe, name, g, src, engine, T, n=KC, sums="norm"):
        pe.wait_ge(bank_free, g + 1)
        for m in range(n):
            pe.wait_ge(*S("norm", engine).at(f"{name}_{m}"))
            last = nc.tensor.matmul(bank[g % 8][:, 0:T], ones, src(m), start=(m == 0), stop=(m == n - 1))
        last.then_inc(*S("norm", "pe").mark(name))

    def act_scale(act, name, g, dst, T, count, eps, ready):
        act.wait_ge(*S("norm", "pe").at(name))
        nc.scalar.activation(dst, bank[g % 8][:, 0:T], ACT.Ln, bias=eps, scale=1.0 / count).then_inc(bank_free, 1)
        act.wait_ge(bank_free, 8 + g + 1)
        nc.scalar.activation(dst, dst, ACT.Exp, scale=-0.5).then_inc(*S("norm", "act").mark(f"{name}_scale"))

    def pre_pe(pe, name, g):
        pe_sum(pe, name, g, lambda m: sq[:, m, :], "act", T1)

    def pre_act(act, name, g, ready):
        for m in range(KC):
            ready(act, m)
            nc.scalar.activation(sq[:, m, :], hs[:, m, :], ACT.Square).then_inc(*S("norm", "act").mark(f"{name}_{m}"))
        act_scale(act, name, g, rs[:, 0, :], T1, D, eps_1, None)
        pre_act_hi(act, name)

    def pre_dve(dve, name, row):
        st, a_ = S("norm", "dve"), S("norm", "act")
        dve.wait_ge(*a_.at(f"{name}_scale"))
        for m in range(KC):
            nc.vector.scalar_tensor_tensor(y[:, m, :], hs[:, m, :], pv("norm_w", row * KC + m), rs[:, 0, :],
                                           ALU.mult, ALU.mult).then_inc(*st.mark(f"{name}_x{m}"))
        for m in range(KC):
            dve.wait_ge(*a_.at(f"{name}_hi{m}"))
            nc.vector.tensor_tensor(xs[:, KC + m, :], y[:, m, :], xs[:, m, :].bitcast(F32), ALU.subtract
                                    ).then_inc(*st.mark(f"{name}_lo{m}"))

    def pre_act_hi(act, name):
        for m in range(KC):
            act.wait_ge(*S("norm", "dve").at(f"{name}_x{m}"))
            nc.scalar.activation(xs[:, m, :], y[:, m, :], ACT.Copy).then_inc(*S("norm", "act").mark(f"{name}_hi{m}"))

    def mix_act(act, name, src, n, ready):
        ready(act)
        for k in range(n):
            nc.scalar.activation(hf[:, k, 0:src(k).shape[1]], src(k), ACT.Copy).then_inc(*S("norm", "act").mark(f"{name}_hi{k}"))

    def mix_dve(dve, name, src, n, ready):
        ready(dve)
        for k in range(n):
            T = src(k).shape[1]
            dve.wait_ge(*S("norm", "act").at(f"{name}_hi{k}"))
            nc.vector.tensor_tensor(hf[:, n + k, 0:T], src(k), hf[:, k, 0:T].bitcast(F32), ALU.subtract
                                    ).then_inc(*S("norm", "dve").mark(f"{name}_lo{k}"))

    def post_pe(pe, name, g):
        pe_sum(pe, name, g, lambda m: sq[:, m, :], "act", T1)

    def post_act(act, name, g):
        for m in range(KC):
            act.wait_ge(bank_free, 8 + g - 8 + m + 1)
            nc.scalar.activation(sq[:, m, :], y[:, m, :], ACT.Square).then_inc(*S("norm", "act").mark(f"{name}_{m}"))
        act_scale(act, name, g, rs[:, 1, :], T1, D, eps_1, None)

    def post_dve(dve, name, g, row, last_block):
        for m in range(KC):
            if m == 0:
                dve.wait_ge(block_used, last_block)
            nc.vector.tensor_copy(y[:, m, :], bank[(g - 8 + m) % 8][:, 0:T1]).then_inc(bank_free, 1)
        dve.wait_ge(*S("norm", "act").at(f"{name}_scale"))
        for m in range(KC):
            nc.vector.scalar_tensor_tensor(y[:, m, :], y[:, m, :], pv("norm_w", row * KC + m), rs[:, 1, :],
                                           ALU.mult, ALU.mult).then_inc(*S("norm", "dve").mark(f"{name}_y{m}"))
        for m in range(KC):
            dve.wait_ge(*S("norm", "dve").at(f"{name}_y{m}"))
            nc.vector.tensor_tensor(hs[:, m, :], hs[:, m, :], y[:, m, :], ALU.add
                                    ).then_inc(*S("norm", "dve").mark(f"{name}_h{m}"))

    def conv_first(act, steps_, tag, tiles, taps, bias):
        for a, (bk, slot, w) in enumerate(tiles):
            args = dict(scale=w[:, taps - 1:taps])
            if bias:
                args["bias"] = w[:, taps:taps + 1]
            nc.scalar.activation(cv[:, slot, :], bk[:, 0:T1], ACT.Identity, **args).then_inc(*steps_.mark(f"{tag}{a}"))

    def conv_rest(dve, steps_, first, tag, tiles, i, taps):
        for tap in range(1, taps):
            for a, (bk, slot, w) in enumerate(tiles):
                o = cv[:, slot, :]
                dve.wait_ge(*(first.at(f"{tag}{a}", i) if tap == 1 else steps_.at(f"{tag}_{tap - 1}{a}", i)))
                ins = nc.vector.scalar_tensor_tensor(o[:, tap:T1], bk[:, 0:T1 - tap], w[:, taps - 1 - tap:taps - tap],
                                                     o[:, tap:T1], ALU.mult, ALU.add)
                if tap == taps - 1 and a == 1:
                    ins.then_inc(bank_free, 2)
                else:
                    ins.then_inc(*steps_.mark(f"{tag}_{tap}{a}"))

    CONV0, _c = {}, 0
    for name, n in (("gdn_in", 32), ("up0", 44), ("up1", 44), ("up2", 44), ("up3", 44)):
        CONV0[name] = _c
        _c += n

    def pairs(engine, pair, steps_=None):
        with ExitStack() as loop:
            i = loop.enter_context(engine.Fori(0, 5))
            if steps_:
                loop.enter_context(steps_.repeat(5))
            for j in range(4):
                pair(j, i, 0)
        for j in range(2):
            pair(j, None, 40)

    def ffn_tiles(f, g0, j, i, base):
        t = 2 * j + base
        if f < 2:
            lo = AT[f"ffn{f}"][0]
            W = par[:, lo:lo + 176].rearrange("p (t k) -> p t k", k=4)
            w = [W[:, i * 8 + (t + a) if i is not None else t + a, :] for a in range(2)]
        else:
            w = [None] * 2
        return [(bank[(g0 + t + a) % 8], 2 * j + a, w[a]) for a in range(2)]

    def ffn_act(act, f, g0):
        st, b0, c0 = S("ffn", "act"), FIRST_BLOCK[f"up{f}"], CONV0[f"up{f}"]

        def pair(j, i, base):
            t, ii = base + 2 * j, 0 if i is None else i
            tiles = ffn_tiles(f, g0, j, i, base)
            split_hi(act, b0 + t + AHEAD, ii)
            split_hi(act, b0 + t + AHEAD + 1, ii)
            act.wait_ge(block_used, ii * 8 + (b0 + t + 2))
            act.wait_ge(conv_taken, ii * 8 + (c0 + t + 2))
            if f < 2:
                conv_first(act, st, f"f{f}_{base}_{j}", tiles, 3, True)
                act.wait_ge(bank_free, ii * 8 + (8 + g0 + t + 2))
                o = cv[:, 2 * j, :]
                nc.scalar.activation(o, o, ACT.Silu).then_inc(*st.mark(f"silu{f}_{base}_{j}"))
            else:
                nc.scalar.activation(cv[:, 2 * j, 0:T2], tiles[0][0][:, 0:T2], ACT.Silu).then_inc(*st.mark(f"silu{f}_{base}_{j}"))

        pairs(act, pair, st)

    def ffn_dve(dve, f, g0):
        st, b0 = S("ffn", "dve"), FIRST_BLOCK[f"up{f}"]

        def pair(j, i, base):
            t, ii = base + 2 * j, 0 if i is None else i
            tiles = ffn_tiles(f, g0, j, i, base)
            split_lo(dve, b0 + t + AHEAD, ii)
            split_lo(dve, b0 + t + AHEAD + 1, ii)
            if f < 2:
                conv_rest(dve, st, S("ffn", "act"), f"f{f}_{base}_{j}", tiles, i, 3)
            else:
                dve.wait_ge(*S("ffn", "act").at(f"silu{f}_{base}_{j}", i))
                nc.vector.tensor_tensor(cv[:, 2 * j + 1, 0:T2], cv[:, 2 * j, 0:T2], tiles[1][0][:, 0:T2], ALU.mult).then_inc(bank_free, 2)

        pairs(dve, pair, st)

    def ffn_pool(pool, f, g0):
        st, T = S("ffn", "pool"), T1 if f < 2 else T2

        def pair(j, i, base):
            ii = 0 if i is None else i
            k = base // 2 + j
            h = cv[:, 2 * j + 1, 0:T]
            hi = hf[:, k if i is None else i * 4 + k, 0:T]
            lo = hf[:, FC + k if i is None else i * 4 + (FC + k), 0:T]
            if f < 2:
                pool.wait_ge(*S("ffn", "act").at(f"silu{f}_{base}_{j}", i))
                nc.gpsimd.tensor_tensor(h, cv[:, 2 * j, 0:T], h, ALU.mult).then_inc(*st.mark(f"h{f}_{base}_{j}"))
                pool.wait_ge(*st.at(f"h{f}_{base}_{j}", i))
            else:
                pool.wait_ge(bank_free, ii * 8 + (8 + g0 + base + 2 * j + 2))
            nc.gpsimd.tensor_copy(hi, h).then_inc(*st.mark(f"hi{f}_{base}_{j}"))
            pool.wait_ge(*st.at(f"hi{f}_{base}_{j}", i))
            nc.gpsimd.tensor_tensor(lo, h, hi.bitcast(F32), ALU.subtract).then_inc(conv_taken, 2)

        pairs(pool, pair, st)

    def ffn_ready(f):
        def ready(pe, k, i):
            c = 8 + CONV0[f"up{f}"] + 2 * (k + 1)
            pe.wait_ge(conv_taken, c if i is None else i * 16 + c)
        return ready

    G, _g = {}, 0
    for name, n in (("pre0", 1), ("gdn_g", 2), ("gdn_in", 48), ("gdn_out", 8), ("post0", 1), ("pre1", 1), ("up0", 44), ("down0", 8),
                    ("post1", 1), ("pre2", 1), ("ml_g", 2), ("ml_in", 24), ("ml_out", 8), ("post2", 1), ("pre3", 1), ("up1", 44),
                    ("down1", 8), ("post3", 1),
                    ("ev_in", 18), ("ev_out", 8), ("lm0", 1), ("lv0", 1), ("up2", 44), ("down2", 8), ("lm1", 1), ("lv1", 1),
                    ("od_g", 1), ("od_in", 17), ("od_out", 8), ("lm2", 1), ("lv2", 1), ("up3", 44), ("down3", 8), ("lm3", 1), ("lv3", 1)):
        G[name] = _g
        _g += n

    def used_after(phase):
        return FIRST_BLOCK[phase] + COUNT[phase]

    at = lambda ap, c: ap[:, CHUNKS[c][0]:CHUNKS[c][0] + CHUNKS[c][1]]
    own = lambda ap, c: ap[0:CHUNKS[c][1]]
    fulls = lambda ap: ap.rearrange("p (c t) -> p c t", t=P)
    fc = lambda ap: fulls(ap[:, HEAD_T:T1])
    wk = lambda lo, n: work[:, lo:lo + n]
    VH = range(4)
    TT, UU, X1, EG = ([xf[:, 4 * s + a, :] for a in VH] for s in range(4))
    AT_, att = ([y[:, 4 * s + a, :] for a in VH] for s in range(2))
    selG, selb = TT, X1
    U1, U2 = TT, X1
    qd = [sq[:, a, :] for a in VH]
    qn, kn = ([sq[:, 4 + 2 * s + k, :] for k in range(2)] for s in range(2))
    kk, kq, qss, kss = ([cv[:, 2 * s + k, :] for k in range(2)] for s in range(4))
    vtok = [mix[:, 0:6, :].rearrange("p a b -> p (a b)")[:, a * NCH * P:(a + 1) * NCH * P] for a in VH]
    ktok = [wk(k * NCH * P, NCH * P) for k in range(2)]
    vnew, vdec, state = ([wk(768 + 512 * s + a * P, P) for a in VH] for s in range(3))
    vst = [wk(2304 + a * T1, T1) for a in VH]
    tok = lambda n: wk(3392 + n * NCH * GV, NCH * GV).rearrange("p (c h) -> p c h", c=NCH)
    g_tok, b_tok, G_tok, nbe_tok, el_tok = (tok(n) for n in range(5))
    b_row, u_row, t_row, G_row, ea = (wk(3632 + n * T1, T1)[0:GV] for n in range(5))
    short = lambda n: wk(4992 + n * 4 * HEAD_T, 4 * HEAD_T)[0:HEAD_T].rearrange("p (a t) -> p a t", a=4)
    sT, sU, sX, sU1, sU2 = (short(n) for n in range(5))
    at_chunk = lambda ap, c: ap[:, c * P:(c + 1) * P]
    VBANK = ((6, 7), (4, 5), (0, 1), (2, 3))
    SB, SB2 = (bank[b][0:HEAD_T, 2 * P:2 * P + 4 * HEAD_T].rearrange("p (a t) -> p a t", a=4) for b in VBANK[3])
    odd = lambda ap, size: ap.rearrange("p (b two s) -> p b two s", two=2, s=size)[:, :, 1, :]
    head = lambda ap, h: ap.rearrange("p c (h o) -> p c h o", o=1)[:, :, h, :]
    EYE = cn("ident").rearrange("p (n o) -> p n o", o=1)

    U1c = lambda a, c: at_chunk(U1[a], c - 1) if c else sU1[:, a, :]
    U2c = lambda a, c: at_chunk(U2[a], c - 1) if c else sU2[:, a, :]

    over_c = lambda ap, n: ap.unsqueeze(1).to_broadcast([ap.shape[0], n, ap.shape[1]])

    def gates_pe(pe, name, g, cols, base, width, T, rhs):
        w = pv(base, 0, KC * width).rearrange("p (k n) -> p k n", k=KC)
        for n, (lo, m) in enumerate(cols):
            pe.wait_ge(bank_free, g + n + 1)
            for k in range(KC):
                last = nc.tensor.matmul(bank[(g + n) % 8][0:m, 0:T], w[:, k, lo:lo + m], rhs(k), start=(k == 0), stop=(k == KC - 1))
            last.then_inc(*S("gates", "pe").mark(f"{name}{n}"))

    def gdn_gates_act(act):
        g = G["gdn_g"]
        act.wait_ge(*S("gates", "pe").at("gdn0"))
        nc.scalar.activation(b_row, bank[g % 8][0:GV, 0:T1], ACT.Sigmoid).then_inc(bank_free, 1)
        act.wait_ge(*S("gates", "pe").at("gdn1"))
        nc.scalar.activation(u_row, bank[(g + 1) % 8][0:GV, 0:T1], ACT.Identity, bias=pv("gdn_dt", rows=GV)).then_inc(bank_free, 1)

    def gdn_in_tiles(j, i):
        lo = AT["gdn_conv"][0]
        W = par[:, lo:lo + 128].rearrange("p (t k) -> p t k", k=4)
        return [(bank[(G["gdn_in"] + 2 * j + a) % 8], 2 * j + a, W[:, i * 8 + (2 * j + a), :]) for a in range(2)]

    def gdn_in_dve(dve):
        st, g0, b0 = S("gin", "dve"), G["gdn_in"], FIRST_BLOCK["gdn_in"]
        dve.wait_ge(bank_free, 8 + g0)
        with dve.Fori(0, 4) as i, st.repeat(4):
            for j in range(4):
                split_lo(dve, b0 + 2 * j + AHEAD, i)
                split_lo(dve, b0 + 2 * j + AHEAD + 1, i)
                conv_rest(dve, st, S("gin", "act"), f"c{j}", gdn_in_tiles(j, i), i, 4)
        split_all(dve, split_lo, "gdn_in", 32)

    def gdn_in_act(act):
        st, g0, b0, c0 = S("gin", "act"), G["gdn_in"], FIRST_BLOCK["gdn_in"], CONV0["gdn_in"]
        with act.Fori(0, 4) as i, st.repeat(4):
            for j in range(4):
                split_hi(act, b0 + 2 * j + AHEAD, i)
                split_hi(act, b0 + 2 * j + AHEAD + 1, i)
                act.wait_ge(block_used, i * 8 + (b0 + 2 * j + 2))
                act.wait_ge(conv_taken, i * 8 + (c0 + 2 * j + 2))
                conv_first(act, st, f"c{j}", gdn_in_tiles(j, i), 4, False)
                act.wait_ge(bank_free, i * 8 + (8 + g0 + 2 * j + 2))
                for a in range(2):
                    nc.scalar.activation(big[:, i * 8 + (2 * j + a), :], cv[:, 2 * j + a, :], ACT.Silu).then_inc(conv_taken, 1)
        with act.Fori(0, 2) as i:
            for j in range(8):
                split_hi(act, b0 + 32 + j + AHEAD, i)
                act.wait_ge(block_used, i * 8 + (b0 + 32 + j + 1))
                nc.scalar.activation(big[:, i * 8 + (32 + j), :], bank[(g0 + 32 + j) % 8][:, 0:T1], ACT.Silu).then_inc(bank_free, 1)

    def gdn_pe(pe):
        m, v, a_ = S("gdn", "pe"), S("gdn", "dve"), S("gdn", "act")
        pl = S("gdn", "pool")
        mm = nc.tensor.matmul
        pe.wait_ge(bank_free, 8 + G["gdn_out"])
        pe.wait_ge(*v.at("g_row"))
        rows_of = lambda c: slice(CHUNKS[c][0], CHUNKS[c][0] + P)
        for c in range(NCH):
            nc.tensor.transpose(bank[0][:, c * GV:(c + 1) * GV], t_row[:, rows_of(c)], ident[0:GV, 0:GV])
        for c in range(NCH):
            last = nc.tensor.transpose(bank[1][:, c * GV:(c + 1) * GV], b_row[:, rows_of(c)], ident[0:GV, 0:GV])
        last.then_inc(*m.mark("to_tok"))
        pe.wait_ge(*v.at("g_tok"))
        upto = cn("upto")
        for c, (lo, n) in enumerate(CHUNKS):
            g_c = g_tok[0:n, c, :]
            mm(bank[2][0:GV, lo:lo + n], g_c, upto[0:n, 0:n], start=True, stop=True)
            mm(bank[3][:, c * GV:(c + 1) * GV], upto[0:n, :], g_c, start=True, stop=True)
            last = mm(bank[4][:, c * GV:(c + 1) * GV], ones[0:n, :], g_c, start=True, stop=True)
        last.then_inc(*m.mark("sums"))

        pe.wait_ge(*v.at("el_tok"))
        with pe.Fori(0, GK // 2) as i, m.repeat(GK // 2):
            for k in range(2):
                pe.wait_ge(*pl.at(f"squares{k}", i))
                mm(bank[2 * k][:, 0:T1], ones, qss[k], start=True, stop=True)
                mm(bank[2 * k + 1][:, 0:T1], ones, kss[k], start=True, stop=True).then_inc(*m.mark(f"norms{k}"))
            for a in VH:
                pe.wait_ge(*pl.at(f"vst{a}", i))
                for c in range(NCH):
                    last = nc.tensor.transpose(own(at_chunk(bank[4 + a], c), c), at(vst[a], c), ident)
                last.then_inc(*m.mark(f"vtok{a}"))
            for k in range(2):
                pe.wait_ge(*v.at(f"kn{k}", i))
                for dst, other in ((2 * k, kn[k]), (2 * k + 1, qn[k])):
                    for c in range(NCH):
                        last = mm(at(bank[dst], c), kn[k][:, rows_of(c)], at(other, c), start=True, stop=True)
                last.then_inc(*m.mark(f"kk{k}"))
                pe.wait_ge(*a_.at(f"vtok{k}", i))
                for c in range(NCH):
                    last = nc.tensor.transpose(own(at_chunk(bank[4 + k], c), c), at(kn[k], c), ident)
                last.then_inc(*m.mark(f"ktok{k}"))
            for a in VH:
                pe.wait_ge(*v.at(f"sel{a}", i))
                pe.wait_ge(*a_.at(("vtok3", "ktok1", "kq0", "kq1")[a], i))
                mm(bank[VBANK[a][0]][:, 0:T1], ones[0:16, :], selG[a][0:16, :], start=True, stop=True)
                mm(bank[VBANK[a][1]][:, 0:T1], ones[0:16, :], selb[a][0:16, :], start=True, stop=True).then_inc(*m.mark(f"rows{a}"))
            for l in range(LAST + 1):
                with_short = lambda a, last: a == 3 and l <= last
                for a in VH if l else ():
                    pe.wait_ge(*a_.at(f"sT_{l - 1}" if with_short(a, SHORT_LAST) else f"T{a}_{l - 1}", i))
                    for c in range(2):
                        last = mm(at_chunk(bank[VBANK[a][0]], c), at(AT_[a], c + 1), at_chunk(TT[a], c), start=True, stop=True)
                    for b in VH if with_short(a, SHORT_LAST) else ():
                        last = mm(SB[:, b, :], AT_[b][0:HEAD_T, 0:HEAD_T], sT[:, b, :], start=True, stop=True)
                    last.then_inc(*m.mark(f"X{a}_{l}"))
                for a in VH if l else ():
                    pe.wait_ge(*v.at(f"sX_{l}" if with_short(a, SHORT_LAST) else f"X{a}_{l}", i))
                    for c in range(2):
                        last = mm(at_chunk(bank[VBANK[a][1]], c), at_chunk(X1[a], c), at_chunk(UU[a], c), start=True, stop=True)
                    for b in VH if with_short(a, SHORT_LAST) else ():
                        last = mm(SB2[:, b, :], sX[:, b, :], sU[:, b, :], start=True, stop=True)
                    last.then_inc(*m.mark(f"Y{a}_{l}"))
                for a in VH if l < LAST else ():
                    if l == 0:
                        pe.wait_ge(*v.at(f"U{a}_0", i))
                        if a == 3:
                            pe.wait_ge(*pl.at("sU_0", i))
                        pe.wait_ge(*a_.at(f"EG{a}", i))
                    else:
                        pe.wait_ge(*v.at(f"sU_{l}" if with_short(a, SHORT_LAST) else f"U{a}_{l}", i))
                    for c in range(2):
                        last = nc.tensor.transpose(at_chunk(bank[VBANK[a][0]], c), at_chunk(UU[a], c), ident)
                    for b in VH if with_short(a, SHORT_LAST - 1) else ():
                        last = nc.tensor.transpose(SB[:, b, :], sU[:, b, :], ident[0:HEAD_T, 0:HEAD_T])
                    last.then_inc(*m.mark(f"T{a}_{l}"))
            for a in VH:
                pe.wait_ge(*v.at(f"U1{a}", i))
                for c in range(NCH):
                    last = mm(at(bank[VBANK[a][1]], c), own(at_chunk(ktok[a // 2], c), c), U2c(a, c), start=True, stop=True)
                last.then_inc(*m.mark(f"w{a}"))
            for c in range(NCH):
                for a in VH:
                    bv, bo = VBANK[a]
                    if c > 0:
                        pe.wait_ge(*v.at(f"S{a}_{c - 1}", i))
                        mm(at(bank[bo], c), state[a], at(qd[a], c), start=True, stop=False)
                    last = mm(own(bank[bv], c)[:, 0:P], U1c(a, c), own(at_chunk(vtok[a], c), c), start=True, stop=(c == 0))
                    if c > 0:
                        last = mm(own(bank[bv], c)[:, 0:P], at(AT_[a], c), state[a], start=False, stop=True)
                    last.then_inc(*m.mark(f"v{a}_{c}"))
                for a in VH:
                    bv, bo = VBANK[a]
                    pe.wait_ge(*a_.at(f"v{a}_{c}", i))
                    if c == 0:
                        pe.wait_ge(*pl.at(f"qd{a}", i))
                    mm(at(bank[bo], c), own(vnew[a], c), own(at(att[a], c), c), start=(c == 0), stop=True).then_inc(*m.mark(f"o{a}_{c}"))
                    if c < NCH - 1:
                        pe.wait_ge(*pl.at(f"d{a}_{c}", i))
                        mm(bank[bv][:, P:2 * P], own(at_chunk(ktok[a // 2], c), c), own(vdec[a], c), start=True, stop=True
                           ).then_inc(*m.mark(f"s{a}_{c}"))
            for a in VH:
                pe.wait_ge(*a_.at(f"osq{a}", i))
                mm(bank[VBANK[a][0]][:, 0:T1], ones, UU[a], start=True, stop=True).then_inc(*m.mark(f"on{a}"))
            pe.wait_ge(*v.at("o3", i))

    def gdn_act(act):
        m, v, a_, pl = S("gdn", "pe"), S("gdn", "dve"), S("gdn", "act"), S("gdn", "pool")
        A = nc.scalar.activation
        act.wait_ge(bank_free, 8 + G["gdn_g"] + 2)
        A(t_row, u_row, ACT.Abs).then_inc(*a_.mark("abs"))
        act.wait_ge(*a_.at("abs"))
        A(t_row, t_row, ACT.Exp, scale=-1.0).then_inc(*a_.mark("e"))
        A(ea[:, 0:1], pv("gdn_a_log", rows=GV), ACT.Exp).then_inc(*a_.mark("ea"))
        act.wait_ge(*a_.at("e"))
        A(t_row, t_row, ACT.Ln, bias=1.0).then_inc(*a_.mark("softplus"))
        act.wait_ge(*m.at("to_tok"))
        A(g_tok.rearrange("p c h -> p (c h)"), bank[0][:, 0:NCH * GV], ACT.Copy).then_inc(*a_.mark("g_tok"))
        A(b_tok.rearrange("p c h -> p (c h)"), bank[1][:, 0:NCH * GV], ACT.Copy).then_inc(*a_.mark("b_tok"))
        act.wait_ge(*v.at("G_tok"))
        act.wait_ge(*v.at("el_tok"))
        flat = lambda ap: ap.rearrange("p c h -> p (c h)")
        A(flat(nbe_tok), flat(G_tok), ACT.Exp).then_inc(*a_.mark("eG"))
        A(flat(el_tok), flat(el_tok), ACT.Exp).then_inc(*a_.mark("el"))
        with act.Fori(0, GK // 2) as i, a_.repeat(GK // 2):
            for k in range(2):
                act.wait_ge(*m.at(f"norms{k}", i))
                A(qss[k], bank[2 * k][:, 0:T1], ACT.Ln, scale=float(GD), bias=eps_q).then_inc(*a_.mark(f"lq{k}"))
                A(kss[k], bank[2 * k + 1][:, 0:T1], ACT.Ln, bias=eps_1).then_inc(*a_.mark(f"lk{k}"))
                act.wait_ge(*a_.at(f"lq{k}", i))
                A(qss[k], qss[k], ACT.Exp, scale=-0.5).then_inc(*a_.mark(f"rq{k}"))
                act.wait_ge(*a_.at(f"lk{k}", i))
                A(kss[k], kss[k], ACT.Exp, scale=-0.5).then_inc(*a_.mark(f"rk{k}"))
            for a in VH:
                act.wait_ge(*m.at(f"vtok{a}", i))
                A(vtok[a][0:HEAD_T, 0:P], bank[4 + a][0:HEAD_T, 0:P], ACT.Copy).then_inc(*a_.mark(f"vtok_s{a}"))
                A(vtok[a][:, P:NCH * P], bank[4 + a][:, P:NCH * P], ACT.Copy).then_inc(*a_.mark(f"vtok{a}"))
            for k in range(2):
                act.wait_ge(*m.at(f"kk{k}", i))
                A(kk[k], bank[2 * k][:, 0:T1], ACT.Copy).then_inc(*a_.mark(f"kk{k}"))
                A(kq[k], bank[2 * k + 1][:, 0:T1], ACT.Copy).then_inc(*a_.mark(f"kq{k}"))
                act.wait_ge(*m.at(f"ktok{k}", i))
                A(ktok[k][0:HEAD_T, 0:P], bank[4 + k][0:HEAD_T, 0:P], ACT.Copy).then_inc(*a_.mark(f"ktok_s{k}"))
                A(ktok[k][:, P:NCH * P], bank[4 + k][:, P:NCH * P], ACT.Copy).then_inc(*a_.mark(f"ktok{k}"))
            for a in VH:
                act.wait_ge(*v.at(f"Z{a}", i))
                A(UU[a], UU[a], ACT.Exp).then_inc(*a_.mark(f"D{a}"))
                A(EG[a], bank[VBANK[a][0]][:, 0:T1], ACT.Exp).then_inc(*a_.mark(f"EG{a}"))
            for l in range(LAST):
                for a in VH:
                    act.wait_ge(*m.at(f"T{a}_{l}", i))
                    A(TT[a][:, 0:2 * P], bank[VBANK[a][0]][:, 0:2 * P], ACT.Copy).then_inc(*a_.mark(f"T{a}_{l}"))
                if l < SHORT_LAST:
                    A(sT, SB, ACT.Copy).then_inc(*a_.mark(f"sT_{l}"))
            for a in VH:
                act.wait_ge(*m.at(f"w{a}", i))
                A(AT_[a], bank[VBANK[a][1]][:, 0:T1], ACT.Copy).then_inc(*a_.mark(f"w{a}"))
            for c in range(NCH):
                for a in VH:
                    act.wait_ge(*m.at(f"v{a}_{c}", i))
                    if c > 0:
                        act.wait_ge(*pl.at(f"d{a}_{c - 1}", i))
                    A(own(vnew[a], c), own(bank[VBANK[a][0]], c)[:, 0:P], ACT.Copy).then_inc(*a_.mark(f"v{a}_{c}"))
            for a in VH:
                act.wait_ge(*m.at(f"o{a}_{NCH - 1}", i))
                A(UU[a], bank[VBANK[a][1]][:, 0:T1], ACT.Square).then_inc(*a_.mark(f"osq{a}"))
            for a in VH:
                act.wait_ge(*m.at(f"on{a}", i))
                A(UU[a], bank[VBANK[a][0]][:, 0:T1], ACT.Ln, scale=1.0 / GD, bias=eps_1).then_inc(*a_.mark(f"ol{a}"))
                act.wait_ge(*a_.at(f"ol{a}", i))
                A(UU[a], UU[a], ACT.Exp, scale=-0.5).then_inc(*a_.mark(f"or{a}"))

    def gdn_dve(dve):
        m, v, a_, pl = S("gdn", "pe"), S("gdn", "dve"), S("gdn", "act"), S("gdn", "pool")
        tt, ts, stt = nc.vector.tensor_tensor, nc.vector.tensor_scalar, nc.vector.scalar_tensor_tensor
        flat = lambda ap: ap.rearrange("p c h -> p (c h)")
        over_i = lambda ap, n: ap.unsqueeze(2).to_broadcast([ap.shape[0], ap.shape[1], n])
        dve.wait_ge(*a_.at("softplus"))
        stt(t_row, u_row, 0.0, t_row, ALU.max, ALU.add).then_inc(*v.mark("sp"))
        dve.wait_ge(*v.at("sp"))
        ts(t_row, t_row, ea[:, 0:1], -1.0, ALU.mult, ALU.mult).then_inc(*v.mark("g_row"))
        dve.wait_ge(*a_.at("b_tok"))
        nc.vector.tensor_copy(ea[:, 1:2], ea[:, 0:1]).then_inc(*v.mark("g_tok"))
        dve.wait_ge(*m.at("sums"))
        nc.vector.tensor_copy(G_row, bank[2][0:16, 0:T1]).then_inc(*v.mark("G_row"))
        nc.vector.tensor_copy(flat(G_tok), bank[3][:, 0:NCH * GV]).then_inc(*v.mark("G_tok"))
        dve.wait_ge(*v.at("G_tok"))
        tt(flat(el_tok), bank[4][:, 0:NCH * GV], flat(G_tok), ALU.subtract).then_inc(*v.mark("el_tok"))
        dve.wait_ge(*a_.at("eG"))
        stt(flat(nbe_tok), flat(nbe_tok), -1.0, flat(b_tok), ALU.mult, ALU.mult).then_inc(*v.mark("nbe"))
        with dve.Fori(0, GK // 2) as i, v.repeat(GK // 2):
            dve.wait_ge(bank_free, 8 + G["gdn_out"])
            for a in VH:
                ts(selG[a][0:16], G_row, EYE[0:16, 4 * i + a, :], None, ALU.mult).then_inc(*v.mark(f"selG{a}"))
                ts(selb[a][0:16], b_row, EYE[0:16, 4 * i + a, :], None, ALU.mult).then_inc(*v.mark(f"sel{a}"))
            for k in range(2):
                dve.wait_ge(*a_.at(f"rk{k}", i))
                tt(qn[k], big[:, 2 * i + k, :], qss[k], ALU.mult).then_inc(*v.mark(f"qn{k}"))
                tt(kn[k], big[:, 2 * i + (8 + k), :], kss[k], ALU.mult).then_inc(*v.mark(f"kn{k}"))
            for a in VH:
                dve.wait_ge(*m.at(f"rows{a}", i))
                for c in range(NCH):
                    w = slice(CHUNKS[c][0], CHUNKS[c][0] + CHUNKS[c][1])
                    stt(UU[a][:, w], bank[VBANK[a][0]][:, w], head(G_tok, 4 * i + a)[:, c, :], cn("neg_chunk")[:, 0:CHUNKS[c][1]],
                        ALU.subtract, ALU.add).then_inc(*v.mark(f"Z{a}" if c == NCH - 1 else f"Z{a}_{c}"))
            for a in VH:
                dve.wait_ge(*a_.at(f"D{a}", i))
                tt(AT_[a], UU[a], kk[a // 2], ALU.mult).then_inc(*v.mark(f"a{a}"))
                dve.wait_ge(*v.at(f"a{a}", i))
                tt(AT_[a], AT_[a], bank[VBANK[a][1]][:, 0:T1], ALU.mult).then_inc(*v.mark(f"A{a}"))
                dve.wait_ge(*v.at(f"A{a}", i))
                tt(fulls(X1[a][:, 0:2 * P]), fc(AT_[a]), over_c(cn("level0_t"), 2), ALU.mult).then_inc(*v.mark(f"u{a}"))
                dve.wait_ge(*v.at(f"u{a}", i))
                dve.wait_ge(*pl.at(f"att{a}", i))
                tt(fulls(UU[a][:, 0:2 * P]), over_c(ident, 2), fulls(X1[a][:, 0:2 * P]), ALU.subtract).then_inc(*v.mark(f"U{a}_0"))
            for l in range(1, LAST + 1):
                level = cn("levels", P, l * P, P)
                for a in VH:
                    dve.wait_ge(*m.at(f"X{a}_{l}", i))
                    tt(fulls(X1[a][:, 0:2 * P]), fulls(bank[VBANK[a][0]][:, 0:2 * P]), over_c(level, 2), ALU.mult).then_inc(*v.mark(f"X{a}_{l}"))
                if l <= SHORT_LAST:
                    tt(sX, SB, over_c(level[0:HEAD_T, 0:HEAD_T], 4), ALU.mult).then_inc(*v.mark(f"sX_{l}"))
                for a in VH:
                    dve.wait_ge(*m.at(f"Y{a}_{l}", i))
                    Uo, Yo = odd(UU[a][:, 0:2 * P], LEVELS[l]), odd(bank[VBANK[a][1]][:, 0:2 * P], LEVELS[l])
                    tt(Uo, Uo, Yo, ALU.subtract).then_inc(*v.mark(f"U{a}_{l}"))
                if l <= SHORT_LAST:
                    tt(sU, sU, SB2, ALU.subtract).then_inc(*v.mark(f"sU_{l}"))
            dve.wait_ge(*v.at(f"U3_{LAST}", i))
            beta = lambda ap: ap.rearrange("p c (h o) -> p c h o", o=4)[0:HEAD_T, 0, i, :]
            tt(sU2, sU, over_i(beta(nbe_tok), HEAD_T), ALU.mult).then_inc(*v.mark("sU2"))
            tt(sU1, sU, over_i(beta(b_tok), HEAD_T), ALU.mult).then_inc(*v.mark("sU1"))
            for a in VH:
                U_ = fulls(UU[a][:, 0:2 * P])
                tt(fulls(U2[a][:, 0:2 * P]), U_, over_i(head(nbe_tok, 4 * i + a)[:, 1:3, 0], P), ALU.mult).then_inc(*v.mark(f"U2{a}"))
                tt(fulls(U1[a][:, 0:2 * P]), U_, over_i(head(b_tok, 4 * i + a)[:, 1:3, 0], P), ALU.mult).then_inc(*v.mark(f"U1{a}"))
            for c in range(NCH - 1):
                for a in VH:
                    dve.wait_ge(*m.at(f"s{a}_{c}", i))
                    s_bank = bank[VBANK[a][0]][:, P:2 * P]
                    if c == 0:
                        nc.vector.tensor_copy(state[a], s_bank).then_inc(*v.mark(f"S{a}_0"))
                    else:
                        dve.wait_ge(*v.at(f"S{a}_{c - 1}", i))
                        stt(state[a], state[a], EG[a][:, CHUNKS[c + 1][0] - 1:CHUNKS[c + 1][0]], s_bank, ALU.mult, ALU.add
                            ).then_inc(*v.mark(f"S{a}_{c}"))
            for a in VH:
                h = 4 * i + (32 + a)
                dve.wait_ge(*a_.at(f"or{a}", i))
                tt(AT_[a], bank[VBANK[a][1]][:, 0:T1], UU[a], ALU.mult).then_inc(*v.mark(f"on{a}"))
                dve.wait_ge(*v.at(f"on{a}", i))
                stt(big[:, h, :], AT_[a], pv("gdn_norm"), big[:, h, :], ALU.mult, ALU.mult).then_inc(*v.mark(f"o{a}"))

    def gdn_pool(pool):
        m, v, a_, pl = S("gdn", "pe"), S("gdn", "dve"), S("gdn", "act"), S("gdn", "pool")
        tt = nc.gpsimd.tensor_tensor
        with pool.Fori(0, GK // 2) as i, pl.repeat(GK // 2):
            pool.wait_ge(bank_free, 8 + G["gdn_out"])
            for k in range(2):
                tt(qss[k], big[:, 2 * i + k, :], big[:, 2 * i + k, :], ALU.mult).then_inc(*pl.mark(f"sq_q{k}"))
                tt(kss[k], big[:, 2 * i + (8 + k), :], big[:, 2 * i + (8 + k), :], ALU.mult).then_inc(*pl.mark(f"squares{k}"))
            for a in VH:
                nc.gpsimd.tensor_copy(vst[a], big[:, 4 * i + (16 + a), :]).then_inc(*pl.mark(f"vst{a}"))
            for a in VH:
                pool.wait_ge(*a_.at(f"D{a}", i))
                tt(att[a], UU[a], kq[a // 2], ALU.mult).then_inc(*pl.mark(f"att{a}"))
            pool.wait_ge(*v.at("A3", i))
            tt(sU, y[0:HEAD_T, 0:4, 0:HEAD_T], over_c(cn("level0_t")[0:HEAD_T, 0:HEAD_T], 4), ALU.mult).then_inc(*pl.mark("su"))
            pool.wait_ge(*pl.at("su", i))
            tt(sU, over_c(ident[0:HEAD_T, 0:HEAD_T], 4), sU, ALU.subtract).then_inc(*pl.mark("sU_0"))
            for a in VH:
                pool.wait_ge(*a_.at(f"EG{a}", i))
                tt(qd[a], qn[a // 2], EG[a], ALU.mult).then_inc(*pl.mark(f"qd{a}"))
            for c in range(NCH - 1):
                for a in VH:
                    pool.wait_ge(*a_.at(f"v{a}_{c}", i))
                    n = CHUNKS[c][1]
                    tt(vdec[a][0:n], vnew[a][0:n], head(el_tok, 4 * i + a)[0:n, c, :].to_broadcast([n, P]), ALU.mult
                       ).then_inc(*pl.mark(f"d{a}_{c}"))

    JB = ((0, 128), (128, 128), (256, 16))
    OFF = (0, T1, T1 + 144)
    r4 = lambda n: work[0:MH, n * T1:(n + 1) * T1]
    f_row, i_row, s_row, t4_row, bsum_row, cmax_row, m_row, c_row = (r4(n) for n in range(8))
    c_tok = work[:, 2180:2192]
    zbuf, pbuf = work[:, 2200:2632], work[:, 2640:3072]
    em, rden = work[:, 3080:3352], work[:, 3360:3632]
    vt = work[:, 3640:4408].rearrange("p (b d) -> p b d", b=3)
    hh = [work[:, 4420 + s * T1:4420 + (s + 1) * T1] for s in range(4)]
    cB = lambda b: work[0:JB[b][1], 2180 + 4 * b:2184 + 4 * b]

    def ml_gates_act(act):
        g, s = G["ml_g"], S("ml", "act")
        A = nc.scalar.activation
        act.wait_ge(*S("norm", "dve").at("post1_h7"))
        act.wait_ge(*S("gates", "pe").at("ml0"))
        A(i_row, bank[g % 8][0:MH, 0:T1], ACT.Identity, bias=pv("ml_ib", rows=MH)).then_inc(bank_free, 1)
        act.wait_ge(*S("gates", "pe").at("ml1"))
        A(f_row, bank[(g + 1) % 8][0:MH, 0:T1], ACT.Identity, bias=pv("ml_fb", rows=MH)).then_inc(bank_free, 1)
        act.wait_ge(bank_free, 8 + g + 2)
        A(i_row, i_row, ACT.Tanh, scale=1.0 / GATE_CAP).then_inc(*s.mark("i"))
        A(f_row, f_row, ACT.Tanh, scale=1.0 / GATE_CAP).then_inc(*s.mark("tf"))
        act.wait_ge(*s.at("tf"))
        A(s_row, f_row, ACT.Abs).then_inc(*s.mark("af"))
        act.wait_ge(*s.at("af"))
        A(s_row, s_row, ACT.Exp, scale=-GATE_CAP).then_inc(*s.mark("ef"))
        act.wait_ge(*s.at("ef"))
        A(s_row, s_row, ACT.Ln, bias=1.0).then_inc(*s.mark("lf"))

    def scan(dve, s, tag, src, other, op, T):
        step, n = 1, 0
        while step < T:
            if n:
                dve.wait_ge(*s.at(f"{tag}{n - 1}"))
            nc.vector.tensor_tensor(other[..., step:T], src[..., step:T], src[..., 0:T - step], op).then_inc(*s.mark(f"{tag}{n}a"))
            nc.vector.tensor_copy(other[..., 0:step], src[..., 0:step]).then_inc(*s.mark(f"{tag}{n}"))
            src, other = other, src
            step, n = step * 2, n + 1
        dve.wait_ge(*s.at(f"{tag}{n - 1}"))
        return src

    def ml_gates_dve(dve):
        s, a_ = S("ml", "dve"), S("ml", "act")
        ts, stt, tt = nc.vector.tensor_scalar, nc.vector.scalar_tensor_tensor, nc.vector.tensor_tensor
        dve.wait_ge(*a_.at("lf"))
        ts(f_row, f_row, GATE_CAP, 0.0, ALU.mult, ALU.min).then_inc(*s.mark("minf"))
        dve.wait_ge(*s.at("minf"))
        tt(f_row, f_row, s_row, ALU.subtract).then_inc(*s.mark("logf"))
        dve.wait_ge(*s.at("logf"))
        b = scan(dve, s, "b", f_row, t4_row, ALU.add, T1)
        stt(c_row, i_row, GATE_CAP, b, ALU.mult, ALU.subtract).then_inc(*s.mark("c"))
        nc.vector.tensor_copy(bsum_row, b).then_inc(*s.mark("bsum"))
        dve.wait_ge(*s.at("bsum"))
        nc.vector.tensor_copy(f_row, c_row).then_inc(*s.mark("c2"))
        dve.wait_ge(*s.at("c2"))
        mx = scan(dve, s, "m", f_row, t4_row, ALU.max, T1)
        nc.vector.tensor_copy(cmax_row, mx).then_inc(*s.mark("cmax"))
        tt(m_row, mx, bsum_row, ALU.add).then_inc(*s.mark("m"))

    def ml_in_act(act):
        g0, b0 = G["ml_in"], FIRST_BLOCK["ml_in"]
        for turn in range(2):
            with act.Fori(0, (2, 1)[turn]) as i:
                for j in range(8):
                    split_hi(act, b0 + 16 * turn + j + AHEAD, i)
                    act.wait_ge(block_used, i * 8 + (b0 + 16 * turn + j + 1))
                    nc.scalar.activation(big[:, i * 8 + (16 * turn + j), :], bank[(g0 + j) % 8][:, 0:T1],
                                         (ACT.Copy, ACT.Sigmoid)[turn]).then_inc(bank_free, 1)

    def ml_pe(pe):
        m, v, a_, pl = S("ml", "pe"), S("ml", "dve"), S("ml", "act"), S("ml", "pool")
        mm = nc.tensor.matmul
        pe.wait_ge(bank_free, 8 + G["ml_out"])
        pe.wait_ge(*v.at("m"))
        for b, (lo, n) in enumerate(JB):
            last = nc.tensor.transpose(bank[0][0:n, 4 * b:4 * b + 4], c_row[:, lo:lo + n], ident[0:MH, 0:MH])
        last.then_inc(*m.mark("ctok"))
        for h in range(MH):
            if h:
                pe.wait_ge(*v.at(f"P{h - 1}"))
                pe.wait_ge(*a_.at(f"em{h - 1}"))
            else:
                pe.wait_ge(*v.at("ctok"))
            sel = ident[0:MH, h:h + 1].to_broadcast([MH, P])
            mm(bank[0][:, 0:T1], sel, cmax_row, start=True, stop=True)
            mm(bank[1][:, 0:T1], sel, m_row, start=True, stop=True).then_inc(*m.mark(f"rows{h}"))
            for b, (lo, n) in enumerate(JB):
                last = mm(bank[2][0:n, OFF[b]:OFF[b] + T1 - lo], big[:, 4 + h, lo:lo + n], big[:, h, lo:T1], start=True, stop=True)
            last.then_inc(*m.mark(f"S{h}"))
            if h:
                pe.wait_ge(*a_.at(f"vt{h - 1}1"))
            for d in range(2):
                for b, (lo, n) in enumerate(JB):
                    last = nc.tensor.transpose(bank[(3, 7)[d]][0:n, b * P:(b + 1) * P], big[:, 8 + 2 * h + d, lo:lo + n], ident)
                last.then_inc(*m.mark(f"vt{h}{d}"))
            pe.wait_ge(*pl.at(f"P{h}"))
            pe.wait_ge(*a_.at(f"vt{h}1"))
            if h:
                pe.wait_ge(*v.at(f"y{h - 1}1"))
            for d in range(3):
                for b, (lo, n) in enumerate(JB):
                    w = ones[0:n, :] if d == 2 else work[0:n, 3640 + b * 256 + d * P:3640 + b * 256 + (d + 1) * P]
                    last = mm(bank[4 + d][:, lo:T1], w, pbuf[0:n, OFF[b]:OFF[b] + T1 - lo], start=(b == 0), stop=(b == 2))
                last.then_inc(*m.mark(f"n{h}{d}"))
            for d in range(2):
                pe.wait_ge(*a_.at(f"sq{h}{d}"))
                last = mm(bank[3][:, 0:T1], ones, hh[2 + d], start=(d == 0), stop=(d == 1))
            last.then_inc(*m.mark(f"ss{h}"))
            if h + 1 < MH:
                pe.wait_ge(*a_.at(f"ln{h}"))

    def ml_act(act):
        m, v, a_, pl = S("ml", "pe"), S("ml", "dve"), S("ml", "act"), S("ml", "pool")
        A = nc.scalar.activation
        for h in range(MH):
            act.wait_ge(*m.at(f"rows{h}"))
            if h:
                act.wait_ge(*v.at(f"den{h - 1}"))
            A(em, bank[1][:, 0:T1], ACT.Exp, scale=-1.0).then_inc(*a_.mark(f"em{h}"))
            act.wait_ge(*v.at(f"Z{h}"))
            A(zbuf[:, 0:416], zbuf[:, 0:416], ACT.Exp, scale=-1.0).then_inc(*a_.mark(f"Ea{h}"))
            A(zbuf[0:16, 416:432], zbuf[0:16, 416:432], ACT.Exp, scale=-1.0).then_inc(*a_.mark(f"E{h}"))
            for d in range(2):
                act.wait_ge(*m.at(f"vt{h}{d}"))
                if h:
                    act.wait_ge(*m.at(f"n{h - 1}2"))
                bk = bank[(3, 7)[d]]
                A(vt[:, 0:2, d * P:(d + 1) * P], bk[:, 0:256].rearrange("p (b d) -> p b d", b=2), ACT.Copy).then_inc(*a_.mark(f"vta{h}{d}"))
                A(vt[0:16, 2, d * P:(d + 1) * P], bk[0:16, 256:384], ACT.Copy).then_inc(*a_.mark(f"vt{h}{d}"))
            act.wait_ge(*m.at(f"n{h}2"))
            if h:
                act.wait_ge(*v.at(f"o{h - 1}1"))
            A(rden, bank[6][:, 0:T1], ACT.Abs).then_inc(*a_.mark(f"ab{h}"))
            for d in range(2):
                act.wait_ge(*v.at(f"y{h}{d}"))
                if h:
                    act.wait_ge(*m.at(f"ss{h - 1}"))
                A(hh[2 + d], hh[d], ACT.Square).then_inc(*a_.mark(f"sq{h}{d}"))
            act.wait_ge(*m.at(f"ss{h}"))
            A(rden, bank[3][:, 0:T1], ACT.Ln, bias=eps_1, scale=1.0 / MV).then_inc(*a_.mark(f"ln{h}"))
            act.wait_ge(*a_.at(f"ln{h}"))
            A(rden, rden, ACT.Exp, scale=-0.5).then_inc(*a_.mark(f"rs{h}"))

    def ml_dve(dve):
        m, v, a_, pl = S("ml", "pe"), S("ml", "dve"), S("ml", "act"), S("ml", "pool")
        ts, stt, tt = nc.vector.tensor_scalar, nc.vector.scalar_tensor_tensor, nc.vector.tensor_tensor
        dve.wait_ge(*m.at("ctok"))
        nc.vector.tensor_copy(c_tok[:, 0:8], bank[0][:, 0:8]).then_inc(*v.mark("ctoka"))
        nc.vector.tensor_copy(c_tok[0:16, 8:12], bank[0][0:16, 8:12]).then_inc(*v.mark("ctok"))
        dve.wait_ge(*v.at("ctok"))
        for h in range(MH):
            dve.wait_ge(*m.at(f"rows{h}"))
            if h:
                dve.wait_ge(*v.at(f"P{h - 1}"))
            for b, (lo, n) in enumerate(JB):
                ts(zbuf[0:n, OFF[b]:OFF[b] + T1 - lo], bank[0][0:n, lo:T1], work[0:n, 2180 + 4 * b + h:2181 + 4 * b + h], 0.0,
                   ALU.subtract, ALU.max).then_inc(*v.mark(f"Z{h}" if b == 2 else f"Z{h}{b}"))
            dve.wait_ge(*a_.at(f"E{h}"))
            dve.wait_ge(*m.at(f"S{h}"))
            if h:
                dve.wait_ge(*m.at(f"n{h - 1}2"))
            tt(pbuf[:, 0:416], zbuf[:, 0:416], bank[2][:, 0:416], ALU.mult).then_inc(*v.mark(f"Pa{h}"))
            tt(pbuf[0:16, 416:432], zbuf[0:16, 416:432], bank[2][0:16, 416:432], ALU.mult).then_inc(*v.mark(f"P{h}"))
            dve.wait_ge(*a_.at(f"ab{h}"))
            tt(rden, rden, em, ALU.max).then_inc(*v.mark(f"den{h}"))
            dve.wait_ge(*v.at(f"den{h}"))
            nc.vector.reciprocal(rden, rden).then_inc(*v.mark(f"r{h}"))
            dve.wait_ge(*v.at(f"r{h}"))
            for d in range(2):
                tt(hh[d], bank[4 + d][:, 0:T1], rden, ALU.mult).then_inc(*v.mark(f"y{h}{d}"))
            dve.wait_ge(*a_.at(f"rs{h}"))
            for d in range(2):
                stt(hh[d], hh[d], pv("ml_norm", 2 * h + d), rden, ALU.mult, ALU.mult).then_inc(*v.mark(f"w{h}{d}"))
            for d in range(2):
                dve.wait_ge(*v.at(f"w{h}{d}"))
                tt(mix[:, 2 * h + d, :], hh[d], big[:, 16 + 2 * h + d, :], ALU.mult).then_inc(*v.mark(f"o{h}{d}"))

    def ml_pool(pool):
        v, pl = S("ml", "dve"), S("ml", "pool")
        for h in range(MH):
            pool.wait_ge(*v.at(f"P{h}"))
            for b, (lo, n) in enumerate(JB):
                o = pbuf[0:n, OFF[b]:OFF[b] + n]
                nc.gpsimd.tensor_tensor(o, o, cn("upto")[0:n, 0:n], ALU.mult).then_inc(*pl.mark(f"P{h}" if b == 2 else f"P{h}{b}"))

    X = lambda k: hs[:, k, N_META:T1]
    yt, sqt = (lambda m: y[:, m, 0:T2]), (lambda m: sq[:, m, 0:T2])

    def ln_pe(pe, n):
        name, g = f"ln{n}", G[f"lm{n}"]
        pe.wait_ge(bank_free, g + 1)
        for m in range(KC):
            pe.wait_ge(bank_free, 8 + g - 8 + m + 1)
            last = nc.tensor.matmul(bank[g % 8][:, 0:T2], ones, yt(m), start=(m == 0), stop=(m == KC - 1))
        last.then_inc(*S("norm", "pe").mark(name + "m"))
        pe_sum(pe, name + "v", g + 1, sqt, "act", T2)

    def ln_act(act, n, which, layer):
        name, g = f"ln{n}", G[f"lm{n}"]
        for m in range(KC):
            act.wait_ge(*S("norm", "dve").at(f"{name}_c{m}"))
            nc.scalar.activation(sqt(m), yt(m), ACT.Square).then_inc(*S("norm", "act").mark(f"{name}v_{m}"))
        act.wait_ge(bank_free, 8 + g + 1)
        act_scale(act, name + "v", g + 1, rs[:, 0, 0:T2], T2, D, eps_ln, None)
        for m in range(KC):
            act.wait_ge(*S("norm", "dve").at(f"{name}_g{m}"))
            nc.scalar.activation(X(m), yt(m), ACT.Identity, bias=pv(which, (2 * layer + 1) * KC + m)
                                 ).then_inc(*S("norm", "act").mark(f"{name}_x{m}"))
        if n < 3:
            x_act(act, name)

    def x_act(act, name):
        for m in range(KC):
            if name != "b2":
                act.wait_ge(*S("norm", "act").at(f"{name}_x{m}"))
            nc.scalar.activation(xs[:, m, 0:T2], X(m), ACT.Copy).then_inc(*S("norm", "act").mark(f"{name}_hi{m}"))

    def x_dve(dve, name):
        for m in range(KC):
            dve.wait_ge(*S("norm", "act").at(f"{name}_hi{m}"))
            nc.vector.tensor_tensor(xs[:, KC + m, 0:T2], X(m), xs[:, m, 0:T2].bitcast(F32), ALU.subtract
                                    ).then_inc(*S("norm", "dve").mark(f"{name}_lo{m}"))

    def ln_dve(dve, n, which, layer, last_block):
        name, g = f"ln{n}", G[f"lm{n}"]
        st = S("norm", "dve")
        stt = nc.vector.scalar_tensor_tensor
        dve.wait_ge(block_used, last_block)
        for m in range(KC):
            stt(yt(m), X(m), ALPHA, bank[(g - 8 + m) % 8][:, 0:T2], ALU.mult, ALU.add).then_inc(bank_free, 1)
        dve.wait_ge(*S("norm", "pe").at(name + "m"))
        for m in range(KC):
            stt(yt(m), bank[g % 8][:, 0:T2], -1.0 / D, yt(m), ALU.mult, ALU.add).then_inc(*st.mark(f"{name}_c{m}"))
        dve.wait_ge(*st.at(f"{name}_c7"))
        nc.vector.memset(rs[:, 1, 0:1], 0.0).then_inc(bank_free, 1)
        dve.wait_ge(*S("norm", "act").at(f"{name}v_scale"))
        for m in range(KC):
            stt(yt(m), yt(m), pv(which, 2 * layer * KC + m), rs[:, 0, 0:T2], ALU.mult, ALU.mult).then_inc(*st.mark(f"{name}_g{m}"))
        if n < 3:
            x_dve(dve, name)

    def in_act(act, phase, kinds):
        g0, b0 = G[phase], FIRST_BLOCK[phase]
        for t, (fn, scale) in enumerate(kinds):
            split_hi(act, b0 + t + AHEAD)
            act.wait_ge(block_used, b0 + t + 1)
            nc.scalar.activation(big[:, t, 0:T2], bank[(g0 + t) % 8][:, 0:T2], fn, scale=scale).then_inc(bank_free, 1)

    QB = 2
    probs = work[:, 0:2048]
    ptr = work[:, 2048:4096]
    st8 = lambda k: work[:, 4096 + 8 * k:4104 + 8 * k]
    qrot = [work[0:96, 4160 + h * T2:4160 + (h + 1) * T2] for h in range(4)]
    krot = [work[0:96, 5184 + h * T2:5184 + (h + 1) * T2] for h in range(4)]
    spare = big[:, 18:24, :].rearrange("p a b -> p (a b)")
    vmla = spare[:, 0:1024].rearrange("p (b d) -> p b d", b=2)
    vswa = spare[:, 1024:1280].rearrange("p (b d) -> p b d", b=2)
    krr, tmp96 = work[0:96, 6208:6464], work[0:96, 6464:6720]

    def attn_pe(pe, ph, units, vtok, width, slots):
        m, v, a_ = S(ph, "pe"), S(ph, "dve"), S(ph, "act")
        mm = nc.tensor.matmul
        U = len(units)
        for n in range(QB):
            W = 128 * (n + 1)
            per = 512 // W
            if n:
                pe.wait_ge(*a_.at("out0"))
            for u, (q, k) in enumerate(units):
                b, o = u // per, (u % per) * W
                last = mm(bank[b][:, o:o + W], q[:, n * 128:(n + 1) * 128], k[:, 0:W], start=True, stop=True)
            last.then_inc(*m.mark(f"s{n}"))
            pe.wait_ge(*v.at(f"p{n}"))
            for j in range(n + 1):
                for u in range(U):
                    t = j * U + u
                    last = nc.tensor.transpose(bank[t // 4][:, (t % 4) * 128:(t % 4 + 1) * 128],
                                               probs[:, u * W + j * 128:u * W + (j + 1) * 128], ident)
                    if t % 4 == 3:
                        last.then_inc(*m.mark(f"t{n}_{t // 4}"))
            for t in range((n + 1) * U // 4):
                pe.wait_ge(*a_.at(f"t{n}_{t}"))
            for u in range(U):
                for j in range(n + 1):
                    o, w = vtok(u, j)
                    t = j * U + u
                    last = mm(o, w, ptr[:, t * 128:(t + 1) * 128], start=(j == 0), stop=(j == n))
            last.then_inc(*m.mark(f"o{n}"))

    def attn_act(act, ph, U, sink, slot):
        m, v, a_ = S(ph, "pe"), S(ph, "dve"), S(ph, "act")
        A = nc.scalar.activation
        for n in range(QB):
            W = 128 * (n + 1)
            act.wait_ge(*v.at(f"e{n}"))
            A(probs[:, 0:U * W], probs[:, 0:U * W], ACT.Exp).then_inc(*a_.mark(f"e{n}"))
            if sink:
                A(st8(2), st8(2), ACT.Exp).then_inc(*a_.mark(f"es{n}"))
            for t in range((n + 1) * U // 4):
                act.wait_ge(*m.at(f"t{n}_{t}"))
                A(ptr[:, t * 512:(t + 1) * 512], bank[t][:, :], ACT.Copy).then_inc(*a_.mark(f"t{n}_{t}"))
            act.wait_ge(*m.at(f"o{n}"))
            A(mix[:, slot:slot + 4, n * 128:(n + 1) * 128], bank[7][:, :].rearrange("p (t i) -> p t i", t=4), ACT.Copy
              ).then_inc(*a_.mark(f"out{n}"))

    def attn_dve(dve, ph, U, scale, mask, sink):
        m, v, a_ = S(ph, "pe"), S(ph, "dve"), S(ph, "act")
        ts, stt, tt = nc.vector.tensor_scalar, nc.vector.scalar_tensor_tensor, nc.vector.tensor_tensor
        for n in range(QB):
            W = 128 * (n + 1)
            per = 512 // W
            pr = probs[:, 0:U * W].rearrange("p (u w) -> p u w", u=U)
            mk = (mask if n else mask[:, 128:256]).unsqueeze(1).to_broadcast([P, per, W])
            dve.wait_ge(*m.at(f"s{n}"))
            for b in range(U // per):
                stt(pr[:, b * per:(b + 1) * per, :], bank[b][:, :].rearrange("p (u w) -> p u w", u=per), scale, mk,
                    ALU.mult, ALU.add).then_inc(*v.mark(f"s{n}_{b}"))
            dve.wait_ge(*v.at(f"s{n}_{U // per - 1}"))
            mx, ng, es, sm = (st8(k)[:, 0:U] for k in range(4))
            nc.vector.reduce_max(mx, pr, axis=AX).then_inc(*v.mark(f"mx{n}"))
            dve.wait_ge(*v.at(f"mx{n}"))
            if sink:
                tt(mx, mx, pv("sinks", 0, 8), ALU.max).then_inc(*v.mark(f"ms{n}"))
                dve.wait_ge(*v.at(f"ms{n}"))
                tt(es, pv("sinks", 0, 8), mx, ALU.subtract).then_inc(*v.mark(f"es{n}"))
            tt(pr, pr, mx.unsqueeze(2).to_broadcast([P, U, W]), ALU.subtract).then_inc(*v.mark(f"e{n}"))
            dve.wait_ge(*a_.at(f"e{n}"))
            nc.vector.reduce_sum(sm, pr, axis=AX).then_inc(*v.mark(f"sm{n}"))
            dve.wait_ge(*v.at(f"sm{n}"))
            if sink:
                dve.wait_ge(*a_.at(f"es{n}"))
                tt(sm, sm, es, ALU.add).then_inc(*v.mark(f"sd{n}"))
                dve.wait_ge(*v.at(f"sd{n}"))
            nc.vector.reciprocal(ng, sm).then_inc(*v.mark(f"r{n}"))
            dve.wait_ge(*v.at(f"r{n}"))
            tt(pr, pr, ng.unsqueeze(2).to_broadcast([P, U, W]), ALU.mult).then_inc(*v.mark(f"p{n}"))

    def swa_units():
        return [(big[64 * a:64 * a + 64, 12 + t, 0:T2], big[64 * a:64 * a + 64, 16, 0:T2]) for a in range(2) for t in range(4)]

    def swa_v(u, j):
        a, t = divmod(u, 4)
        return bank[7][64 * a:64 * a + 64, t * 128:(t + 1) * 128], vswa[:, j, 64 * a:64 * a + 64]

    def even_pe(pe):
        m, a_ = S("swa", "pe"), S("swa", "act")
        pe.wait_ge(bank_free, 8 + G["ev_out"])
        for j in range(2):
            last = nc.tensor.transpose(bank[6][:, j * 128:(j + 1) * 128], big[:, 17, j * 128:(j + 1) * 128], ident)
        last.then_inc(*m.mark("vt"))
        attn_pe(pe, "swa", swa_units(), swa_v, 64, 4)

    def even_act(act):
        act.wait_ge(*S("swa", "pe").at("vt"))
        nc.scalar.activation(vswa, bank[6][:, 0:256].rearrange("p (b d) -> p b d", b=2), ACT.Copy).then_inc(*S("swa", "act").mark("vt"))
        attn_act(act, "swa", 8, True, 4)

    def even_pool(pool):
        pl = S("swa", "pool")
        pool.wait_ge(bank_free, 8 + G["ev_out"])
        for t in range(4):
            nc.gpsimd.tensor_tensor(cv[:, t, 0:T2], big[:, 4 + t, 0:T2], big[:, 8 + t, 0:T2], ALU.mult).then_inc(*pl.mark(f"z{t}"))
        for t in range(4):
            pool.wait_ge(*S("swa", "dve").at(f"z{t}_2"))
            nc.gpsimd.tensor_tensor(mix[:, t, 0:T2], cv[:, 4 + t, 0:T2], big[:, t, 0:T2], ALU.mult).then_inc(*pl.mark(f"y{t}"))

    def even_dve(dve):
        v, pl = S("swa", "dve"), S("swa", "pool")
        attn_dve(dve, "swa", 8, 64 ** -0.5, cn("swa_mask"), True)
        for tap in range(3):
            for t in range(4):
                w = pv("ev_conv", 3 * t + 2 - tap)
                o, z = cv[:, 4 + t, 0:T2], cv[:, t, 0:T2]
                if tap == 0:
                    dve.wait_ge(*pl.at(f"z{t}"))
                    nc.vector.tensor_scalar(o, z, w, None, ALU.mult).then_inc(*v.mark(f"z{t}_0"))
                else:
                    dve.wait_ge(*v.at(f"z{t}_{tap - 1}"))
                    nc.vector.scalar_tensor_tensor(o[:, tap:], z[:, 0:T2 - tap], w, o[:, tap:], ALU.mult, ALU.add
                                                   ).then_inc(*v.mark(f"z{t}_{tap}"))

    GR, NG = 16, T2 // 16
    LA, LB, RR = (xf[:, 2 * s:2 * s + 2, 0:T2] for s in range(3))
    QG = xf[:, 6:8, 0:T2]
    KG = [y[:, 2 * s:2 * s + 2, 0:T2] for s in range(4)]
    last_tiles = big[:, 33:48, :].rearrange("p a b -> p (a b)")
    gp = [last_tiles[:, h * 384:384 + h * 384] for h in range(4)]
    vg = last_tiles[:, 1536:2560].rearrange("p (b d) -> p b d", b=2)
    go = [sq[:, h, 0:T2] for h in range(4)]
    gs = [sq[:, 4 + h, 0:T2] for h in range(4)]
    glow = cv[0:16, 0, 0:T2]

    def odd_pe(pe):
        m, v, a_, pl = S("gla", "pe"), S("gla", "dve"), S("gla", "act"), S("gla", "pool")
        mm = nc.tensor.matmul
        pe.wait_ge(bank_free, 8 + G["od_out"])
        pe.wait_ge(*a_.at("glow"))
        for t in range(2):
            last = mm(bank[0][:, t * T2:(t + 1) * T2], pv("gla_w", 128 * t, 128, 16), glow, start=True, stop=True)
        last.then_inc(*m.mark("gate"))
        for h in range(4):
            for j in range(2):
                last = nc.tensor.transpose(bank[1 + j][:, h * 128:(h + 1) * 128], big[:, 4 + h, j * 128:(j + 1) * 128], ident)
        last.then_inc(*m.mark("vt"))
        mla_pe(pe)
        pe.wait_ge(*S("mla", "act").at("out1"))
        pe.wait_ge(*v.at("qg"))
        for g in range(NG):
            pe.wait_ge(*pl.at(f"k{g}"))
            for h in range(4):
                t, a = divmod(h, 2)
                rows = slice(64 * a, 64 * a + 64)
                for j in range(1 if g < 8 else 2):
                    o = (0 if j == 0 else 128) + 16 * g
                    last = mm(bank[3 + h][:, o:o + 16], KG[g % 4][rows, t, j * 128:(j + 1) * 128], QG[rows, t, 16 * g:16 * g + 16],
                              start=True, stop=True)
            last.then_inc(*m.mark(f"s{g}"))
        for h in range(4):
            pe.wait_ge(*v.at(f"p{h}"))
            b = (0, 1, 2, 7)[h]
            mm(bank[b][:, 0:T2], vg[:, 0, h * 128:(h + 1) * 128], gp[h][:, 0:T2], start=True, stop=False)
            mm(bank[b][:, 128:T2], vg[:, 1, h * 128:(h + 1) * 128], gp[h][:, T2:T2 + 128], start=False, stop=True
               ).then_inc(*m.mark(f"o{h}"))
        for h in range(4):
            pe.wait_ge(*a_.at(f"sq{h}"))
            mm(bank[3 + h][:, 0:T2], ones, gs[h], start=True, stop=True).then_inc(*m.mark(f"ss{h}"))

    def odd_gate_act(act):
        act.wait_ge(*S("gates", "pe").at("od0"))
        nc.scalar.activation(glow, bank[G["od_g"] % 8][0:16, 0:T2], ACT.Copy).then_inc(bank_free, 1)

    def odd_act(act):
        m, v, a_, pl = S("gla", "pe"), S("gla", "dve"), S("gla", "act"), S("gla", "pool")
        A = nc.scalar.activation
        act.wait_ge(bank_free, 8 + G["od_g"] + 1)
        A(rs[:, 1, 0:1], eps_1, ACT.Copy).then_inc(*a_.mark("glow"))
        act.wait_ge(*m.at("gate"))
        for t in range(2):
            A(LA[:, t, :], bank[0][:, t * T2:(t + 1) * T2], ACT.Identity, bias=pv("gla_b", t)).then_inc(*a_.mark(f"x{t}"))
        act.wait_ge(*a_.at("x1"))
        A(LB, LA, ACT.Abs).then_inc(*a_.mark("abs"))
        act.wait_ge(*a_.at("abs"))
        A(LB, LB, ACT.Exp, scale=-1.0).then_inc(*a_.mark("e"))
        act.wait_ge(*a_.at("e"))
        A(LB, LB, ACT.Ln, bias=1.0).then_inc(*a_.mark("ln"))
        act.wait_ge(*m.at("vt"))
        for j in range(2):
            A(vg[:, j, :], bank[1 + j][:, :], ACT.Copy).then_inc(*a_.mark(f"vt{j}"))
        mla_act(act)
        act.wait_ge(*v.at("dq"))
        A(QG, QG, ACT.Exp).then_inc(*a_.mark("qg"))
        for g in range(NG):
            W = 128 if g < 8 else 256
            act.wait_ge(*v.at(f"k{g}"))
            A(KG[g % 4][:, :, 0:W], KG[g % 4][:, :, 0:W], ACT.Exp, scale=-1.0).then_inc(*a_.mark(f"k{g}"))
        for h in range(4):
            act.wait_ge(*m.at(f"o{h}"))
            A(gs[h], bank[(0, 1, 2, 7)[h]][:, 0:T2], ACT.Square).then_inc(*a_.mark(f"sq{h}"))
        for h in range(4):
            act.wait_ge(*m.at(f"ss{h}"))
            A(gs[h], bank[3 + h][:, 0:T2], ACT.Ln, scale=1.0 / 128, bias=eps_1).then_inc(*a_.mark(f"l{h}"))
        for h in range(4):
            act.wait_ge(*a_.at(f"l{h}"))
            A(gs[h], gs[h], ACT.Exp, scale=-0.5).then_inc(*a_.mark(f"r{h}"))

    def odd_dve(dve):
        m, v, a_, pl = S("gla", "pe"), S("gla", "dve"), S("gla", "act"), S("gla", "pool")
        ts, stt, tt = nc.vector.tensor_scalar, nc.vector.scalar_tensor_tensor, nc.vector.tensor_tensor
        dve.wait_ge(*a_.at("ln"))
        ts(LA, LA, 0.0, 1.0 / 16, ALU.min, ALU.mult).then_inc(*v.mark("min"))
        dve.wait_ge(*v.at("min"))
        stt(LA, LB, -1.0 / 16, LA, ALU.mult, ALU.add).then_inc(*v.mark("la"))
        dve.wait_ge(*v.at("la"))
        b = scan(dve, v, "b", LA, LB, ALU.add, T2)
        groups = lambda ap: ap.rearrange("p t (g k) -> p t g k", k=GR)
        r = RR[:, :, 0:NG]
        nc.vector.memset(r[:, :, 0:1], 0.0).then_inc(*v.mark("r0"))
        nc.vector.tensor_copy(r[:, :, 1:NG], groups(b)[:, :, 0:NG - 1, GR - 1]).then_inc(*v.mark("r"))
        dve.wait_ge(*v.at("r"))
        tt(groups(QG), groups(b), r.unsqueeze(3).to_broadcast([P, 2, NG, GR]), ALU.subtract).then_inc(*v.mark("dq"))
        mla_dve(dve)
        dve.wait_ge(*a_.at("qg"))
        tt(QG, QG, big[:, 0:2, 0:T2], ALU.mult).then_inc(*v.mark("qg"))
        for g in range(NG):
            W = 128 if g < 8 else 256
            if g >= 4:
                dve.wait_ge(*m.at(f"s{g - 4}"))
            for t in range(2):
                ts(KG[g % 4][:, t, 0:W], b[:, t, 0:W], RR[:, t, g:g + 1], -80.0, ALU.subtract, ALU.max
                   ).then_inc(*v.mark(f"k{g}" if t else f"k{g}a"))
        dve.wait_ge(*m.at(f"s{NG - 1}"))
        for h in range(4):
            tt(gp[h][:, 0:128], bank[3 + h][:, 0:128], cn("upto"), ALU.mult).then_inc(*v.mark(f"pa{h}"))
            nc.vector.tensor_copy(gp[h][:, 128:256], bank[3 + h][:, 128:256]).then_inc(*v.mark(f"pb{h}"))
            tt(gp[h][:, 256:384], bank[3 + h][:, 256:384], cn("upto"), ALU.mult).then_inc(*v.mark(f"p{h}"))
        for h in range(4):
            dve.wait_ge(*a_.at(f"r{h}"))
            tt(go[h], bank[(0, 1, 2, 7)[h]][:, 0:T2], gs[h], ALU.mult).then_inc(*v.mark(f"y{h}"))
        for h in range(4):
            dve.wait_ge(*v.at(f"y{h}"))
            stt(mix[:, h, 0:T2], go[h], pv("gla_norm"), big[:, 8 + h, 0:T2], ALU.mult, ALU.mult).then_inc(*v.mark(f"o{h}"))

    def odd_pool(pool):
        m, v, a_, pl = S("gla", "pe"), S("gla", "dve"), S("gla", "act"), S("gla", "pool")
        for g in range(NG):
            W = 128 if g < 8 else 256
            pool.wait_ge(*a_.at(f"k{g}"))
            nc.gpsimd.tensor_tensor(KG[g % 4][:, :, 0:W], KG[g % 4][:, :, 0:W], big[:, 2:4, 0:W], ALU.mult).then_inc(*pl.mark(f"k{g}"))

    cq = [cv[:, 1 + t, 0:T2] for t in range(2)]
    ckv = cv[:, 3, 0:T2]
    csq = [cv[:, 4 + t, 0:T2] for t in range(3)]
    crs = [cv[:, 7, 0:T2], rs[:, 1, 0:T2]]
    MLAW = big[:, 24:33, :].rearrange("p a b -> p (a b)")[:, 0:2304]

    def mla_pe(pe):
        m, v, a_ = S("mla", "pe"), S("mla", "dve"), S("mla", "act")
        mm = nc.tensor.matmul
        pe.wait_ge(*a_.at("sq"))
        for t in range(2):
            last = mm(bank[3][:, 0:T2], ones, csq[t], start=(t == 0), stop=(t == 1))
        last = mm(bank[4][:, 0:T2], ones, csq[2], start=True, stop=True)
        last.then_inc(*m.mark("ss"))
        pe.wait_ge(*v.at("ckv"))
        pe.wait_ge(mla_loaded, 16)
        B = (0, 5, 6, 7)
        for h in range(4):
            if h == 0:
                pe.wait_ge(*S("gla", "act").at("x1"))
            for s in range(2):
                for t in range(2):
                    last = mm(bank[B[h]][0:96, s * T2:(s + 1) * T2], MLAW[:, 768 * s + 384 * t + 96 * h:768 * s + 384 * t + 96 * h + 96],
                              cq[t], start=(t == 0), stop=(t == 1))
            last.then_inc(*m.mark(f"q{h}"))
        pe.wait_ge(*S("gla", "act").at("vt1"))
        for h in range(4):
            last = mm(bank[1 + h // 2][0:64, (h % 2) * T2:(h % 2 + 1) * T2], MLAW[:, 1536 + 64 * h:1600 + 64 * h], ckv, start=True, stop=True)
        last.then_inc(*m.mark("k"))
        pe.wait_ge(*a_.at("rkv"))
        for j in range(2):
            last = mm(bank[3 + j][:, :], ckv[:, j * 128:(j + 1) * 128], MLAW[:, 1792:2304], start=True, stop=True)
        last.then_inc(*m.mark("v"))
        pe.wait_ge(*v.at("q3"))
        pe.wait_ge(*a_.at("v1"))
        units = [(qrot[h], krot[h]) for h in range(4)]
        attn_pe(pe, "mla", units, lambda u, j: (bank[7][:, u * 128:(u + 1) * 128], vmla[:, j, u * 128:(u + 1) * 128]), 128, 4)

    def mla_act(act):
        m, v, a_ = S("mla", "pe"), S("mla", "dve"), S("mla", "act")
        A = nc.scalar.activation
        for t in range(3):
            last = A(csq[t], big[:, 12 + t, 0:T2], ACT.Square)
        last.then_inc(*a_.mark("sq"))
        act.wait_ge(*m.at("ss"))
        for n, name in enumerate(("q", "kv")):
            A(crs[n], bank[3 + n][:, 0:T2], ACT.Ln, scale=1.0 / (256, 128)[n], bias=eps_1).then_inc(*a_.mark(f"l{name}"))
        for n, name in enumerate(("q", "kv")):
            act.wait_ge(*a_.at(f"l{name}"))
            A(crs[n], crs[n], ACT.Exp, scale=-0.5).then_inc(*a_.mark(f"r{name}"))
        act.wait_ge(*m.at("k"))
        for h in range(4):
            A(krot[h][0:64], bank[1 + h // 2][0:64, (h % 2) * T2:(h % 2 + 1) * T2], ACT.Copy).then_inc(*a_.mark(f"k{h}"))
        act.wait_ge(*m.at("v"))
        for j in range(2):
            A(vmla[:, j, :], bank[3 + j][:, :], ACT.Copy).then_inc(*a_.mark(f"v{j}"))
        attn_act(act, "mla", 4, False, 4)

    def mla_dve(dve):
        m, v, a_ = S("mla", "pe"), S("mla", "dve"), S("mla", "act")
        ts, stt, tt = nc.vector.tensor_scalar, nc.vector.scalar_tensor_tensor, nc.vector.tensor_tensor
        dve.wait_ge(*a_.at("rkv"))
        for t in range(2):
            stt(cq[t], big[:, 12 + t, 0:T2], pv("mla_qn", t), crs[0], ALU.mult, ALU.mult).then_inc(*v.mark(f"cq{t}"))
        stt(ckv, big[:, 14, 0:T2], pv("mla_kvn"), crs[1], ALU.mult, ALU.mult).then_inc(*v.mark("ckv"))
        cos, sin = cn("cos", 96), cn("sin", 96)
        tt(krr[64:96], big[64:96, 15, 0:T2], cos[64:96], ALU.mult).then_inc(*v.mark("kr0"))
        tt(tmp96[64:96], big[64:96, 16, 0:T2], sin[64:96], ALU.mult).then_inc(*v.mark("kr1"))
        dve.wait_ge(*v.at("kr1"))
        for h in range(4):
            tt(krot[h][64:96], krr[64:96], tmp96[64:96], ALU.add).then_inc(*v.mark(f"kr{h + 2}"))
        for h in range(4):
            bk = bank[(0, 5, 6, 7)[h]]
            dve.wait_ge(*m.at(f"q{h}"))
            tt(qrot[h], bk[0:96, 0:T2], cos, ALU.mult).then_inc(*v.mark(f"qa{h}"))
            dve.wait_ge(*v.at(f"q{h - 1}" if h else "kr5"))
            tt(tmp96, bk[0:96, T2:2 * T2], sin, ALU.mult).then_inc(*v.mark(f"qb{h}"))
            dve.wait_ge(*v.at(f"qb{h}"))
            tt(qrot[h], qrot[h], tmp96, ALU.add).then_inc(*v.mark(f"q{h}"))
        attn_dve(dve, "mla", 4, 96 ** -0.5, cn("mla_mask"), False)
    con_eps = sb("con_eps", [P, 4])

    def sp_out(sp):
        o = out.rearrange("p (c t) -> p c t", t=T2)
        for m in range(KC):
            sp.wait_ge(*S("norm", "act").at(f"ln3_x{m}"))
            sp.dma_start(o[:, m, :], X(m)).then_inc(stored, 16)
        sp.wait_ge(stored, 16 * KC)

    eps_1 = con_eps[:, 0:1]
    eps_q = con_eps[:, 1:2]
    eps_ln = con_eps[:, 2:3]
    block = ctx.enter_context(nc.Block())
    xk = lambda k: y[:, k, :]

    def mix_ready(name):
        return lambda pe, k, i: pe.wait_ge(*S("norm", "dve").at(f"{name}_lo{k}"))

    def even_done(e):
        e.wait_ge(*S("swa", "pool").at("y3"))
        e.wait_ge(*S("swa", "act").at("out1"))

    def odd_done(e):
        e.wait_ge(*S("gla", "dve").at("o3"))
        e.wait_ge(*S("mla", "act").at("out1"))

    mix1 = lambda k: mix[:, k, :]
    mix2 = lambda k: mix[:, k, 0:T2]

    @block.sync
    def _(sp):
        sp_stream(sp)
        sp_out(sp)

    @block.gpsimd
    def _(pool):
        nc.gpsimd.memset(con_eps[:, 2:3], LN_EPS).then_inc(*S("init", "pool").mark("epsln"))
        nc.gpsimd.memset(con_eps[:, 0:1], RMS_EPS).then_inc(*S("init", "pool").mark("eps"))
        nc.gpsimd.memset(con_eps[:, 1:2], L2_EPS * GD).then_inc(*S("init", "pool").mark("epsq"))
        gdn_pool(pool)
        ffn_pool(pool, 0, G["up0"])
        ml_pool(pool)
        ffn_pool(pool, 1, G["up1"])
        even_pool(pool)
        ffn_pool(pool, 2, G["up2"])
        odd_pool(pool)
        ffn_pool(pool, 3, G["up3"])

    @block.scalar
    def _(act):
        act.wait_ge(hs_loaded, 16)
        act.wait_ge(loaded, 32)
        act.wait_ge(*S("init", "pool").at("epsq"))
        for n in range(AHEAD):
            split_hi(act, n)
        nc.scalar.preload_act_table_set(LN_EXP)
        pre_act(act, "pre0", G["pre0"], lambda act, m: None)
        gdn_gates_act(act)
        nc.scalar.preload_act_table_set(SILU)
        gdn_in_act(act)
        nc.scalar.preload_act_table_set(LN_EXP)
        gdn_act(act)
        mix_act(act, "gdn", lambda k: big[:, 32 + k, :], 16, lambda e: e.wait_ge(*S("gdn", "dve").at("o3")))
        split_all(act, split_hi, "gdn_out")
        nc.scalar.preload_act_table_set(LN_EXP)
        post_act(act, "post0", G["post0"])
        nc.scalar.preload_act_table_set(LN_EXP)
        pre_act(act, "pre1", G["pre1"], lambda act, m: act.wait_ge(*S("norm", "dve").at(f"post0_h{m}")))
        nc.scalar.preload_act_table_set(SILU)
        ffn_act(act, 0, G["up0"])
        split_all(act, split_hi, "down0")
        nc.scalar.preload_act_table_set(LN_EXP)
        post_act(act, "post1", G["post1"])
        nc.scalar.preload_act_table_set(LN_EXP)
        pre_act(act, "pre2", G["pre2"], lambda act, m: act.wait_ge(*S("norm", "dve").at(f"post1_h{m}")))
        ml_gates_act(act)
        ml_in_act(act)
        nc.scalar.preload_act_table_set(LN_EXP)
        ml_act(act)
        mix_act(act, "ml", mix1, 8, lambda e: e.wait_ge(*S("ml", "dve").at("o31")))
        split_all(act, split_hi, "ml_out")
        nc.scalar.preload_act_table_set(LN_EXP)
        post_act(act, "post2", G["post2"])
        nc.scalar.preload_act_table_set(LN_EXP)
        pre_act(act, "pre3", G["pre3"], lambda act, m: act.wait_ge(*S("norm", "dve").at(f"post2_h{m}")))
        nc.scalar.preload_act_table_set(SILU)
        ffn_act(act, 1, G["up1"])
        split_all(act, split_hi, "down1")
        nc.scalar.preload_act_table_set(LN_EXP)
        post_act(act, "post3", G["post3"])
        act.wait_ge(*S("norm", "dve").at("post3_h7"))
        x_act(act, "b2")
        in_act(act, "ev_in", [(ACT.Copy, 1.0)] * 18)
        nc.scalar.preload_act_table_set(LN_EXP)
        even_act(act)
        mix_act(act, "ev", mix2, 8, even_done)
        split_all(act, split_hi, "ev_out")
        nc.scalar.preload_act_table_set(LN_EXP)
        ln_act(act, 0, "ln_mix", 0)
        nc.scalar.preload_act_table_set(SILU)
        ffn_act(act, 2, G["up2"])
        split_all(act, split_hi, "down2")
        nc.scalar.preload_act_table_set(LN_EXP)
        ln_act(act, 1, "ln_ffn", 0)
        act.wait_ge(block_used, used_after("down2"))
        act.dma_start(MLAW, mla).then_inc(mla_loaded, 16)
        odd_gate_act(act)
        nc.scalar.preload_act_table_set(SILU)
        in_act(act, "od_in", [(ACT.Copy, 0.125)] * 2 + [(ACT.Copy, 1.0)] * 6 + [(ACT.Silu, 1.0)] * 4 + [(ACT.Copy, 1.0)] * 5)
        nc.scalar.preload_act_table_set(LN_EXP)
        odd_act(act)
        mix_act(act, "od", mix2, 8, odd_done)
        split_all(act, split_hi, "od_out")
        nc.scalar.preload_act_table_set(LN_EXP)
        ln_act(act, 2, "ln_mix", 1)
        nc.scalar.preload_act_table_set(SILU)
        ffn_act(act, 3, G["up3"])
        split_all(act, split_hi, "down3")
        nc.scalar.preload_act_table_set(LN_EXP)
        ln_act(act, 3, "ln_ffn", 1)

    @block.vector
    def _(dve):
        nc.vector.memset(rs[:, 0, 0:1], 0.0).then_inc(bank_free, 8)
        nc.vector.memset(rs[:, 1, 0:1], 0.0).then_inc(conv_taken, 8)
        dve.wait_ge(loaded, 32)
        for n in range(AHEAD):
            split_lo(dve, n)
        pre_dve(dve, "pre0", 0)
        gdn_in_dve(dve)
        gdn_dve(dve)
        mix_dve(dve, "gdn", lambda k: big[:, 32 + k, :], 16, lambda e: e.wait_ge(*S("gdn", "dve").at("o3")))
        split_all(dve, split_lo, "gdn_out")
        post_dve(dve, "post0", G["post0"], 1, used_after("gdn_out"))
        pre_dve(dve, "pre1", 2)
        ffn_dve(dve, 0, G["up0"])
        split_all(dve, split_lo, "down0")
        post_dve(dve, "post1", G["post1"], 3, used_after("down0"))
        pre_dve(dve, "pre2", 4)
        ml_gates_dve(dve)
        split_all(dve, split_lo, "ml_in")
        ml_dve(dve)
        mix_dve(dve, "ml", mix1, 8, lambda e: e.wait_ge(*S("ml", "dve").at("o31")))
        split_all(dve, split_lo, "ml_out")
        post_dve(dve, "post2", G["post2"], 5, used_after("ml_out"))
        pre_dve(dve, "pre3", 6)
        ffn_dve(dve, 1, G["up1"])
        split_all(dve, split_lo, "down1")
        post_dve(dve, "post3", G["post3"], 7, used_after("down1"))
        x_dve(dve, "b2")
        split_all(dve, split_lo, "ev_in")
        even_dve(dve)
        mix_dve(dve, "ev", mix2, 8, even_done)
        split_all(dve, split_lo, "ev_out")
        ln_dve(dve, 0, "ln_mix", 0, used_after("ev_out"))
        ffn_dve(dve, 2, G["up2"])
        split_all(dve, split_lo, "down2")
        ln_dve(dve, 1, "ln_ffn", 0, used_after("down2"))
        split_all(dve, split_lo, "od_in")
        odd_dve(dve)
        mix_dve(dve, "od", mix2, 8, odd_done)
        split_all(dve, split_lo, "od_out")
        ln_dve(dve, 2, "ln_mix", 1, used_after("od_out"))
        ffn_dve(dve, 3, G["up3"])
        split_all(dve, split_lo, "down3")
        ln_dve(dve, 3, "ln_ffn", 1, used_after("down3"))

    @block.tensor
    def _(pe):
        pe.wait_ge(loaded, 32)
        pre_pe(pe, "pre0", G["pre0"])
        pe.wait_ge(*S("norm", "dve").at("pre0_lo7"))
        gates_pe(pe, "gdn", G["gdn_g"], ((0, 16), (16, 16)), "gdn_gates", 32, T1, xk)
        pe_tiles(pe, "gdn_in", G["gdn_in"])
        gdn_pe(pe)
        pe_wide(pe, "gdn_out", G["gdn_out"], mix_ready("gdn"))
        post_pe(pe, "post0", G["post0"])
        pre_pe(pe, "pre1", G["pre1"])
        pe.wait_ge(*S("norm", "dve").at("pre1_lo7"))
        pe_tiles(pe, "up0", G["up0"])
        pe_wide(pe, "down0", G["down0"], ffn_ready(0))
        post_pe(pe, "post1", G["post1"])
        pre_pe(pe, "pre2", G["pre2"])
        pe.wait_ge(*S("norm", "dve").at("pre2_lo7"))
        gates_pe(pe, "ml", G["ml_g"], ((0, 4), (4, 4)), "ml_gates", 8, T1, xk)
        pe_tiles(pe, "ml_in", G["ml_in"])
        ml_pe(pe)
        pe_wide(pe, "ml_out", G["ml_out"], mix_ready("ml"))
        post_pe(pe, "post2", G["post2"])
        pre_pe(pe, "pre3", G["pre3"])
        pe.wait_ge(*S("norm", "dve").at("pre3_lo7"))
        pe_tiles(pe, "up1", G["up1"])
        pe_wide(pe, "down1", G["down1"], ffn_ready(1))
        post_pe(pe, "post3", G["post3"])
        pe.wait_ge(*S("norm", "dve").at("b2_lo7"))
        pe_tiles(pe, "ev_in", G["ev_in"])
        even_pe(pe)
        pe_wide(pe, "ev_out", G["ev_out"], mix_ready("ev"))
        ln_pe(pe, 0)
        pe.wait_ge(*S("norm", "dve").at("ln0_lo7"))
        pe_tiles(pe, "up2", G["up2"])
        pe_wide(pe, "down2", G["down2"], ffn_ready(2))
        ln_pe(pe, 1)
        pe.wait_ge(*S("norm", "dve").at("ln1_lo7"))
        gates_pe(pe, "od", G["od_g"], ((0, 16),), "g_low", 16, T2, X)
        pe_tiles(pe, "od_in", G["od_in"])
        odd_pe(pe)
        pe_wide(pe, "od_out", G["od_out"], mix_ready("od"))
        ln_pe(pe, 2)
        pe.wait_ge(*S("norm", "dve").at("ln2_lo7"))
        pe_tiles(pe, "up3", G["up3"])
        pe_wide(pe, "down3", G["down3"], ffn_ready(3))
        ln_pe(pe, 3)
    ctx.close()

INPUTS = ["stream", "params", "consts", "mla", "hs"]


def kernel(**inputs):
    import concourse.bacc as bacc
    from concourse.bass_utils import run_bass_kernel_spmd

    table = {}
    for _ in range(2):
        nc = bacc.Bacc("TRN2", target_bir_lowering=False, num_devices=1)
        aps = [nc.dram_tensor(name, SHAPES[name], F32, kind="ExternalInput").ap() for name in INPUTS]
        out = nc.dram_tensor("y_out", (P, KC * T2), F32, kind="ExternalOutput").ap()
        build(nc, *aps, out, table)
    arrays = lay_out({name: np.asarray(v) for name, v in inputs.items()})
    result = run_bass_kernel_spmd(nc, [arrays], core_ids=[0]).results[0]["y_out"]
    return np.ascontiguousarray(result.reshape(P, KC, T2).transpose(2, 1, 0).reshape(1, T2, D))
```

```python
from contextlib import ExitStack

import numpy as np

import concourse.bass as bass
from concourse import mybir
from concourse.alu_op_type import AluOpType as ALU

F32 = mybir.dt.float32
F32R = mybir.dt.float32r
ACT = mybir.ActivationFunctionType
AX = mybir.AxisListType.X

P = 128
D = 1024
KC = D // P
N_META, SEQ = 16, 256
T1 = N_META + SEQ
T2 = SEQ
RMS_EPS = L2_EPS = 1e-6
LN_EPS = 1e-5

GK, GV, GD = 8, 16, 128
CHUNKS = ((0, T1 % P), (T1 % P, P), (T1 % P + P, P))
NCH, HEAD_T = len(CHUNKS), T1 % P
LEVELS = [1 << s for s in range(7)]
SHORT_LAST = HEAD_T.bit_length() - 2
LAST = len(LEVELS) - 1
MH, MV = 4, 256
LN_EXP = "natural_log_exp_and_others"
SILU = "silu_and_others"
GATE_CAP = 15.0
FF = 2816
FC = FF // P
ALPHA = 4.0 ** 0.25
NEG = -1.0e30
WORK = 6720

SLOTS = 4
AHEAD = 3
BLOCK = 8 * P


class Steps:

    def __init__(self, sem, table, key):
        self.sem, self.seen = sem, 0
        self.table = table.setdefault(key, {})
        self.counted = table.get("counted", False)
        self.loop = None

    def mark(self, name):
        self.seen += 1
        base, turns = self.loop or (0, 1)
        self.table[name] = (base, self.seen, turns)
        return self.sem, 1

    def repeat(self, turns):
        return _Repeat(self, turns)

    def at(self, name, i=None):
        if not self.counted and name not in self.table:
            return self.sem, 1
        base, seen, turns = self.table[name]
        per_turn = self.table.get(("per turn", base), 0)
        if i is None:
            return self.sem, base + (turns - 1) * per_turn + seen
        return self.sem, i * per_turn + (base + seen)


class _Repeat:
    def __init__(self, steps, turns):
        self.steps, self.turns = steps, turns

    def __enter__(self):
        s = self.steps
        self.base = s.seen
        s.loop, s.seen = (self.base, self.turns), 0
        return self

    def __exit__(self, *_):
        s = self.steps
        s.table[("per turn", self.base)] = s.seen
        s.seen, s.loop = self.base + self.turns * s.seen, None


PARAMS = [
    ("norm_w", 8 * KC), ("gdn_conv", 32 * 4), ("gdn_norm", 1), ("ml_norm", 8),
    ("ffn0", 44 * 4), ("ffn1", 44 * 4), ("ev_conv", 4 * 3), ("gla_b", 2), ("gla_norm", 1),
    ("mla_qn", 2), ("mla_kvn", 1), ("ln_mix", 2 * 2 * KC), ("ln_ffn", 2 * 2 * KC), ("sinks", 8),
    ("gdn_a_log", 1), ("gdn_dt", 1), ("ml_ib", 1), ("ml_fb", 1),
    ("gdn_gates", KC * 32), ("ml_gates", KC * 8), ("g_low", KC * 16), ("gla_w", 256),
]
AT, _n = {}, 0
for _name, _cols in PARAMS:
    AT[_name] = (_n, _n + _cols)
    _n += _cols
NPARAM = _n

CONSTS = [
    ("ident", 128), ("ones", 128), ("upto", 128), ("neg_chunk", P), ("levels", len(LEVELS) * P), ("level0_t", P),
    ("swa_mask", 256), ("mla_mask", 256), ("cos", T2), ("sin", T2),
]
CAT, _n = {}, 0
for _name, _cols in CONSTS:
    CAT[_name] = (_n, _n + _cols)
    _n += _cols
NCONST = _n

PHASES = [("gdn_in", "tiles", 48), ("gdn_out", "wide", 16), ("up0", "tiles", 44), ("down0", "wide", 22),
          ("ml_in", "tiles", 24), ("ml_out", "wide", 8), ("up1", "tiles", 44), ("down1", "wide", 22),
          ("ev_in", "tiles", 18), ("ev_out", "wide", 8), ("up2", "tiles", 44), ("down2", "wide", 22),
          ("od_in", "tiles", 17), ("od_out", "wide", 8), ("up3", "tiles", 44), ("down3", "wide", 22)]
FIRST_BLOCK, _n = {}, 0
for _name, _kind, _count in PHASES:
    FIRST_BLOCK[_name] = _n
    _n += _count
NBLOCKS = _n
COUNT = {n: c for n, _, c in PHASES}


def constants():
    c = np.zeros((P, NCONST), np.float32)
    r, q = np.arange(P)[:, None], np.arange(P)[None]
    put = lambda name, a: c[:a.shape[0], CAT[name][0]:CAT[name][0] + a.shape[1]].__setitem__(slice(None), a)
    put("ident", np.eye(P, dtype=np.float32))
    put("ones", np.ones((P, P), np.float32))
    put("upto", (r <= q).astype(np.float32))
    put("neg_chunk", np.where(r <= q, 0, NEG).astype(np.float32))
    i, j = r, q
    put("levels", np.concatenate([((i // (2 * s) == j // (2 * s)) & (i // s % 2 == 1) & (j // s % 2 == 0))
                                  .astype(np.float32) for s in LEVELS], 1))
    put("level0_t", ((i % 2 == 0) & (j == i + 1)).astype(np.float32))
    same = np.where(q <= r, 0, NEG).astype(np.float32)
    put("swa_mask", np.concatenate([np.where(q > r, 0, NEG).astype(np.float32), same], 1))
    put("mla_mask", np.concatenate([0 * same, same], 1))
    freq = 10000.0 ** (-np.arange(0, 32, 2, dtype=np.float32) / 32)
    ang = (np.arange(T2, dtype=np.float32)[:, None] * freq[None]).T
    cos, sin = np.ones((96, T2), np.float32), np.zeros((96, T2), np.float32)
    cos[64:80] = cos[80:96] = np.cos(ang)
    sin[64:80], sin[80:96] = -np.sin(ang), np.sin(ang)
    put("cos", cos)
    put("sin", sin)
    return c


def tile_blocks(w):
    n = w.shape[1] // P
    return w.reshape(KC, P, n, P).transpose(2, 1, 0, 3).reshape(n, P, BLOCK)


def wide_blocks(w):
    return w.reshape(-1, P, BLOCK)


SWAP = np.r_[16:32, 0:16]


def lay_out(a):
    f = FF
    stream = []
    gw = a["gdn_w_in"][0]
    stream += [tile_blocks(gw[:, :6144]), wide_blocks(a["gdn_w_out"][0])]
    mw = a["ml_w_in"][0]

    def ffn(gate, up, down):
        both = np.stack([gate.reshape(D, FC, P), up.reshape(D, FC, P)], 2).reshape(D, 2 * f)
        return [tile_blocks(both), wide_blocks(down)]

    ev, od = a["ev_w_in_2"][0], a["od_w_in_2"][0]
    heads = np.arange(1536, 2048).reshape(8, 64)
    order = np.concatenate([np.r_[heads[t], heads[t + 4]] for t in range(4)])
    evw = np.concatenate([ev[:, :1536], ev[:, order], ev[:, 2048:]], 1)
    evo = a["ev_w_out_2"][0]
    evo = np.concatenate([evo[:512], evo[order - 1024]], 0)
    kr = od[:, 1936:1968]
    odw = np.concatenate([od[:, :1024], od[:, 1040:1936]] + [kr] * 4 + [kr[:, SWAP]] * 4, 1)
    u = a["ffn_w_up"]
    stream += ffn(u[0, :, :f], u[0, :, f:], a["ffn_w_down"][0])
    stream += [tile_blocks(mw[:, :3072]), wide_blocks(a["ml_w_out"][0])]
    stream += ffn(u[1, :, :f], u[1, :, f:], a["ffn_w_down"][1])
    stream += [tile_blocks(evw), wide_blocks(evo)]
    g2, u2, d2 = a["ffn_w_gate_2"], a["ffn_w_up_2"], a["ffn_w_down_2"]
    stream += ffn(g2[0], u2[0], d2[0])
    stream += [tile_blocks(odw), wide_blocks(a["od_w_out_2"][0])]
    stream += ffn(g2[1], u2[1], d2[1])
    stream = np.concatenate(stream, 0)
    assert stream.shape == (NBLOCKS, P, BLOCK)

    params = np.zeros((P, NPARAM), np.float32)

    def put(name, v):
        params[:v.shape[0], AT[name][0]:AT[name][1]] = v

    def per_tile(v):
        return v.reshape(v.shape[0], -1, P).transpose(2, 1, 0).reshape(P, -1)

    def rows(v):
        return v.reshape(-1, P).T

    put("norm_w", rows(a["norm_w"].reshape(8, D)))
    put("gdn_conv", per_tile(a["gdn_conv_w"][0]))
    put("gdn_norm", a["gdn_norm_w"][0][:, None])
    put("ml_norm", rows(a["ml_norm_w"]))
    for n in range(2):
        cw = np.concatenate([a["ffn_conv_w"][n], a["ffn_conv_b"][n][None]], 0)
        both = np.stack([cw[:, :f].reshape(4, FC, P), cw[:, f:].reshape(4, FC, P)], 2).reshape(4, 2 * f)
        put(f"ffn{n}", per_tile(both))
    put("ev_conv", per_tile(a["ev_conv_w_2"][0]))
    put("gla_b", rows(a["od_gla_b_gate_2"]))
    put("gla_norm", a["od_gla_norm_g_2"][0][:, None])
    put("mla_qn", rows(a["od_mla_q_norm_g_2"]))
    put("mla_kvn", rows(a["od_mla_kv_norm_g_2"]))
    for name in ("ln_mix", "ln_ffn"):
        put(name, rows(np.stack([a[name + "_g_2"], a[name + "_b_2"]], 1).reshape(4, D)))
    put("sinks", np.broadcast_to(a["ev_sinks_2"], (P, 8)))
    put("gdn_a_log", a["gdn_a_log"][0][:, None])
    put("gdn_dt", a["gdn_dt_bias"][0][:, None])
    put("ml_ib", a["ml_gate_b"][0, :4][:, None])
    put("ml_fb", a["ml_gate_b"][0, 4:][:, None])
    put("gdn_gates", gw[:, 6144:].reshape(KC, P, 32).transpose(1, 0, 2).reshape(P, -1))
    put("ml_gates", mw[:, 3072:].reshape(KC, P, 8).transpose(1, 0, 2).reshape(P, -1))
    put("g_low", od[:, 1024:1040].reshape(KC, P, 16).transpose(1, 0, 2).reshape(P, -1))
    put("gla_w", a["od_gla_w_gate_2"][0])

    uq = a["od_mla_w_uq_2"][0]
    swapped = uq.reshape(256, 4, 96)[:, :, np.r_[0:64, 64 + SWAP]].reshape(256, 384)
    ukv = a["od_mla_w_ukv_2"][0].reshape(P, 4, 192)
    mla = np.concatenate([uq.reshape(2, P, 384).transpose(1, 0, 2).reshape(P, -1),
                          swapped.reshape(2, P, 384).transpose(1, 0, 2).reshape(P, -1),
                          ukv[:, :, :64].reshape(P, 256), ukv[:, :, 64:].reshape(P, 512)], 1)
    hs = np.concatenate([a["meta_tokens"], a["x"][0]], 0).T.reshape(KC, P, T1).transpose(1, 0, 2)
    return {name: np.ascontiguousarray(v) for name, v in dict(
        stream=stream, params=params, consts=constants(), mla=mla, hs=hs.reshape(P, -1)).items()}


SHAPES = dict(stream=(NBLOCKS, P, BLOCK), params=(P, NPARAM), consts=(P, NCONST), mla=(P, 2304),
              hs=(P, KC * T1))


def build(nc, stream, params, consts, mla, hs_in, out, table):
    ctx = ExitStack()

    def sb(name, shape):
        return ctx.enter_context(nc.sbuf_tensor(name, shape, F32))

    def sem(name):
        return ctx.enter_context(nc.semaphore(name))

    def shared(name, shape, other, other_shape):
        with nc.sbuf_tensor(name, shape, F32) as first:
            pass
        return first, ctx.enter_context(nc.sbuf_tensor(other, other_shape, F32R))

    raw = sb("raw", [P, SLOTS, BLOCK])
    whi = ctx.enter_context(nc.sbuf_tensor("whi", [P, SLOTS, BLOCK], F32R))
    wlo = ctx.enter_context(nc.sbuf_tensor("wlo", [P, SLOTS, BLOCK], F32R))
    par = sb("par", [P, NPARAM])
    con = sb("con", [P, NCONST])
    hs = sb("hs_sb", [P, KC, T1])
    xf, xs = shared("xf", [P, 2 * KC, T1], "xs", [P, 2 * KC, T1])
    y = sb("y", [P, KC, T1])
    sq = sb("sq", [P, KC, T1])
    rs = sb("rs", [P, 2, T1])
    big, hf = shared("big", [P, 48, T1], "hf", [P, 48, T1])
    mix = sb("mix", [P, KC, T1])
    cv = sb("cv", [P, 8, T1])
    work = sb("work", [P, WORK])
    bank = [ctx.enter_context(nc.psum_tensor(f"bank{i}", [P, 512], F32)) for i in range(8)]

    def pv(name, k=0, n=1, rows=P):
        lo = AT[name][0] + k
        return par[0:rows, lo:lo + n]

    def cn(name, rows=P, lo=0, cols=None):
        a, b = CAT[name]
        return con[0:rows, a + lo:a + lo + cols if cols else b]

    ones, ident = cn("ones"), cn("ident")

    loaded = sem("loaded")
    hs_loaded = sem("hs_loaded")
    mla_loaded = sem("mla_loaded")
    block_loaded = [sem(f"block_loaded{s}") for s in range(SLOTS)]
    hi_split = sem("hi_split")
    block_split = sem("block_split")
    block_used = sem("block_used")
    bank_free = sem("bank_free")
    conv_taken = sem("conv_taken")
    stored = sem("stored")

    steps = {}

    def S(phase, engine):
        key = f"{phase}_{engine}"
        if key not in steps:
            steps[key] = Steps(sem(key), table, key)
        return steps[key]

    def sp_stream(sp):
        sp.dma_start(hs[:, :, :], hs_in.rearrange("p (c t) -> p c t", t=T1)).then_inc(hs_loaded, 16)
        sp.dma_start(con[:, :], consts).then_inc(loaded, 16)
        sp.dma_start(par[:, :], params).then_inc(loaded, 16)
        for s in range(SLOTS):
            sp.dma_start(raw[:, s, :], stream[s]).then_inc(block_loaded[s], 16)
        rounds = NBLOCKS // SLOTS
        with sp.Fori(0, rounds - 1) as r:
            for s in range(SLOTS):
                sp.wait_ge(block_split, r * SLOTS + (s + 1))
                sp.dma_start(raw[:, s, :], stream[(r + 1) * SLOTS + s]).then_inc(block_loaded[s], 16)
        for n in range(rounds * SLOTS, NBLOCKS):
            sp.wait_ge(block_split, n - SLOTS + 1)
            sp.dma_start(raw[:, n % SLOTS, :], stream[n]).then_inc(block_loaded[n % SLOTS], 16)

    def split_hi(act, n, i=0):
        s = n % SLOTS
        act.wait_ge(block_loaded[s], i * (16 * 8 // SLOTS) + 16 * (n // SLOTS + 1))
        if n >= SLOTS:
            act.wait_ge(block_used, i * 8 + (n - SLOTS + 1))
        nc.scalar.activation(whi[:, s, :], raw[:, s, :], ACT.Copy).then_inc(hi_split, 1)

    def split_lo(dve, n, i=0):
        s = n % SLOTS
        dve.wait_ge(hi_split, i * 8 + (n + 1))
        nc.vector.tensor_tensor(wlo[:, s, :], raw[:, s, :], whi[:, s, :].bitcast(F32), ALU.subtract).then_inc(block_split, 1)

    def split_all(engine, split, phase, lo=0, count=None):
        b0 = FIRST_BLOCK[phase] + AHEAD + lo
        n = min(count or COUNT[phase] - lo, NBLOCKS - b0)
        if n >= 16:
            with engine.Fori(0, n // 8) as i:
                for j in range(8):
                    split(engine, b0 + j, i)
        for j in range(n // 8 * 8 if n >= 16 else 0, n):
            split(engine, b0 + j)

    POOL_CHUNKS = (0, 2, 4)

    def lo_done(name, m):
        return S("norm", "pool" if m in POOL_CHUNKS else "dve").at(f"{name}_lo{m}")

    def added(name, m):
        return S("norm", "pool" if m in POOL_CHUNKS else "dve").at(f"{name}_h{m}")

    def x_lo(engine, ops, who, name, src, T, chunks):
        for m in chunks:
            engine.wait_ge(*S("norm", "act").at(f"{name}_hi{m}"))
            ops.tensor_tensor(xs[:, KC + m, 0:T], src(m), xs[:, m, 0:T].bitcast(F32), ALU.subtract
                              ).then_inc(*S("norm", who).mark(f"{name}_lo{m}"))

    DVE_CHUNKS = [m for m in range(KC) if m not in POOL_CHUNKS]

    def three(out_, slot, c, hi, lo, start, stop):
        w = slice(c * P, (c + 1) * P)
        nc.tensor.matmul(out_, whi[:, slot, w], hi, start=start, stop=False)
        nc.tensor.matmul(out_, whi[:, slot, w], lo, start=False, stop=False)
        return nc.tensor.matmul(out_, wlo[:, slot, w], hi, start=False, stop=stop)

    def pe_tiles(pe, phase, g0, name):
        b0, n = FIRST_BLOCK[phase], COUNT[phase]
        T = T1 if b0 < FIRST_BLOCK["ev_in"] else T2

        def tile(j, i=0):
            g = g0 + j
            pe.wait_ge(block_split, i * 8 + (b0 + j + 1))
            pe.wait_ge(bank_free, i * 8 + (g + 1))
            for k in range(KC):
                if j == 0:
                    pe.wait_ge(*lo_done(name, k))
                last = three(rhs_out(g, phase), (b0 + j) % SLOTS, k, xs[:, k, 0:T], xs[:, KC + k, 0:T], k == 0, k == KC - 1)
            last.then_inc(block_used, 1)

        tile(0)
        turns = (n - 1) // 8
        with pe.Fori(0, turns) as i:
            for j in range(1, 9):
                tile(j, i)
        for j in range(turns * 8 + 1, n):
            tile(j)

    def rhs_out(g, phase):
        return bank[g % 8][:, 0:T1 if FIRST_BLOCK[phase] < FIRST_BLOCK["ev_in"] else T2]

    def pe_wide(pe, phase, g0, ready):
        b0, n = FIRST_BLOCK[phase], COUNT[phase]
        T = T1 if b0 < FIRST_BLOCK["ev_in"] else T2
        def rows(k, i=None):
            at = k if i is None else i * 8 + k
            lo = n + k if i is None else i * 8 + (n + k)
            pe.wait_ge(block_split, (0 if i is None else i * 8) + (b0 + k + 1))
            ready(pe, k, i)
            for m in range(8):
                if k == 0 and i is None:
                    pe.wait_ge(bank_free, g0 + m + 1)
                last = three(rhs_out(g0 + m, phase), (b0 + k) % SLOTS, m, hf[:, at, 0:T], hf[:, lo, 0:T], k == 0, k == n - 1)
            last.then_inc(block_used, 1)

        if n == 22:
            rows(0)
            with pe.Fori(0, 2) as i:
                for k in range(1, 9):
                    rows(k, i)
            for k in range(17, 22):
                rows(k)
        else:
            for k in range(n):
                rows(k)


    def pe_sum(pe, name, g, src, T):
        pe.wait_ge(bank_free, g + 1)
        for m in range(KC):
            pe.wait_ge(*S("norm", "act").at(f"{name}_{m}"))
            last = nc.tensor.matmul(bank[g % 8][:, 0:T], ones, src(m), start=(m == 0), stop=(m == KC - 1))
        last.then_inc(*S("norm", "pe").mark(name))

    def act_scale(act, name, g, dst, T, count, eps):
        act.wait_ge(*S("norm", "pe").at(name))
        nc.scalar.activation(dst, bank[g % 8][:, 0:T], ACT.Ln, bias=eps, scale=1.0 / count).then_inc(bank_free, 1)
        act.wait_ge(bank_free, 8 + g + 1)
        nc.scalar.activation(dst, dst, ACT.Exp, scale=-0.5).then_inc(*S("norm", "act").mark(f"{name}_scale"))

    def pre_pe(pe, name, g):
        pe_sum(pe, name, g, lambda m: sq[:, m, :], T1)

    def pre_act(act, name, g, ready, meanwhile=lambda: None):
        for m in range(KC):
            ready(act, m)
            nc.scalar.activation(sq[:, m, :], hs[:, m, :], ACT.Square).then_inc(*S("norm", "act").mark(f"{name}_{m}"))
        meanwhile()
        act_scale(act, name, g, rs[:, 0, :], T1, D, eps_1)
        pre_act_hi(act, name)

    def pre_dve(dve, name, row, after=None):
        st, a_ = S("norm", "dve"), S("norm", "act")
        dve.wait_ge(*a_.at(f"{name}_scale"))
        for m in range(KC):
            if after and m in POOL_CHUNKS:
                dve.wait_ge(*added(after, m))
            nc.vector.scalar_tensor_tensor(y[:, m, :], hs[:, m, :], pv("norm_w", row * KC + m), rs[:, 0, :],
                                           ALU.mult, ALU.mult).then_inc(*st.mark(f"{name}_x{m}"))
        x_lo(dve, nc.vector, "dve", name, lambda m: y[:, m, :], T1, DVE_CHUNKS)

    def pre_pool(pool, name):
        x_lo(pool, nc.gpsimd, "pool", name, lambda m: y[:, m, :], T1, POOL_CHUNKS)

    def pre_act_hi(act, name):
        for m in range(KC):
            act.wait_ge(*S("norm", "dve").at(f"{name}_x{m}"))
            nc.scalar.activation(xs[:, m, :], y[:, m, :], ACT.Copy).then_inc(*S("norm", "act").mark(f"{name}_hi{m}"))

    def mix_act(act, name, src, n, ready):
        ready(act)
        for k in range(n):
            nc.scalar.activation(hf[:, k, 0:src(k).shape[1]], src(k), ACT.Copy).then_inc(*S("norm", "act").mark(f"{name}_hi{k}"))

    def mix_dve(dve, name, src, n, ready):
        ready(dve)
        for k in range(n):
            T = src(k).shape[1]
            dve.wait_ge(*S("norm", "act").at(f"{name}_hi{k}"))
            nc.vector.tensor_tensor(hf[:, n + k, 0:T], src(k), hf[:, k, 0:T].bitcast(F32), ALU.subtract
                                    ).then_inc(*S("norm", "dve").mark(f"{name}_lo{k}"))

    def post_pe(pe, name, g):
        pe_sum(pe, name, g, lambda m: sq[:, m, :], T1)

    def post_act(act, name, g):
        for m in range(KC):
            act.wait_ge(bank_free, 8 + g - 8 + m + 1)
            nc.scalar.activation(sq[:, m, :], y[:, m, :], ACT.Square).then_inc(*S("norm", "act").mark(f"{name}_{m}"))
        act_scale(act, name, g, rs[:, 1, :], T1, D, eps_1)

    def post_dve(dve, name, g, row, last_block):
        for m in range(KC):
            if m == 0:
                dve.wait_ge(block_used, last_block)
            nc.vector.tensor_copy(y[:, m, :], bank[(g - 8 + m) % 8][:, 0:T1]).then_inc(bank_free, 1)
        dve.wait_ge(*S("norm", "act").at(f"{name}_scale"))
        for m in range(KC):
            nc.vector.scalar_tensor_tensor(y[:, m, :], y[:, m, :], pv("norm_w", row * KC + m), rs[:, 1, :],
                                           ALU.mult, ALU.mult).then_inc(*S("norm", "dve").mark(f"{name}_y{m}"))
        add_y(dve, nc.vector, "dve", name, DVE_CHUNKS)

    def add_y(engine, ops, who, name, chunks):
        for m in chunks:
            engine.wait_ge(*S("norm", "dve").at(f"{name}_y{m}"))
            ops.tensor_tensor(hs[:, m, :], hs[:, m, :], y[:, m, :], ALU.add).then_inc(*S("norm", who).mark(f"{name}_h{m}"))

    def post_pool(pool, name):
        add_y(pool, nc.gpsimd, "pool", name, POOL_CHUNKS)

    def conv_first(steps_, tag, tiles, taps, bias):
        for a, (bk, slot, w) in enumerate(tiles):
            args = dict(scale=w[:, taps - 1:taps])
            if bias:
                args["bias"] = w[:, taps:taps + 1]
            nc.scalar.activation(cv[:, slot, :], bk[:, 0:T1], ACT.Identity, **args).then_inc(*steps_.mark(f"{tag}{a}"))

    def conv_rest(dve, steps_, first, tag, tiles, i, taps):
        for tap in range(1, taps):
            for a, (bk, slot, w) in enumerate(tiles):
                o = cv[:, slot, :]
                dve.wait_ge(*(first.at(f"{tag}{a}", i) if tap == 1 else steps_.at(f"{tag}_{tap - 1}{a}", i)))
                ins = nc.vector.scalar_tensor_tensor(o[:, tap:T1], bk[:, 0:T1 - tap], w[:, taps - 1 - tap:taps - tap],
                                                     o[:, tap:T1], ALU.mult, ALU.add)
                if tap == taps - 1 and a == 1:
                    ins.then_inc(bank_free, 2)
                else:
                    ins.then_inc(*steps_.mark(f"{tag}_{tap}{a}"))

    CONV0, _c = {}, 0
    for name, n in (("gdn_in", 32), ("up0", 44), ("up1", 44), ("up2", 44), ("up3", 44)):
        CONV0[name] = _c
        _c += n

    def pairs(engine, pair, steps_=None):
        with ExitStack() as loop:
            i = loop.enter_context(engine.Fori(0, 5))
            if steps_:
                loop.enter_context(steps_.repeat(5))
            for j in range(4):
                pair(j, i, 0)
        for j in range(2):
            pair(j, None, 40)

    def ffn_tiles(f, g0, j, i, base):
        t = 2 * j + base
        if f < 2:
            lo = AT[f"ffn{f}"][0]
            W = par[:, lo:lo + 176].rearrange("p (t k) -> p t k", k=4)
            w = [W[:, i * 8 + (t + a) if i is not None else t + a, :] for a in range(2)]
        else:
            w = [None] * 2
        return [(bank[(g0 + t + a) % 8], 2 * j + a, w[a]) for a in range(2)]

    def ffn_act(act, f, g0):
        st, b0, c0 = S("ffn", "act"), FIRST_BLOCK[f"up{f}"], CONV0[f"up{f}"]

        def pair(j, i, base):
            t, ii = base + 2 * j, 0 if i is None else i
            tiles = ffn_tiles(f, g0, j, i, base)
            split_hi(act, b0 + t + AHEAD, ii)
            split_hi(act, b0 + t + AHEAD + 1, ii)
            act.wait_ge(block_used, ii * 8 + (b0 + t + 2))
            act.wait_ge(conv_taken, ii * 8 + (c0 + t + 2))
            if f < 2:
                conv_first(st, f"f{f}_{base}_{j}", tiles, 3, True)
                act.wait_ge(bank_free, ii * 8 + (8 + g0 + t + 2))
                o = cv[:, 2 * j, :]
                nc.scalar.activation(o, o, ACT.Silu).then_inc(*st.mark(f"silu{f}_{base}_{j}"))
            else:
                nc.scalar.activation(cv[:, 2 * j, 0:T2], tiles[0][0][:, 0:T2], ACT.Silu).then_inc(*st.mark(f"silu{f}_{base}_{j}"))

        pairs(act, pair, st)

    def ffn_dve(dve, f, g0):
        st, b0 = S("ffn", "dve"), FIRST_BLOCK[f"up{f}"]

        def pair(j, i, base):
            t, ii = base + 2 * j, 0 if i is None else i
            tiles = ffn_tiles(f, g0, j, i, base)
            split_lo(dve, b0 + t + AHEAD, ii)
            split_lo(dve, b0 + t + AHEAD + 1, ii)
            if f < 2:
                conv_rest(dve, st, S("ffn", "act"), f"f{f}_{base}_{j}", tiles, i, 3)
            else:
                dve.wait_ge(*S("ffn", "act").at(f"silu{f}_{base}_{j}", i))
                nc.vector.tensor_tensor(cv[:, 2 * j + 1, 0:T2], cv[:, 2 * j, 0:T2], tiles[1][0][:, 0:T2], ALU.mult).then_inc(bank_free, 2)

        pairs(dve, pair, st)

    def ffn_pool(pool, f, g0):
        st, T = S("ffn", "pool"), T1 if f < 2 else T2

        def pair(j, i, base):
            ii = 0 if i is None else i
            k = base // 2 + j
            h = cv[:, 2 * j + 1, 0:T]
            hi = hf[:, k if i is None else i * 4 + k, 0:T]
            lo = hf[:, FC + k if i is None else i * 4 + (FC + k), 0:T]
            if f < 2:
                pool.wait_ge(*S("ffn", "act").at(f"silu{f}_{base}_{j}", i))
                nc.gpsimd.tensor_tensor(h, cv[:, 2 * j, 0:T], h, ALU.mult).then_inc(*st.mark(f"h{f}_{base}_{j}"))
                pool.wait_ge(*st.at(f"h{f}_{base}_{j}", i))
            else:
                pool.wait_ge(bank_free, ii * 8 + (8 + g0 + base + 2 * j + 2))
            nc.gpsimd.tensor_copy(hi, h).then_inc(*st.mark(f"hi{f}_{base}_{j}"))
            pool.wait_ge(*st.at(f"hi{f}_{base}_{j}", i))
            nc.gpsimd.tensor_tensor(lo, h, hi.bitcast(F32), ALU.subtract).then_inc(conv_taken, 2)

        pairs(pool, pair, st)

    def ffn_ready(f):
        def ready(pe, k, i):
            c = 8 + CONV0[f"up{f}"] + 2 * (k + 1)
            pe.wait_ge(conv_taken, c if i is None else i * 16 + c)
        return ready

    G, _g = {}, 0
    for name, n in (("pre0", 1), ("gdn_g", 2), ("gdn_in", 48), ("gdn_out", 8), ("post0", 1), ("pre1", 1), ("up0", 44), ("down0", 8),
                    ("post1", 1), ("pre2", 1), ("ml_g", 2), ("ml_in", 24), ("ml_out", 8), ("post2", 1), ("pre3", 1), ("up1", 44),
                    ("down1", 8), ("post3", 1),
                    ("ev_in", 18), ("ev_out", 8), ("lm0", 1), ("lv0", 1), ("up2", 44), ("down2", 8), ("lm1", 1), ("lv1", 1),
                    ("od_g", 1), ("od_in", 17), ("od_out", 8), ("lm2", 1), ("lv2", 1), ("up3", 44), ("down3", 8), ("lm3", 1), ("lv3", 1)):
        G[name] = _g
        _g += n

    def used_after(phase):
        return FIRST_BLOCK[phase] + COUNT[phase]

    at = lambda ap, c: ap[:, CHUNKS[c][0]:CHUNKS[c][0] + CHUNKS[c][1]]
    own = lambda ap, c: ap[0:CHUNKS[c][1]]
    fulls = lambda ap: ap.rearrange("p (c t) -> p c t", t=P)
    fc = lambda ap: fulls(ap[:, HEAD_T:T1])
    wk = lambda lo, n: work[:, lo:lo + n]
    VH = range(4)
    TT, UU, X1, EG = ([xf[:, 4 * s + a, :] for a in VH] for s in range(4))
    AT_, att = ([y[:, 4 * s + a, :] for a in VH] for s in range(2))
    selG, selb = TT, X1
    U1, U2 = TT, X1
    qd = [sq[:, a, :] for a in VH]
    qn, kn = ([sq[:, 4 + 2 * s + k, :] for k in range(2)] for s in range(2))
    kk, kq, qss, kss = ([cv[:, 2 * s + k, :] for k in range(2)] for s in range(4))
    vtok = [mix[:, 0:6, :].rearrange("p a b -> p (a b)")[:, a * NCH * P:(a + 1) * NCH * P] for a in VH]
    ktok = [wk(k * NCH * P, NCH * P) for k in range(2)]
    vnew, vdec, state = ([wk(768 + 512 * s + a * P, P) for a in VH] for s in range(3))
    vst = [wk(2304 + a * T1, T1) for a in VH]
    tok = lambda n: wk(3392 + n * NCH * GV, NCH * GV).rearrange("p (c h) -> p c h", c=NCH)
    g_tok, b_tok, G_tok, nbe_tok, el_tok = (tok(n) for n in range(5))
    b_row, u_row, t_row, G_row, ea = (wk(3632 + n * T1, T1)[0:GV] for n in range(5))
    short = lambda n: wk(4992 + n * 4 * HEAD_T, 4 * HEAD_T)[0:HEAD_T].rearrange("p (a t) -> p a t", a=4)
    sT, sU, sX, sU1, sU2 = (short(n) for n in range(5))
    at_chunk = lambda ap, c: ap[:, c * P:(c + 1) * P]
    VBANK = ((6, 7), (4, 5), (0, 1), (2, 3))
    SB, SB2 = (bank[b][0:HEAD_T, 2 * P:2 * P + 4 * HEAD_T].rearrange("p (a t) -> p a t", a=4) for b in VBANK[3])
    odd = lambda ap, size: ap.rearrange("p (b two s) -> p b two s", two=2, s=size)[:, :, 1, :]
    head = lambda ap, h: ap.rearrange("p c (h o) -> p c h o", o=1)[:, :, h, :]
    EYE = cn("ident").rearrange("p (n o) -> p n o", o=1)

    U1c = lambda a, c: at_chunk(U1[a], c - 1) if c else sU1[:, a, :]
    U2c = lambda a, c: at_chunk(U2[a], c - 1) if c else sU2[:, a, :]

    over_c = lambda ap, n: ap.unsqueeze(1).to_broadcast([ap.shape[0], n, ap.shape[1]])

    def gates_pe(pe, name, g, cols, base, width, T, rhs, ready):
        w = pv(base, 0, KC * width).rearrange("p (k n) -> p k n", k=KC)
        for n, (lo, m) in enumerate(cols):
            pe.wait_ge(bank_free, g + n + 1)
            for k in range(KC):
                if n == 0:
                    pe.wait_ge(*ready(k))
                last = nc.tensor.matmul(bank[(g + n) % 8][0:m, 0:T], w[:, k, lo:lo + m], rhs(k), start=(k == 0), stop=(k == KC - 1))
            last.then_inc(*S("gates", "pe").mark(f"{name}{n}"))

    def gdn_gates_act(act):
        g = G["gdn_g"]
        act.wait_ge(*S("gates", "pe").at("gdn0"))
        nc.scalar.activation(b_row, bank[g % 8][0:GV, 0:T1], ACT.Sigmoid).then_inc(bank_free, 1)
        act.wait_ge(*S("gates", "pe").at("gdn1"))
        nc.scalar.activation(u_row, bank[(g + 1) % 8][0:GV, 0:T1], ACT.Identity, bias=pv("gdn_dt", rows=GV)).then_inc(bank_free, 1)

    def gdn_in_tiles(j, i):
        lo = AT["gdn_conv"][0]
        W = par[:, lo:lo + 128].rearrange("p (t k) -> p t k", k=4)
        return [(bank[(G["gdn_in"] + 2 * j + a) % 8], 2 * j + a, W[:, i * 8 + (2 * j + a), :]) for a in range(2)]

    def gdn_in_dve(dve):
        st, g0, b0 = S("gin", "dve"), G["gdn_in"], FIRST_BLOCK["gdn_in"]
        dve.wait_ge(bank_free, 8 + g0)
        with dve.Fori(0, 4) as i, st.repeat(4):
            for j in range(4):
                split_lo(dve, b0 + 2 * j + AHEAD, i)
                conv_rest(dve, st, S("gin", "act"), f"c{j}", gdn_in_tiles(j, i), i, 4)
                split_lo(dve, b0 + 2 * j + AHEAD + 1, i)
        split_all(dve, split_lo, "gdn_in", 32)

    def gdn_in_act(act):
        st, g0, b0, c0 = S("gin", "act"), G["gdn_in"], FIRST_BLOCK["gdn_in"], CONV0["gdn_in"]
        with act.Fori(0, 4) as i, st.repeat(4):
            for j in range(4):
                split_hi(act, b0 + 2 * j + AHEAD, i)
                act.wait_ge(block_used, i * 8 + (b0 + 2 * j + 2))
                act.wait_ge(conv_taken, i * 8 + (c0 + 2 * j + 2))
                conv_first(st, f"c{j}", gdn_in_tiles(j, i), 4, False)
                split_hi(act, b0 + 2 * j + AHEAD + 1, i)
                act.wait_ge(bank_free, i * 8 + (8 + g0 + 2 * j + 2))
                for a in range(2):
                    nc.scalar.activation(big[:, i * 8 + (2 * j + a), :], cv[:, 2 * j + a, :], ACT.Silu).then_inc(conv_taken, 1)
        with act.Fori(0, 2) as i:
            for j in range(8):
                split_hi(act, b0 + 32 + j + AHEAD, i)
                act.wait_ge(block_used, i * 8 + (b0 + 32 + j + 1))
                nc.scalar.activation(big[:, i * 8 + (32 + j), :], bank[(g0 + 32 + j) % 8][:, 0:T1], ACT.Silu).then_inc(bank_free, 1)

    def gdn_pe(pe):
        m, v, a_ = S("gdn", "pe"), S("gdn", "dve"), S("gdn", "act")
        pl = S("gdn", "pool")
        mm = nc.tensor.matmul
        pe.wait_ge(bank_free, 8 + G["gdn_out"])
        pe.wait_ge(*v.at("g_row"))
        rows_of = lambda c: slice(CHUNKS[c][0], CHUNKS[c][0] + P)
        for c in range(NCH):
            nc.tensor.transpose(bank[0][:, c * GV:(c + 1) * GV], t_row[:, rows_of(c)], ident[0:GV, 0:GV])
        for c in range(NCH):
            last = nc.tensor.transpose(bank[1][:, c * GV:(c + 1) * GV], b_row[:, rows_of(c)], ident[0:GV, 0:GV])
        last.then_inc(*m.mark("to_tok"))
        pe.wait_ge(*v.at("g_tok"))
        upto = cn("upto")
        for c, (lo, n) in enumerate(CHUNKS):
            g_c = g_tok[0:n, c, :]
            mm(bank[2][0:GV, lo:lo + n], g_c, upto[0:n, 0:n], start=True, stop=True)
            mm(bank[3][:, c * GV:(c + 1) * GV], upto[0:n, :], g_c, start=True, stop=True)
            last = mm(bank[4][:, c * GV:(c + 1) * GV], ones[0:n, :], g_c, start=True, stop=True)
        last.then_inc(*m.mark("sums"))

        pe.wait_ge(*v.at("el_tok"))
        with pe.Fori(0, GK // 2) as i, m.repeat(GK // 2):
            for k in range(2):
                pe.wait_ge(*pl.at(f"squares{k}", i))
                mm(bank[2 * k][:, 0:T1], ones, qss[k], start=True, stop=True)
                mm(bank[2 * k + 1][:, 0:T1], ones, kss[k], start=True, stop=True).then_inc(*m.mark(f"norms{k}"))
            for a in VH:
                pe.wait_ge(*pl.at(f"vst{a}", i))
                for c in range(NCH):
                    last = nc.tensor.transpose(own(at_chunk(bank[4 + a], c), c), at(vst[a], c), ident)
                last.then_inc(*m.mark(f"vtok{a}"))
            for k in range(2):
                pe.wait_ge(*v.at(f"kn{k}", i))
                for dst, other in ((2 * k, kn[k]), (2 * k + 1, qn[k])):
                    for c in range(NCH):
                        last = mm(at(bank[dst], c), kn[k][:, rows_of(c)], at(other, c), start=True, stop=True)
                last.then_inc(*m.mark(f"kk{k}"))
                pe.wait_ge(*a_.at(f"vtok{k}", i))
                for c in range(NCH):
                    last = nc.tensor.transpose(own(at_chunk(bank[4 + k], c), c), at(kn[k], c), ident)
                last.then_inc(*m.mark(f"ktok{k}"))
            for a in VH:
                pe.wait_ge(*v.at(f"sel{a}", i))
                pe.wait_ge(*a_.at(("vtok3", "ktok1", "kq0", "kq1")[a], i))
                mm(bank[VBANK[a][0]][:, 0:T1], ones[0:16, :], selG[a][0:16, :], start=True, stop=True)
                mm(bank[VBANK[a][1]][:, 0:T1], ones[0:16, :], selb[a][0:16, :], start=True, stop=True).then_inc(*m.mark(f"rows{a}"))
            for l in range(LAST + 1):
                with_short = lambda a, last: a == 3 and l <= last
                for a in VH if l else ():
                    pe.wait_ge(*a_.at(f"sT_{l - 1}" if with_short(a, SHORT_LAST) else f"T{a}_{l - 1}", i))
                    for c in range(2):
                        last = mm(at_chunk(bank[VBANK[a][0]], c), at(AT_[a], c + 1), at_chunk(TT[a], c), start=True, stop=True)
                    for b in VH if with_short(a, SHORT_LAST) else ():
                        last = mm(SB[:, b, :], AT_[b][0:HEAD_T, 0:HEAD_T], sT[:, b, :], start=True, stop=True)
                    last.then_inc(*m.mark(f"X{a}_{l}"))
                for a in VH if l else ():
                    pe.wait_ge(*v.at(f"sX_{l}" if with_short(a, SHORT_LAST) else f"X{a}_{l}", i))
                    for c in range(2):
                        last = mm(at_chunk(bank[VBANK[a][1]], c), at_chunk(X1[a], c), at_chunk(UU[a], c), start=True, stop=True)
                    for b in VH if with_short(a, SHORT_LAST) else ():
                        last = mm(SB2[:, b, :], sX[:, b, :], sU[:, b, :], start=True, stop=True)
                    last.then_inc(*m.mark(f"Y{a}_{l}"))
                for a in VH if l < LAST else ():
                    if l == 0:
                        pe.wait_ge(*v.at(f"U{a}_0", i))
                        if a == 3:
                            pe.wait_ge(*pl.at("sU_0", i))
                        pe.wait_ge(*a_.at(f"EG{a}", i))
                    else:
                        pe.wait_ge(*v.at(f"sU_{l}" if with_short(a, SHORT_LAST) else f"U{a}_{l}", i))
                    for c in range(2):
                        last = nc.tensor.transpose(at_chunk(bank[VBANK[a][0]], c), at_chunk(UU[a], c), ident)
                    for b in VH if with_short(a, SHORT_LAST - 1) else ():
                        last = nc.tensor.transpose(SB[:, b, :], sU[:, b, :], ident[0:HEAD_T, 0:HEAD_T])
                    last.then_inc(*m.mark(f"T{a}_{l}"))
            for a in VH:
                pe.wait_ge(*v.at(f"U1{a}", i))
                for c in range(NCH):
                    last = mm(at(bank[VBANK[a][1]], c), own(at_chunk(ktok[a // 2], c), c), U2c(a, c), start=True, stop=True)
                last.then_inc(*m.mark(f"w{a}"))
            for c in range(NCH):
                for a in VH:
                    bv, bo = VBANK[a]
                    if c > 0:
                        pe.wait_ge(*v.at(f"S{a}_{c - 1}", i))
                        mm(at(bank[bo], c), state[a], at(qd[a], c), start=True, stop=False)
                    last = mm(own(bank[bv], c)[:, 0:P], U1c(a, c), own(at_chunk(vtok[a], c), c), start=True, stop=(c == 0))
                    if c > 0:
                        last = mm(own(bank[bv], c)[:, 0:P], at(AT_[a], c), state[a], start=False, stop=True)
                    last.then_inc(*m.mark(f"v{a}_{c}"))
                for a in VH:
                    bv, bo = VBANK[a]
                    pe.wait_ge(*a_.at(f"v{a}_{c}", i))
                    if c == 0:
                        pe.wait_ge(*pl.at(f"qd{a}", i))
                    mm(at(bank[bo], c), own(vnew[a], c), own(at(att[a], c), c), start=(c == 0), stop=True).then_inc(*m.mark(f"o{a}_{c}"))
                    if c < NCH - 1:
                        pe.wait_ge(*pl.at(f"d{a}_{c}", i))
                        mm(bank[bv][:, P:2 * P], own(at_chunk(ktok[a // 2], c), c), own(vdec[a], c), start=True, stop=True
                           ).then_inc(*m.mark(f"s{a}_{c}"))
            for a in VH:
                pe.wait_ge(*a_.at(f"osq{a}", i))
                mm(bank[VBANK[a][0]][:, 0:T1], ones, UU[a], start=True, stop=True).then_inc(*m.mark(f"on{a}"))
            pe.wait_ge(*v.at("on3", i))

    def gdn_act(act):
        m, v, a_, pl = S("gdn", "pe"), S("gdn", "dve"), S("gdn", "act"), S("gdn", "pool")
        A = nc.scalar.activation
        act.wait_ge(bank_free, 8 + G["gdn_g"] + 2)
        A(t_row, u_row, ACT.Abs).then_inc(*a_.mark("abs"))
        act.wait_ge(*a_.at("abs"))
        A(t_row, t_row, ACT.Exp, scale=-1.0).then_inc(*a_.mark("e"))
        A(ea[:, 0:1], pv("gdn_a_log", rows=GV), ACT.Exp).then_inc(*a_.mark("ea"))
        act.wait_ge(*a_.at("e"))
        A(t_row, t_row, ACT.Ln, bias=1.0).then_inc(*a_.mark("softplus"))
        act.wait_ge(*m.at("to_tok"))
        A(g_tok.rearrange("p c h -> p (c h)"), bank[0][:, 0:NCH * GV], ACT.Copy).then_inc(*a_.mark("g_tok"))
        A(b_tok.rearrange("p c h -> p (c h)"), bank[1][:, 0:NCH * GV], ACT.Copy).then_inc(*a_.mark("b_tok"))
        act.wait_ge(*v.at("G_tok"))
        act.wait_ge(*v.at("el_tok"))
        flat = lambda ap: ap.rearrange("p c h -> p (c h)")
        A(flat(nbe_tok), flat(G_tok), ACT.Exp).then_inc(*a_.mark("eG"))
        A(flat(el_tok), flat(el_tok), ACT.Exp).then_inc(*a_.mark("el"))
        with act.Fori(0, GK // 2) as i, a_.repeat(GK // 2):
            for k in range(2):
                act.wait_ge(*m.at(f"norms{k}", i))
                A(qss[k], bank[2 * k][:, 0:T1], ACT.Ln, scale=float(GD), bias=eps_q).then_inc(*a_.mark(f"lq{k}"))
                A(kss[k], bank[2 * k + 1][:, 0:T1], ACT.Ln, bias=eps_1).then_inc(*a_.mark(f"lk{k}"))
                act.wait_ge(*a_.at(f"lq{k}", i))
                A(qss[k], qss[k], ACT.Exp, scale=-0.5).then_inc(*a_.mark(f"rq{k}"))
                act.wait_ge(*a_.at(f"lk{k}", i))
                A(kss[k], kss[k], ACT.Exp, scale=-0.5).then_inc(*a_.mark(f"rk{k}"))
            for a in VH:
                act.wait_ge(*m.at(f"vtok{a}", i))
                A(vtok[a][0:HEAD_T, 0:P], bank[4 + a][0:HEAD_T, 0:P], ACT.Copy).then_inc(*a_.mark(f"vtok_s{a}"))
                A(vtok[a][:, P:NCH * P], bank[4 + a][:, P:NCH * P], ACT.Copy).then_inc(*a_.mark(f"vtok{a}"))
            for k in range(2):
                act.wait_ge(*m.at(f"kk{k}", i))
                A(kk[k], bank[2 * k][:, 0:T1], ACT.Copy).then_inc(*a_.mark(f"kk{k}"))
                A(kq[k], bank[2 * k + 1][:, 0:T1], ACT.Copy).then_inc(*a_.mark(f"kq{k}"))
                act.wait_ge(*m.at(f"ktok{k}", i))
                A(ktok[k][0:HEAD_T, 0:P], bank[4 + k][0:HEAD_T, 0:P], ACT.Copy).then_inc(*a_.mark(f"ktok_s{k}"))
                A(ktok[k][:, P:NCH * P], bank[4 + k][:, P:NCH * P], ACT.Copy).then_inc(*a_.mark(f"ktok{k}"))
            for a in VH:
                act.wait_ge(*v.at(f"Z{a}", i))
                A(UU[a], UU[a], ACT.Exp).then_inc(*a_.mark(f"D{a}"))
                A(EG[a], bank[VBANK[a][0]][:, 0:T1], ACT.Exp).then_inc(*a_.mark(f"EG{a}"))
            for l in range(LAST):
                for a in VH:
                    act.wait_ge(*m.at(f"T{a}_{l}", i))
                    A(TT[a][:, 0:2 * P], bank[VBANK[a][0]][:, 0:2 * P], ACT.Copy).then_inc(*a_.mark(f"T{a}_{l}"))
                if l < SHORT_LAST:
                    A(sT, SB, ACT.Copy).then_inc(*a_.mark(f"sT_{l}"))
            for a in VH:
                act.wait_ge(*m.at(f"w{a}", i))
                A(AT_[a], bank[VBANK[a][1]][:, 0:T1], ACT.Copy).then_inc(*a_.mark(f"w{a}"))
            for c in range(NCH):
                for a in VH:
                    act.wait_ge(*m.at(f"v{a}_{c}", i))
                    if c > 0:
                        act.wait_ge(*pl.at(f"d{a}_{c - 1}", i))
                    A(own(vnew[a], c), own(bank[VBANK[a][0]], c)[:, 0:P], ACT.Copy).then_inc(*a_.mark(f"v{a}_{c}"))
            for a in VH:
                act.wait_ge(*m.at(f"o{a}_{NCH - 1}", i))
                A(UU[a], bank[VBANK[a][1]][:, 0:T1], ACT.Square).then_inc(*a_.mark(f"osq{a}"))
            for a in range(5):
                if a < 4:
                    act.wait_ge(*m.at(f"on{a}", i))
                    A(UU[a], bank[VBANK[a][0]][:, 0:T1], ACT.Ln, scale=1.0 / GD, bias=eps_1).then_inc(*a_.mark(f"ol{a}"))
                if a:
                    act.wait_ge(*a_.at(f"ol{a - 1}", i))
                    A(UU[a - 1], UU[a - 1], ACT.Exp, scale=-0.5).then_inc(*a_.mark(f"or{a - 1}"))

    def gdn_dve(dve):
        m, v, a_, pl = S("gdn", "pe"), S("gdn", "dve"), S("gdn", "act"), S("gdn", "pool")
        tt, ts, stt = nc.vector.tensor_tensor, nc.vector.tensor_scalar, nc.vector.scalar_tensor_tensor
        flat = lambda ap: ap.rearrange("p c h -> p (c h)")
        over_i = lambda ap, n: ap.unsqueeze(2).to_broadcast([ap.shape[0], ap.shape[1], n])
        dve.wait_ge(*a_.at("softplus"))
        stt(t_row, u_row, 0.0, t_row, ALU.max, ALU.add).then_inc(*v.mark("sp"))
        dve.wait_ge(*v.at("sp"))
        ts(t_row, t_row, ea[:, 0:1], -1.0, ALU.mult, ALU.mult).then_inc(*v.mark("g_row"))
        dve.wait_ge(*a_.at("b_tok"))
        nc.vector.tensor_copy(ea[:, 1:2], ea[:, 0:1]).then_inc(*v.mark("g_tok"))
        dve.wait_ge(*m.at("sums"))
        nc.vector.tensor_copy(G_row, bank[2][0:16, 0:T1]).then_inc(*v.mark("G_row"))
        nc.vector.tensor_copy(flat(G_tok), bank[3][:, 0:NCH * GV]).then_inc(*v.mark("G_tok"))
        dve.wait_ge(*v.at("G_tok"))
        tt(flat(el_tok), bank[4][:, 0:NCH * GV], flat(G_tok), ALU.subtract).then_inc(*v.mark("el_tok"))
        dve.wait_ge(*a_.at("eG"))
        stt(flat(nbe_tok), flat(nbe_tok), -1.0, flat(b_tok), ALU.mult, ALU.mult).then_inc(*v.mark("nbe"))
        with dve.Fori(0, GK // 2) as i, v.repeat(GK // 2):
            dve.wait_ge(bank_free, 8 + G["gdn_out"])
            for a in VH:
                ts(selG[a][0:16], G_row, EYE[0:16, 4 * i + a, :], None, ALU.mult).then_inc(*v.mark(f"selG{a}"))
                ts(selb[a][0:16], b_row, EYE[0:16, 4 * i + a, :], None, ALU.mult).then_inc(*v.mark(f"sel{a}"))
            for k in range(2):
                dve.wait_ge(*a_.at(f"rk{k}", i))
                tt(qn[k], big[:, 2 * i + k, :], qss[k], ALU.mult).then_inc(*v.mark(f"qn{k}"))
                tt(kn[k], big[:, 2 * i + (8 + k), :], kss[k], ALU.mult).then_inc(*v.mark(f"kn{k}"))
            for a in VH:
                dve.wait_ge(*m.at(f"rows{a}", i))
                for c in range(NCH):
                    w = slice(CHUNKS[c][0], CHUNKS[c][0] + CHUNKS[c][1])
                    stt(UU[a][:, w], bank[VBANK[a][0]][:, w], head(G_tok, 4 * i + a)[:, c, :], cn("neg_chunk")[:, 0:CHUNKS[c][1]],
                        ALU.subtract, ALU.add).then_inc(*v.mark(f"Z{a}" if c == NCH - 1 else f"Z{a}_{c}"))
            for a in VH:
                dve.wait_ge(*pl.at(f"a{a}", i))
                tt(AT_[a], AT_[a], bank[VBANK[a][1]][:, 0:T1], ALU.mult).then_inc(*v.mark(f"A{a}"))
                dve.wait_ge(*v.at(f"A{a}", i))
                tt(fulls(X1[a][:, 0:2 * P]), fc(AT_[a]), over_c(cn("level0_t"), 2), ALU.mult).then_inc(*v.mark(f"u{a}"))
                dve.wait_ge(*v.at(f"u{a}", i))
                dve.wait_ge(*pl.at(f"att{a}", i))
                tt(fulls(UU[a][:, 0:2 * P]), over_c(ident, 2), fulls(X1[a][:, 0:2 * P]), ALU.subtract).then_inc(*v.mark(f"U{a}_0"))
            for l in range(1, LAST + 1):
                level = cn("levels", P, l * P, P)
                for a in VH:
                    dve.wait_ge(*m.at(f"X{a}_{l}", i))
                    tt(fulls(X1[a][:, 0:2 * P]), fulls(bank[VBANK[a][0]][:, 0:2 * P]), over_c(level, 2), ALU.mult).then_inc(*v.mark(f"X{a}_{l}"))
                if l <= SHORT_LAST:
                    tt(sX, SB, over_c(level[0:HEAD_T, 0:HEAD_T], 4), ALU.mult).then_inc(*v.mark(f"sX_{l}"))
                for a in VH:
                    dve.wait_ge(*m.at(f"Y{a}_{l}", i))
                    Uo, Yo = odd(UU[a][:, 0:2 * P], LEVELS[l]), odd(bank[VBANK[a][1]][:, 0:2 * P], LEVELS[l])
                    tt(Uo, Uo, Yo, ALU.subtract).then_inc(*v.mark(f"U{a}_{l}"))
                if l <= SHORT_LAST:
                    tt(sU, sU, SB2, ALU.subtract).then_inc(*v.mark(f"sU_{l}"))
            dve.wait_ge(*v.at(f"U3_{LAST}", i))
            beta = lambda ap: ap.rearrange("p c (h o) -> p c h o", o=4)[0:HEAD_T, 0, i, :]
            tt(sU2, sU, over_i(beta(nbe_tok), HEAD_T), ALU.mult).then_inc(*v.mark("sU2"))
            tt(sU1, sU, over_i(beta(b_tok), HEAD_T), ALU.mult).then_inc(*v.mark("sU1"))
            for a in VH:
                U_ = fulls(UU[a][:, 0:2 * P])
                tt(fulls(U2[a][:, 0:2 * P]), U_, over_i(head(nbe_tok, 4 * i + a)[:, 1:3, 0], P), ALU.mult).then_inc(*v.mark(f"U2{a}"))
                tt(fulls(U1[a][:, 0:2 * P]), U_, over_i(head(b_tok, 4 * i + a)[:, 1:3, 0], P), ALU.mult).then_inc(*v.mark(f"U1{a}"))
            for c in range(NCH - 1):
                for a in VH:
                    dve.wait_ge(*m.at(f"s{a}_{c}", i))
                    s_bank = bank[VBANK[a][0]][:, P:2 * P]
                    if c == 0:
                        nc.vector.tensor_copy(state[a], s_bank).then_inc(*v.mark(f"S{a}_0"))
                    else:
                        dve.wait_ge(*v.at(f"S{a}_{c - 1}", i))
                        stt(state[a], state[a], EG[a][:, CHUNKS[c + 1][0] - 1:CHUNKS[c + 1][0]], s_bank, ALU.mult, ALU.add
                            ).then_inc(*v.mark(f"S{a}_{c}"))
            for a in VH:
                dve.wait_ge(*a_.at(f"or{a}", i))
                tt(AT_[a], bank[VBANK[a][1]][:, 0:T1], UU[a], ALU.mult).then_inc(*v.mark(f"on{a}"))
            for a in VH:
                h = 4 * i + (32 + a)
                dve.wait_ge(*v.at(f"on{a}", i))
                stt(big[:, h, :], AT_[a], pv("gdn_norm"), big[:, h, :], ALU.mult, ALU.mult).then_inc(*v.mark(f"o{a}"))

    def gdn_pool(pool):
        v, a_, pl = S("gdn", "dve"), S("gdn", "act"), S("gdn", "pool")
        tt = nc.gpsimd.tensor_tensor
        with pool.Fori(0, GK // 2) as i, pl.repeat(GK // 2):
            pool.wait_ge(bank_free, 8 + G["gdn_out"])
            for k in range(2):
                tt(qss[k], big[:, 2 * i + k, :], big[:, 2 * i + k, :], ALU.mult).then_inc(*pl.mark(f"sq_q{k}"))
                tt(kss[k], big[:, 2 * i + (8 + k), :], big[:, 2 * i + (8 + k), :], ALU.mult).then_inc(*pl.mark(f"squares{k}"))
            for a in VH:
                nc.gpsimd.tensor_copy(vst[a], big[:, 4 * i + (16 + a), :]).then_inc(*pl.mark(f"vst{a}"))
            for a in VH:
                pool.wait_ge(*a_.at(f"D{a}", i))
                tt(AT_[a], UU[a], kk[a // 2], ALU.mult).then_inc(*pl.mark(f"a{a}"))
                tt(att[a], UU[a], kq[a // 2], ALU.mult).then_inc(*pl.mark(f"att{a}"))
            pool.wait_ge(*v.at("A3", i))
            tt(sU, y[0:HEAD_T, 0:4, 0:HEAD_T], over_c(cn("level0_t")[0:HEAD_T, 0:HEAD_T], 4), ALU.mult).then_inc(*pl.mark("su"))
            pool.wait_ge(*pl.at("su", i))
            tt(sU, over_c(ident[0:HEAD_T, 0:HEAD_T], 4), sU, ALU.subtract).then_inc(*pl.mark("sU_0"))
            for a in VH:
                pool.wait_ge(*a_.at(f"EG{a}", i))
                tt(qd[a], qn[a // 2], EG[a], ALU.mult).then_inc(*pl.mark(f"qd{a}"))
            for c in range(NCH - 1):
                for a in VH:
                    pool.wait_ge(*a_.at(f"v{a}_{c}", i))
                    n = CHUNKS[c][1]
                    tt(vdec[a][0:n], vnew[a][0:n], head(el_tok, 4 * i + a)[0:n, c, :].to_broadcast([n, P]), ALU.mult
                       ).then_inc(*pl.mark(f"d{a}_{c}"))

    JB = ((0, 128), (128, 128), (256, 16))
    OFF = (0, T1, T1 + 144)
    r4 = lambda n: work[0:MH, n * T1:(n + 1) * T1]
    f_row, i_row, s_row, t4_row, bsum_row, cmax_row, m_row, c_row = (r4(n) for n in range(8))
    c_tok = work[:, 2180:2192]
    zbuf, pbuf = work[:, 2200:2632], [work[:, 2640:3072], work[:, 5800:6232]]
    em = [work[:, 3080:3352], work[:, 5520:5792]]
    rden = work[:, 3360:3632]
    vt = work[:, 3640:4408].rearrange("p (b d) -> p b d", b=3)
    hh = [work[:, 4420 + s * T1:4420 + (s + 1) * T1] for s in range(4)]

    def ml_gates_act(act):
        g, s = G["ml_g"], S("ml", "act")
        A = nc.scalar.activation
        act.wait_ge(*S("gates", "pe").at("ml0"))
        A(i_row, bank[g % 8][0:MH, 0:T1], ACT.Identity, bias=pv("ml_ib", rows=MH)).then_inc(bank_free, 1)
        act.wait_ge(*S("gates", "pe").at("ml1"))
        A(f_row, bank[(g + 1) % 8][0:MH, 0:T1], ACT.Identity, bias=pv("ml_fb", rows=MH)).then_inc(bank_free, 1)
        act.wait_ge(bank_free, 8 + g + 2)
        A(i_row, i_row, ACT.Tanh, scale=1.0 / GATE_CAP).then_inc(*s.mark("i"))
        A(f_row, f_row, ACT.Tanh, scale=1.0 / GATE_CAP).then_inc(*s.mark("tf"))
        act.wait_ge(*s.at("tf"))
        A(s_row, f_row, ACT.Abs).then_inc(*s.mark("af"))
        act.wait_ge(*s.at("af"))
        A(s_row, s_row, ACT.Exp, scale=-GATE_CAP).then_inc(*s.mark("ef"))
        act.wait_ge(*s.at("ef"))
        A(s_row, s_row, ACT.Ln, bias=1.0).then_inc(*s.mark("lf"))

    def scan(dve, s, tag, src, other, op, T):
        step, n = 1, 0
        while step < T:
            if n:
                dve.wait_ge(*s.at(f"{tag}{n - 1}"))
            nc.vector.tensor_tensor(other[..., step:T], src[..., step:T], src[..., 0:T - step], op).then_inc(*s.mark(f"{tag}{n}a"))
            nc.vector.tensor_copy(other[..., 0:step], src[..., 0:step]).then_inc(*s.mark(f"{tag}{n}"))
            src, other = other, src
            step, n = step * 2, n + 1
        dve.wait_ge(*s.at(f"{tag}{n - 1}"))
        return src

    def ml_gates_dve(dve):
        s, a_ = S("ml", "dve"), S("ml", "act")
        ts, stt, tt = nc.vector.tensor_scalar, nc.vector.scalar_tensor_tensor, nc.vector.tensor_tensor
        dve.wait_ge(*a_.at("lf"))
        ts(f_row, f_row, GATE_CAP, 0.0, ALU.mult, ALU.min).then_inc(*s.mark("minf"))
        dve.wait_ge(*s.at("minf"))
        tt(f_row, f_row, s_row, ALU.subtract).then_inc(*s.mark("logf"))
        dve.wait_ge(*s.at("logf"))
        b = scan(dve, s, "b", f_row, t4_row, ALU.add, T1)
        split_all(dve, split_lo, "ml_in", 4, 4)
        stt(c_row, i_row, GATE_CAP, b, ALU.mult, ALU.subtract).then_inc(*s.mark("c"))
        nc.vector.tensor_copy(bsum_row, b).then_inc(*s.mark("bsum"))
        dve.wait_ge(*s.at("bsum"))
        nc.vector.tensor_copy(f_row, c_row).then_inc(*s.mark("c2"))
        dve.wait_ge(*s.at("c2"))
        mx = scan(dve, s, "m", f_row, t4_row, ALU.max, T1)
        nc.vector.tensor_copy(cmax_row, mx).then_inc(*s.mark("cmax"))
        tt(m_row, mx, bsum_row, ALU.add).then_inc(*s.mark("m"))

    def ml_in_act(act):
        g0, b0 = G["ml_in"], FIRST_BLOCK["ml_in"]
        for turn in range(2):
            with act.Fori(0, (2, 1)[turn]) as i:
                for j in range(8):
                    split_hi(act, b0 + 16 * turn + j + AHEAD, i)
                    act.wait_ge(block_used, i * 8 + (b0 + 16 * turn + j + 1))
                    nc.scalar.activation(big[:, i * 8 + (16 * turn + j), :], bank[(g0 + j) % 8][:, 0:T1],
                                         (ACT.Copy, ACT.Sigmoid)[turn]).then_inc(bank_free, 1)

    def ml_pe(pe):
        m, v, a_, pl = S("ml", "pe"), S("ml", "dve"), S("ml", "act"), S("ml", "pool")
        mm = nc.tensor.matmul
        pe.wait_ge(bank_free, 8 + G["ml_out"])
        pe.wait_ge(*v.at("m"))
        for b, (lo, n) in enumerate(JB):
            last = nc.tensor.transpose(bank[0][0:n, 4 * b:4 * b + 4], c_row[:, lo:lo + n], ident[0:MH, 0:MH])
        last.then_inc(*m.mark("ctok"))
        def weights(h):
            if h:
                pe.wait_ge(*v.at(f"P{h - 1}"))
                pe.wait_ge(*a_.at(f"em{h - 1}"))
            else:
                pe.wait_ge(*v.at("ctok"))
            sel = ident[0:MH, h:h + 1].to_broadcast([MH, P])
            mm(bank[0][:, 0:T1], sel, cmax_row, start=True, stop=True)
            mm(bank[1][:, 0:T1], sel, m_row, start=True, stop=True).then_inc(*m.mark(f"rows{h}"))
            for b, (lo, n) in enumerate(JB):
                last = mm(bank[2][0:n, OFF[b]:OFF[b] + T1 - lo], big[:, 4 + h, lo:lo + n], big[:, h, lo:T1], start=True, stop=True)
            last.then_inc(*m.mark(f"S{h}"))

        def values(h):
            if h > 1:
                pe.wait_ge(*a_.at(f"ln{h - 2}"))
            if h:
                pe.wait_ge(*a_.at(f"vt{h - 1}1"))
            for d in range(2):
                for b, (lo, n) in enumerate(JB):
                    last = nc.tensor.transpose(bank[(3, 7)[d]][0:n, b * P:(b + 1) * P], big[:, 8 + 2 * h + d, lo:lo + n], ident)
                last.then_inc(*m.mark(f"vt{h}{d}"))

        weights(0)
        values(0)
        for h in range(MH):
            if h + 1 < MH:
                weights(h + 1)
            pe.wait_ge(*pl.at(f"P{h}"))
            pe.wait_ge(*a_.at(f"vt{h}1"))
            if h:
                pe.wait_ge(*v.at(f"y{h - 1}1"))
            for d in range(3):
                for b, (lo, n) in enumerate(JB):
                    w = ones[0:n, :] if d == 2 else work[0:n, 3640 + b * 256 + d * P:3640 + b * 256 + (d + 1) * P]
                    last = mm(bank[4 + d][:, lo:T1], w, pbuf[h % 2][0:n, OFF[b]:OFF[b] + T1 - lo], start=(b == 0), stop=(b == 2))
                last.then_inc(*m.mark(f"n{h}{d}"))
            if h + 1 < MH:
                values(h + 1)
                pe.wait_ge(*a_.at(f"vt{h + 1}0"))
            for d in range(2):
                pe.wait_ge(*a_.at(f"sq{h}{d}"))
                last = mm(bank[3][:, 0:T1], ones, hh[2 + d], start=(d == 0), stop=(d == 1))
            last.then_inc(*m.mark(f"ss{h}"))

    def ml_act(act):
        m, v, a_ = S("ml", "pe"), S("ml", "dve"), S("ml", "act")
        A = nc.scalar.activation

        def weights(h):
            act.wait_ge(*m.at(f"rows{h}"))
            if h > 1:
                act.wait_ge(*v.at(f"den{h - 2}"))
            A(em[h % 2], bank[1][:, 0:T1], ACT.Exp, scale=-1.0).then_inc(*a_.mark(f"em{h}"))
            act.wait_ge(*v.at(f"Z{h}"))
            A(zbuf[:, 0:416], zbuf[:, 0:416], ACT.Exp, scale=-1.0).then_inc(*a_.mark(f"Ea{h}"))
            A(zbuf[0:16, 416:432], zbuf[0:16, 416:432], ACT.Exp, scale=-1.0).then_inc(*a_.mark(f"E{h}"))

        def values(h):
            for d in range(2):
                act.wait_ge(*m.at(f"vt{h}{d}"))
                if h:
                    act.wait_ge(*m.at(f"n{h - 1}2"))
                bk = bank[(3, 7)[d]]
                A(vt[:, 0:2, d * P:(d + 1) * P], bk[:, 0:256].rearrange("p (b d) -> p b d", b=2), ACT.Copy).then_inc(*a_.mark(f"vta{h}{d}"))
                A(vt[0:16, 2, d * P:(d + 1) * P], bk[0:16, 256:384], ACT.Copy).then_inc(*a_.mark(f"vt{h}{d}"))

        weights(0)
        values(0)
        for h in range(MH):
            if h + 1 < MH:
                weights(h + 1)
            act.wait_ge(*m.at(f"n{h}2"))
            if h:
                act.wait_ge(*v.at(f"o{h - 1}1"))
            A(rden, bank[6][:, 0:T1], ACT.Abs).then_inc(*a_.mark(f"ab{h}"))
            if h + 1 < MH:
                values(h + 1)
            for d in range(2):
                act.wait_ge(*v.at(f"y{h}{d}"))
                if h:
                    act.wait_ge(*m.at(f"ss{h - 1}"))
                A(hh[2 + d], hh[d], ACT.Square).then_inc(*a_.mark(f"sq{h}{d}"))
            act.wait_ge(*m.at(f"ss{h}"))
            A(rden, bank[3][:, 0:T1], ACT.Ln, bias=eps_1, scale=1.0 / MV).then_inc(*a_.mark(f"ln{h}"))
            act.wait_ge(*a_.at(f"ln{h}"))
            A(rden, rden, ACT.Exp, scale=-0.5).then_inc(*a_.mark(f"rs{h}"))

    def ml_dve(dve):
        m, v, a_ = S("ml", "pe"), S("ml", "dve"), S("ml", "act")
        ts, stt, tt = nc.vector.tensor_scalar, nc.vector.scalar_tensor_tensor, nc.vector.tensor_tensor
        dve.wait_ge(*m.at("ctok"))
        nc.vector.tensor_copy(c_tok[:, 0:8], bank[0][:, 0:8]).then_inc(*v.mark("ctoka"))
        nc.vector.tensor_copy(c_tok[0:16, 8:12], bank[0][0:16, 8:12]).then_inc(*v.mark("ctok"))
        dve.wait_ge(*v.at("ctok"))

        def weights(h):
            dve.wait_ge(*m.at(f"rows{h}"))
            if h:
                dve.wait_ge(*v.at(f"P{h - 1}"))
            for b, (lo, n) in enumerate(JB):
                ts(zbuf[0:n, OFF[b]:OFF[b] + T1 - lo], bank[0][0:n, lo:T1], work[0:n, 2180 + 4 * b + h:2181 + 4 * b + h], 0.0,
                   ALU.subtract, ALU.max).then_inc(*v.mark(f"Z{h}" if b == 2 else f"Z{h}{b}"))
            dve.wait_ge(*m.at(f"S{h}"))
            dve.wait_ge(*a_.at(f"E{h}"))
            if h > 1:
                dve.wait_ge(*m.at(f"n{h - 2}2"))
            tt(pbuf[h % 2][:, 0:416], zbuf[:, 0:416], bank[2][:, 0:416], ALU.mult).then_inc(*v.mark(f"Pa{h}"))
            tt(pbuf[h % 2][0:16, 416:432], zbuf[0:16, 416:432], bank[2][0:16, 416:432], ALU.mult).then_inc(*v.mark(f"P{h}"))

        weights(0)
        for h in range(MH):
            if h + 1 < MH:
                weights(h + 1)
            dve.wait_ge(*a_.at(f"ab{h}"))
            tt(rden, rden, em[h % 2], ALU.max).then_inc(*v.mark(f"den{h}"))
            dve.wait_ge(*v.at(f"den{h}"))
            nc.vector.reciprocal(rden, rden).then_inc(*v.mark(f"r{h}"))
            dve.wait_ge(*v.at(f"r{h}"))
            for d in range(2):
                tt(hh[d], bank[4 + d][:, 0:T1], rden, ALU.mult).then_inc(*v.mark(f"y{h}{d}"))
            dve.wait_ge(*a_.at(f"rs{h}"))
            for d in range(2):
                stt(hh[d], hh[d], pv("ml_norm", 2 * h + d), rden, ALU.mult, ALU.mult).then_inc(*v.mark(f"w{h}{d}"))
            for d in range(2):
                dve.wait_ge(*v.at(f"w{h}{d}"))
                tt(mix[:, 2 * h + d, :], hh[d], big[:, 16 + 2 * h + d, :], ALU.mult).then_inc(*v.mark(f"o{h}{d}"))

    def ml_pool(pool):
        v, pl = S("ml", "dve"), S("ml", "pool")
        for h in range(MH):
            pool.wait_ge(*v.at(f"P{h}"))
            for b, (lo, n) in enumerate(JB):
                o = pbuf[h % 2][0:n, OFF[b]:OFF[b] + n]
                nc.gpsimd.tensor_tensor(o, o, cn("upto")[0:n, 0:n], ALU.mult).then_inc(*pl.mark(f"P{h}" if b == 2 else f"P{h}{b}"))

    X = lambda k: hs[:, k, N_META:T1]
    yt, sqt = (lambda m: y[:, m, 0:T2]), (lambda m: sq[:, m, 0:T2])

    def ln_pe(pe, n):
        name, g = f"ln{n}", G[f"lm{n}"]
        pe.wait_ge(bank_free, g + 1)
        for m in range(KC):
            pe.wait_ge(bank_free, 8 + g - 8 + m + 1)
            last = nc.tensor.matmul(bank[g % 8][:, 0:T2], ones, yt(m), start=(m == 0), stop=(m == KC - 1))
        last.then_inc(*S("norm", "pe").mark(name + "m"))
        pe_sum(pe, name + "v", g + 1, sqt, T2)

    def ln_act(act, n, which, layer):
        name, g = f"ln{n}", G[f"lm{n}"]
        for m in range(KC):
            act.wait_ge(*S("norm", "dve").at(f"{name}_c{m}"))
            nc.scalar.activation(sqt(m), yt(m), ACT.Square).then_inc(*S("norm", "act").mark(f"{name}v_{m}"))
        act.wait_ge(bank_free, 8 + g + 1)
        act_scale(act, name + "v", g + 1, rs[:, 0, 0:T2], T2, D, eps_ln)
        for m in range(KC):
            act.wait_ge(*S("norm", "dve").at(f"{name}_g{m}"))
            beta = pv(which, (2 * layer + 1) * KC + m)
            nc.scalar.activation(X(m), yt(m), ACT.Identity, bias=beta).then_inc(*S("norm", "act").mark(f"{name}_x{m}"))
            if n < 3:
                nc.scalar.activation(xs[:, m, 0:T2], yt(m), ACT.Identity, bias=beta).then_inc(*S("norm", "act").mark(f"{name}_hi{m}"))

    def x_act(act, name):
        for m in range(KC):
            act.wait_ge(*added("post3", m))
            nc.scalar.activation(xs[:, m, 0:T2], X(m), ACT.Copy).then_inc(*S("norm", "act").mark(f"{name}_hi{m}"))

    def x_dve(dve, name):
        x_lo(dve, nc.vector, "dve", name, X, T2, DVE_CHUNKS)

    def x_pool(pool, name):
        x_lo(pool, nc.gpsimd, "pool", name, X, T2, POOL_CHUNKS)

    def ln_dve(dve, n, which, layer, last_block):
        name, g = f"ln{n}", G[f"lm{n}"]
        st = S("norm", "dve")
        stt = nc.vector.scalar_tensor_tensor
        dve.wait_ge(block_used, last_block)
        for m in range(KC):
            stt(yt(m), X(m), ALPHA, bank[(g - 8 + m) % 8][:, 0:T2], ALU.mult, ALU.add).then_inc(bank_free, 1)
        dve.wait_ge(*S("norm", "pe").at(name + "m"))
        for m in range(KC):
            stt(yt(m), bank[g % 8][:, 0:T2], -1.0 / D, yt(m), ALU.mult, ALU.add).then_inc(*st.mark(f"{name}_c{m}"))
        dve.wait_ge(*st.at(f"{name}_c7"))
        nc.vector.memset(rs[:, 1, 0:1], 0.0).then_inc(bank_free, 1)
        dve.wait_ge(*S("norm", "act").at(f"{name}v_scale"))
        for m in range(KC):
            stt(yt(m), yt(m), pv(which, 2 * layer * KC + m), rs[:, 0, 0:T2], ALU.mult, ALU.mult).then_inc(*st.mark(f"{name}_g{m}"))
        if n < 3:
            x_dve(dve, name)

    def in_act(act, phase, kinds):
        g0, b0 = G[phase], FIRST_BLOCK[phase]
        for t, (fn, scale) in enumerate(kinds):
            split_hi(act, b0 + t + AHEAD)
            act.wait_ge(block_used, b0 + t + 1)
            nc.scalar.activation(big[:, t, 0:T2], bank[(g0 + t) % 8][:, 0:T2], fn, scale=scale).then_inc(bank_free, 1)

    QB = 2
    probs = work[:, 0:2048]
    ptr = work[:, 2048:4096]
    st8 = lambda k: work[:, 4096 + 8 * k:4104 + 8 * k]
    qrot = [work[0:96, 4160 + h * T2:4160 + (h + 1) * T2] for h in range(4)]
    krot = [work[0:96, 5184 + h * T2:5184 + (h + 1) * T2] for h in range(4)]
    spare = big[:, 18:24, :].rearrange("p a b -> p (a b)")
    vmla = spare[:, 0:1024].rearrange("p (b d) -> p b d", b=2)
    vswa = spare[:, 1024:1280].rearrange("p (b d) -> p b d", b=2)
    krr, tmp96 = work[0:96, 6208:6464], work[0:96, 6464:6720]

    def halves(U):
        return range(U // 2), range(U // 2, U)

    def attn_pe(pe, ph, units, vtok, meanwhile=lambda n: None):
        m, v, a_ = S(ph, "pe"), S(ph, "dve"), S(ph, "act")
        mm = nc.tensor.matmul
        U = len(units)
        for n in range(QB):
            W = 128 * (n + 1)
            per = 512 // W
            if n:
                pe.wait_ge(*a_.at("out0"))
            for u, (q, k) in enumerate(units):
                b, o = u // per, (u % per) * W
                last = mm(bank[b][:, o:o + W], q[:, n * 128:(n + 1) * 128], k[:, 0:W], start=True, stop=True)
            last.then_inc(*m.mark(f"s{n}"))
            meanwhile(2 * n)
            for us in halves(U):
                pe.wait_ge(*v.at(f"p{n}_{us[0]}"))
                for j in range(n + 1):
                    for u in us:
                        t = j * U + u
                        last = nc.tensor.transpose(bank[t // 4][:, (t % 4) * 128:(t % 4 + 1) * 128],
                                                   probs[:, u * W + j * 128:u * W + (j + 1) * 128], ident)
                        if t % 4 == 3:
                            last.then_inc(*m.mark(f"t{n}_{t // 4}"))
            meanwhile(2 * n + 1)
            for t in range((n + 1) * U // 4):
                pe.wait_ge(*a_.at(f"t{n}_{t}"))
            for u in range(U):
                for j in range(n + 1):
                    o, w = vtok(u, j)
                    t = j * U + u
                    last = mm(o, w, ptr[:, t * 128:(t + 1) * 128], start=(j == 0), stop=(j == n))
            last.then_inc(*m.mark(f"o{n}"))

    def attn_act(act, ph, U, sink, slot, meanwhile=lambda n: None):
        m, v, a_ = S(ph, "pe"), S(ph, "dve"), S(ph, "act")
        A = nc.scalar.activation
        for n in range(QB):
            W = 128 * (n + 1)
            for us in halves(U):
                act.wait_ge(*v.at(f"e{n}_{us[0]}"))
                if sink:
                    es = st8(2)[:, us[0]:us[-1] + 1]
                    A(es, es, ACT.Exp).then_inc(*a_.mark(f"es{n}_{us[0]}"))
                for u in us:
                    p = probs[:, u * W:(u + 1) * W]
                    A(p, p, ACT.Exp, bias=st8(1)[:, u:u + 1]).then_inc(*a_.mark(f"e{n}_{u}"))
            meanwhile(2 * n)
            order = sorted(range((n + 1) * U // 4), key=lambda t: t * 4 % U)
            for t in order:
                act.wait_ge(*m.at(f"t{n}_{t}"))
                A(ptr[:, t * 512:(t + 1) * 512], bank[t][:, :], ACT.Copy).then_inc(*a_.mark(f"t{n}_{t}"))
            meanwhile(2 * n + 1)
            act.wait_ge(*m.at(f"o{n}"))
            A(mix[:, slot:slot + 4, n * 128:(n + 1) * 128], bank[7][:, :].rearrange("p (t i) -> p t i", t=4), ACT.Copy
              ).then_inc(*a_.mark(f"out{n}"))

    def attn_dve(dve, ph, U, scale, mask, sink, meanwhile=lambda n: None):
        m, v, a_ = S(ph, "pe"), S(ph, "dve"), S(ph, "act")
        ts, stt, tt = nc.vector.tensor_scalar, nc.vector.scalar_tensor_tensor, nc.vector.tensor_tensor
        for n in range(QB):
            W = 128 * (n + 1)
            per = 512 // W
            pr = probs[:, 0:U * W].rearrange("p (u w) -> p u w", u=U)
            mk = (mask if n else mask[:, 128:256]).unsqueeze(1).to_broadcast([P, per, W])
            dve.wait_ge(*m.at(f"s{n}"))
            for b in range(U // per):
                stt(pr[:, b * per:(b + 1) * per, :], bank[b][:, :].rearrange("p (u w) -> p u w", u=per), scale, mk,
                    ALU.mult, ALU.add).then_inc(*v.mark(f"s{n}_{b}"))
            dve.wait_ge(*v.at(f"s{n}_{U // per - 1}"))
            for us in halves(U):
                w = slice(us[0], us[-1] + 1)
                mx, ng, es = (st8(k)[:, w] for k in range(3))
                nc.vector.reduce_max(mx, pr[:, w, :], axis=AX).then_inc(*v.mark(f"mx{n}_{us[0]}"))
                dve.wait_ge(*v.at(f"mx{n}_{us[0]}"))
                if sink:
                    tt(mx, mx, pv("sinks", 0, 8)[:, w], ALU.max).then_inc(*v.mark(f"ms{n}_{us[0]}"))
                    dve.wait_ge(*v.at(f"ms{n}_{us[0]}"))
                    tt(es, pv("sinks", 0, 8)[:, w], mx, ALU.subtract).then_inc(*v.mark(f"es{n}_{us[0]}"))
                ts(ng, mx, -1.0, None, ALU.mult).then_inc(*v.mark(f"e{n}_{us[0]}"))
            meanwhile(2 * n)
            for us in halves(U):
                w = slice(us[0], us[-1] + 1)
                es, sm, rc = (st8(k)[:, w] for k in range(2, 5))
                dve.wait_ge(*a_.at(f"e{n}_{us[-1]}"))
                nc.vector.reduce_sum(sm, pr[:, w, :], axis=AX).then_inc(*v.mark(f"sm{n}_{us[0]}"))
                dve.wait_ge(*v.at(f"sm{n}_{us[0]}"))
                if sink:
                    tt(sm, sm, es, ALU.add).then_inc(*v.mark(f"sd{n}_{us[0]}"))
                    dve.wait_ge(*v.at(f"sd{n}_{us[0]}"))
                nc.vector.reciprocal(rc, sm).then_inc(*v.mark(f"r{n}_{us[0]}"))
                dve.wait_ge(*v.at(f"r{n}_{us[0]}"))
                tt(pr[:, w, :], pr[:, w, :], rc.unsqueeze(2).to_broadcast([P, len(us), W]), ALU.mult).then_inc(*v.mark(f"p{n}_{us[0]}"))
            meanwhile(2 * n + 1)

    def swa_units():
        return [(big[64 * a:64 * a + 64, 12 + t, 0:T2], big[64 * a:64 * a + 64, 16, 0:T2]) for a in range(2) for t in range(4)]

    def swa_v(u, j):
        a, t = divmod(u, 4)
        return bank[7][64 * a:64 * a + 64, t * 128:(t + 1) * 128], vswa[:, j, 64 * a:64 * a + 64]

    def even_pe(pe):
        m = S("swa", "pe")
        pe.wait_ge(bank_free, 8 + G["ev_out"])
        for j in range(2):
            last = nc.tensor.transpose(bank[6][:, j * 128:(j + 1) * 128], big[:, 17, j * 128:(j + 1) * 128], ident)
        last.then_inc(*m.mark("vt"))
        attn_pe(pe, "swa", swa_units(), swa_v)

    def even_act(act):
        act.wait_ge(*S("swa", "pe").at("vt"))
        nc.scalar.activation(vswa, bank[6][:, 0:256].rearrange("p (b d) -> p b d", b=2), ACT.Copy).then_inc(*S("swa", "act").mark("vt"))
        attn_act(act, "swa", 8, True, 4)

    def even_pool(pool):
        pl = S("swa", "pool")
        pool.wait_ge(bank_free, 8 + G["ev_out"])
        for t in range(4):
            nc.gpsimd.tensor_tensor(cv[:, t, 0:T2], big[:, 4 + t, 0:T2], big[:, 8 + t, 0:T2], ALU.mult).then_inc(*pl.mark(f"z{t}"))
        for t in range(4):
            pool.wait_ge(*S("swa", "dve").at(f"z{t}_2"))
            nc.gpsimd.tensor_tensor(mix[:, t, 0:T2], cv[:, 4 + t, 0:T2], big[:, t, 0:T2], ALU.mult).then_inc(*pl.mark(f"y{t}"))

    def even_dve(dve):
        v, pl = S("swa", "dve"), S("swa", "pool")

        def conv_taps(taps):
            for tap in taps:
                for t in range(4):
                    w = pv("ev_conv", 3 * t + 2 - tap)
                    o, z = cv[:, 4 + t, 0:T2], cv[:, t, 0:T2]
                    if tap == 0:
                        dve.wait_ge(*pl.at(f"z{t}"))
                        nc.vector.tensor_scalar(o, z, w, None, ALU.mult).then_inc(*v.mark(f"z{t}_0"))
                    else:
                        dve.wait_ge(*v.at(f"z{t}_{tap - 1}"))
                        nc.vector.scalar_tensor_tensor(o[:, tap:], z[:, 0:T2 - tap], w, o[:, tap:], ALU.mult, ALU.add
                                                       ).then_inc(*v.mark(f"z{t}_{tap}"))

        attn_dve(dve, "swa", 8, 64 ** -0.5, cn("swa_mask"), True, lambda n: conv_taps(((0,), (1, 2), (), ())[n]))

    GR, NG = 16, T2 // 16
    PH = 64 // GR
    GLA_PARTS = ((0, 1), (2, 3), (4, 5), ())
    LA, LB, RR = (xf[:, 2 * s:2 * s + 2, 0:T2] for s in range(3))
    LB_SUM = LA if (T2 - 1).bit_length() % 2 == 0 else LB
    QG = xf[:, 6:8, 0:T2]
    KG = [y[:, 2 * s:2 * s + 2, 0:T2] for s in range(PH)]
    KP, QP = ([xf[:, 8 + 2 * s + o:10 + 2 * s + o, 0:T2 // 2] for s in (0, 2)] for o in (0, 2))
    last_tiles = big[:, 33:48, :].rearrange("p a b -> p (a b)")
    gp = [last_tiles[:, h * 512:512 + h * 512] for h in range(4)]
    vg = last_tiles[:, 2048:3072].rearrange("p (b d) -> p b d", b=2)
    go = [sq[:, h, 0:T2] for h in range(4)]
    gs = [sq[:, 4 + h, 0:T2] for h in range(4)]
    glow = cv[0:16, 0, 0:T2]

    def gla_scores_pe(pe, parts):
        mm = nc.tensor.matmul
        for part in parts:
            if part == 0:
                pe.wait_ge(*S("gla", "dve").at("qg"))
            pe.wait_ge(*S("gla", "pool").at(f"k{part}"))
            for h in range(4):
                t, a = divmod(h, 2)
                rows = slice(64 * a, 64 * a + 64)
                if part < PH:
                    for n in range(NG // PH):
                        g = PH * n + part
                        o = 128 * (n // 2) + 16 * g
                        last = mm(bank[3 + h][64 * (n % 2):64 * (n % 2) + 64, o:o + 16], KG[part][rows, t, 64 * n:64 * n + 64],
                                  QG[rows, t, 16 * g:16 * g + 16], start=True, stop=True)
                elif part == PH:
                    for n in range(2):
                        last = mm(bank[3 + h][0:64, 256 * n + 64:256 * n + 128], KP[0][rows, t, 64 * n:64 * n + 64],
                                  QP[0][rows, t, 64 * n:64 * n + 64], start=True, stop=True)
                else:
                    last = mm(bank[3 + h][:, 128:256], KP[1][rows, t, :], QP[1][rows, t, :], start=True, stop=True)
            last.then_inc(*S("gla", "pe").mark(f"s{part}"))

    def gla_keys_act(act, parts):
        A, v, a_ = nc.scalar.activation, S("gla", "dve"), S("gla", "act")
        for part in parts:
            if part == 0:
                act.wait_ge(*v.at("dq"))
                A(QG, QG, ACT.Exp).then_inc(*a_.mark("qg"))
            act.wait_ge(*v.at(f"k{part}"))
            if part < PH:
                A(KG[part], KG[part], ACT.Exp, scale=-1.0).then_inc(*a_.mark(f"k{part}"))
            else:
                A(KP[part - PH], KP[part - PH], ACT.Exp, scale=-1.0).then_inc(*a_.mark(f"k{part}a"))
                A(QP[part - PH], QP[part - PH], ACT.Exp).then_inc(*a_.mark(f"k{part}"))

    def gla_keys_dve(dve, parts):
        v, tt = S("gla", "dve"), nc.vector.tensor_tensor
        b = LB_SUM
        for part in parts:
            if part < PH:
                K4 = KG[part].rearrange("p t (n k) -> p t n k", k=64)
                r = RR[:, :, 0:NG].rearrange("p t (n g) -> p t n g", g=PH)[:, :, :, part]
                tt(K4, b.rearrange("p t (n k) -> p t n k", k=64), r.unsqueeze(3).to_broadcast([P, 2, NG // PH, 64]), ALU.subtract
                   ).then_inc(*v.mark(f"k{part}a"))
                dve.wait_ge(*v.at(f"k{part}a"))
                nc.vector.tensor_scalar(KG[part], KG[part], -80.0, None, ALU.max).then_inc(*v.mark(f"k{part}"))
            else:
                n = part - PH
                size = 64 << n
                for t in range(2):
                    halves = b[:, t, :].rearrange("p (n two k) -> p n two k", two=2, k=size)
                    r = halves[:, :, 0, size - 1].unsqueeze(2).to_broadcast([P, T2 // (2 * size), size])
                    for dst, half in ((KP[n], 0), (QP[n], 1)):
                        tt(dst[:, t, :].rearrange("p (n k) -> p n k", k=size), halves[:, :, half, :], r, ALU.subtract
                           ).then_inc(*v.mark(f"k{part}" if t and half else f"k{part}{t}{half}"))
            if part == 0:
                dve.wait_ge(*S("gla", "act").at("qg"))
                tt(QG, QG, big[:, 0:2, 0:T2], ALU.mult).then_inc(*v.mark("qg"))

    def odd_pe(pe):
        m, v, a_ = S("gla", "pe"), S("gla", "dve"), S("gla", "act")
        mm = nc.tensor.matmul
        pe.wait_ge(bank_free, 8 + G["od_out"])
        pe.wait_ge(*a_.at("glow"))
        for t in range(2):
            last = mm(bank[0][:, t * T2:(t + 1) * T2], pv("gla_w", 128 * t, 128, 16), glow, start=True, stop=True)
        last.then_inc(*m.mark("gate"))
        pe.wait_ge(*S("mla", "act").at("sq"))
        for t in range(2):
            last = mm(bank[3][:, 0:T2], ones, csq[t], start=(t == 0), stop=(t == 1))
        last = mm(bank[4][:, 0:T2], ones, csq[2], start=True, stop=True)
        last.then_inc(*S("mla", "pe").mark("ss"))
        for h in range(4):
            for j in range(2):
                last = nc.tensor.transpose(bank[1 + j][:, h * 128:(h + 1) * 128], big[:, 4 + h, j * 128:(j + 1) * 128], ident)
        last.then_inc(*m.mark("vt"))
        mla_pe(pe)
        pe.wait_ge(*S("mla", "act").at("out1"))
        for h in range(4):
            pe.wait_ge(*v.at(f"p{h}"))
            b = (0, 1, 2, 7)[h]
            mm(bank[b][:, 0:T2], vg[:, 0, h * 128:(h + 1) * 128], gp[h][:, 0:T2], start=True, stop=False)
            mm(bank[b][:, 128:T2], vg[:, 1, h * 128:(h + 1) * 128], gp[h][:, T2:T2 + 128], start=False, stop=True
               ).then_inc(*m.mark(f"o{h}"))
        for h in range(4):
            pe.wait_ge(*a_.at(f"sq{h}"))
            mm(bank[3 + h][:, 0:T2], ones, gs[h], start=True, stop=True).then_inc(*m.mark(f"ss{h}"))

    def odd_gate_act(act):
        act.wait_ge(*S("gates", "pe").at("od0"))
        nc.scalar.activation(glow, bank[G["od_g"] % 8][0:16, 0:T2], ACT.Copy).then_inc(bank_free, 1)

    def odd_act(act):
        m, a_ = S("gla", "pe"), S("gla", "act")
        A = nc.scalar.activation
        act.wait_ge(bank_free, 8 + G["od_out"])
        for t in range(3):
            last = A(csq[t], big[:, 12 + t, 0:T2], ACT.Square)
        last.then_inc(*S("mla", "act").mark("sq"))
        A(rs[:, 1, 0:1], eps_1, ACT.Copy).then_inc(*a_.mark("glow"))
        act.wait_ge(*m.at("gate"))
        for t in range(2):
            A(LA[:, t, :], bank[0][:, t * T2:(t + 1) * T2], ACT.Identity, bias=pv("gla_b", t)).then_inc(*a_.mark(f"x{t}"))
        act.wait_ge(*a_.at("x1"))
        A(LB, LA, ACT.Abs).then_inc(*a_.mark("abs"))
        act.wait_ge(*a_.at("abs"))
        A(LB, LB, ACT.Exp, scale=-1.0).then_inc(*a_.mark("e"))
        act.wait_ge(*a_.at("e"))
        A(LB, LB, ACT.Ln, bias=1.0).then_inc(*a_.mark("ln"))
        mla_norm_act(act)
        act.wait_ge(*m.at("vt"))
        for j in range(2):
            A(vg[:, j, :], bank[1 + j][:, :], ACT.Copy).then_inc(*a_.mark(f"vt{j}"))
        mla_act(act)
        for h in range(4):
            act.wait_ge(*m.at(f"o{h}"))
            A(gs[h], bank[(0, 1, 2, 7)[h]][:, 0:T2], ACT.Square).then_inc(*a_.mark(f"sq{h}"))
        for h in range(4):
            act.wait_ge(*m.at(f"ss{h}"))
            A(gs[h], bank[3 + h][:, 0:T2], ACT.Ln, scale=1.0 / 128, bias=eps_1).then_inc(*a_.mark(f"l{h}"))
        for h in range(4):
            act.wait_ge(*a_.at(f"l{h}"))
            A(gs[h], gs[h], ACT.Exp, scale=-0.5).then_inc(*a_.mark(f"r{h}"))

    def odd_dve(dve):
        m, v, a_, pl = S("gla", "pe"), S("gla", "dve"), S("gla", "act"), S("gla", "pool")
        ts, stt, tt = nc.vector.tensor_scalar, nc.vector.scalar_tensor_tensor, nc.vector.tensor_tensor
        mla_norm_dve(dve)
        dve.wait_ge(*a_.at("ln"))
        ts(LA, LA, 0.0, 1.0 / 16, ALU.min, ALU.mult).then_inc(*v.mark("min"))
        dve.wait_ge(*v.at("min"))
        stt(LA, LB, -1.0 / 16, LA, ALU.mult, ALU.add).then_inc(*v.mark("la"))
        dve.wait_ge(*v.at("la"))
        b = scan(dve, v, "b", LA, LB, ALU.add, T2)
        assert b is LB_SUM
        groups = lambda ap: ap.rearrange("p t (g k) -> p t g k", k=GR)
        r = RR[:, :, 0:NG]
        nc.vector.memset(r[:, :, 0:1], 0.0).then_inc(*v.mark("r0"))
        nc.vector.tensor_copy(r[:, :, 1:NG], groups(b)[:, :, 0:NG - 1, GR - 1]).then_inc(*v.mark("r"))
        dve.wait_ge(*v.at("r"))
        tt(groups(QG), groups(b), r.unsqueeze(3).to_broadcast([P, 2, NG, GR]), ALU.subtract).then_inc(*v.mark("dq"))
        mla_dve(dve)
        dve.wait_ge(*m.at(f"s{PH + 1}"))
        dve.wait_ge(*pl.at("gp"))
        for h in range(4):
            for lo in (0, 64):
                both = lambda ap: ap[lo:lo + 64].rearrange("p (b q) -> p b q", q=256)[:, :, lo:128]
                mask = cn("upto")[lo:lo + 64, lo:128].unsqueeze(1).to_broadcast([64, 2, 128 - lo])
                tt(both(gp[h]), both(bank[3 + h][:, :]), mask, ALU.mult).then_inc(*v.mark(f"p{lo}{h}"))
            nc.vector.tensor_copy(gp[h][:, 128:256], bank[3 + h][:, 128:256]).then_inc(*v.mark(f"p{h}"))
        for h in range(4):
            dve.wait_ge(*a_.at(f"r{h}"))
            tt(go[h], bank[(0, 1, 2, 7)[h]][:, 0:T2], gs[h], ALU.mult).then_inc(*v.mark(f"y{h}"))
        for h in range(4):
            dve.wait_ge(*v.at(f"y{h}"))
            stt(mix[:, h, 0:T2], go[h], pv("gla_norm"), big[:, 8 + h, 0:T2], ALU.mult, ALU.mult).then_inc(*v.mark(f"o{h}"))

    def odd_pool(pool):
        a_, pl = S("gla", "act"), S("gla", "pool")
        pool.wait_ge(bank_free, 8 + G["od_out"])
        for h in range(4):
            nc.gpsimd.memset(gp[h][64:128, :].rearrange("p (b q) -> p b q", q=256)[:, :, 0:64], 0.0
                             ).then_inc(*pl.mark("gp" if h == 3 else f"gp{h}"))
        pool.wait_ge(*pl.at("gp"))
        for part in range(PH + 2):
            pool.wait_ge(*a_.at(f"k{part}"))
            if part < PH:
                nc.gpsimd.tensor_tensor(KG[part], KG[part], big[:, 2:4, 0:T2], ALU.mult).then_inc(*pl.mark(f"k{part}"))
                continue
            size = 64 << (part - PH)
            for t in range(2):
                for dst, src, half in ((KP[part - PH], 2, 0), (QP[part - PH], 0, 1)):
                    d = dst[:, t, :].rearrange("p (n k) -> p n k", k=size)
                    x = big[:, src + t, 0:T2].rearrange("p (n two k) -> p n two k", two=2, k=size)[:, :, half, :]
                    nc.gpsimd.tensor_tensor(d, d, x, ALU.mult).then_inc(*pl.mark(f"k{part}" if t and half else f"k{part}{t}{half}"))

    cq = [cv[:, 1 + t, 0:T2] for t in range(2)]
    ckv = cv[:, 3, 0:T2]
    csq = [cv[:, 4 + t, 0:T2] for t in range(3)]
    crs = [cv[:, 7, 0:T2], rs[:, 1, 0:T2]]
    MLAW = big[:, 24:33, :].rearrange("p a b -> p (a b)")[:, 0:2304]

    def mla_pe(pe):
        m, v, a_ = S("mla", "pe"), S("mla", "dve"), S("mla", "act")
        mm = nc.tensor.matmul
        pe.wait_ge(*v.at("ckv"))
        pe.wait_ge(mla_loaded, 16)
        B = (0, 5, 6, 7)
        for h in range(4):
            if h == 0:
                pe.wait_ge(*S("gla", "act").at("x1"))
            for s in range(2):
                for t in range(2):
                    last = mm(bank[B[h]][0:96, s * T2:(s + 1) * T2], MLAW[:, 768 * s + 384 * t + 96 * h:768 * s + 384 * t + 96 * h + 96],
                              cq[t], start=(t == 0), stop=(t == 1))
            last.then_inc(*m.mark(f"q{h}"))
        pe.wait_ge(*S("gla", "act").at("vt1"))
        for h in range(4):
            last = mm(bank[1 + h // 2][0:64, (h % 2) * T2:(h % 2 + 1) * T2], MLAW[:, 1536 + 64 * h:1600 + 64 * h], ckv, start=True, stop=True)
        last.then_inc(*m.mark("k"))
        pe.wait_ge(*a_.at("rkv"))
        for j in range(2):
            last = mm(bank[3 + j][:, :], ckv[:, j * 128:(j + 1) * 128], MLAW[:, 1792:2304], start=True, stop=True)
        last.then_inc(*m.mark("v"))
        pe.wait_ge(*v.at("q3"))
        pe.wait_ge(*a_.at("v1"))
        units = [(qrot[h], krot[h]) for h in range(4)]
        attn_pe(pe, "mla", units, lambda u, j: (bank[7][:, u * 128:(u + 1) * 128], vmla[:, j, u * 128:(u + 1) * 128]), lambda n: gla_scores_pe(pe, GLA_PARTS[n]))

    def mla_norm_act(act):
        m, a_ = S("mla", "pe"), S("mla", "act")
        A = nc.scalar.activation
        act.wait_ge(*m.at("ss"))
        for n, name in enumerate(("q", "kv")):
            A(crs[n], bank[3 + n][:, 0:T2], ACT.Ln, scale=1.0 / (256, 128)[n], bias=eps_1).then_inc(*a_.mark(f"l{name}"))
        for n, name in enumerate(("q", "kv")):
            act.wait_ge(*a_.at(f"l{name}"))
            A(crs[n], crs[n], ACT.Exp, scale=-0.5).then_inc(*a_.mark(f"r{name}"))

    def mla_act(act):
        m, a_ = S("mla", "pe"), S("mla", "act")
        A = nc.scalar.activation
        act.wait_ge(*m.at("k"))
        for h in range(4):
            A(krot[h][0:64], bank[1 + h // 2][0:64, (h % 2) * T2:(h % 2 + 1) * T2], ACT.Copy).then_inc(*a_.mark(f"k{h}"))
        act.wait_ge(*m.at("v"))
        for j in range(2):
            A(vmla[:, j, :], bank[3 + j][:, :], ACT.Copy).then_inc(*a_.mark(f"v{j}"))
        attn_act(act, "mla", 4, False, 4, lambda n: gla_keys_act(act, GLA_PARTS[n]))

    def mla_norm_dve(dve):
        v, a_ = S("mla", "dve"), S("mla", "act")
        stt, tt = nc.vector.scalar_tensor_tensor, nc.vector.tensor_tensor
        dve.wait_ge(*a_.at("rkv"))
        for t in range(2):
            stt(cq[t], big[:, 12 + t, 0:T2], pv("mla_qn", t), crs[0], ALU.mult, ALU.mult).then_inc(*v.mark(f"cq{t}"))
        stt(ckv, big[:, 14, 0:T2], pv("mla_kvn"), crs[1], ALU.mult, ALU.mult).then_inc(*v.mark("ckv"))
        cos, sin = cn("cos", 96), cn("sin", 96)
        tt(krr[64:96], big[64:96, 15, 0:T2], cos[64:96], ALU.mult).then_inc(*v.mark("kr0"))
        tt(tmp96[64:96], big[64:96, 16, 0:T2], sin[64:96], ALU.mult).then_inc(*v.mark("kr1"))
        dve.wait_ge(*v.at("kr1"))
        for h in range(4):
            tt(krot[h][64:96], krr[64:96], tmp96[64:96], ALU.add).then_inc(*v.mark(f"kr{h + 2}"))

    def mla_dve(dve):
        m, v = S("mla", "pe"), S("mla", "dve")
        tt = nc.vector.tensor_tensor
        cos, sin = cn("cos", 96), cn("sin", 96)
        for h in range(4):
            bk = bank[(0, 5, 6, 7)[h]]
            dve.wait_ge(*m.at(f"q{h}"))
            tt(qrot[h], bk[0:96, 0:T2], cos, ALU.mult).then_inc(*v.mark(f"qa{h}"))
            dve.wait_ge(*v.at(f"q{h - 1}" if h else "kr5"))
            tt(tmp96, bk[0:96, T2:2 * T2], sin, ALU.mult).then_inc(*v.mark(f"qb{h}"))
            dve.wait_ge(*v.at(f"qb{h}"))
            tt(qrot[h], qrot[h], tmp96, ALU.add).then_inc(*v.mark(f"q{h}"))
        attn_dve(dve, "mla", 4, 96 ** -0.5, cn("mla_mask"), False, lambda n: gla_keys_dve(dve, GLA_PARTS[n]))
    con_eps = sb("con_eps", [P, 4])

    def sp_out(sp):
        o = out.rearrange("p (c t) -> p c t", t=T2)
        for m in range(KC):
            sp.wait_ge(*S("norm", "act").at(f"ln3_x{m}"))
            sp.dma_start(o[:, m, :], X(m)).then_inc(stored, 16)
        sp.wait_ge(stored, 16 * KC)

    eps_1 = con_eps[:, 0:1]
    eps_q = con_eps[:, 1:2]
    eps_ln = con_eps[:, 2:3]
    block = ctx.enter_context(nc.Block())
    xk = lambda k: y[:, k, :]

    def mix_ready(name):
        return lambda pe, k, i: pe.wait_ge(*S("norm", "dve").at(f"{name}_lo{k}"))

    def even_done(e):
        e.wait_ge(*S("swa", "pool").at("y3"))
        e.wait_ge(*S("swa", "act").at("out1"))

    def odd_done(e):
        e.wait_ge(*S("gla", "dve").at("o3"))
        e.wait_ge(*S("mla", "act").at("out1"))

    mix1 = lambda k: mix[:, k, :]
    mix2 = lambda k: mix[:, k, 0:T2]

    @block.sync
    def _(sp):
        sp_stream(sp)
        sp_out(sp)

    @block.gpsimd
    def _(pool):
        nc.gpsimd.memset(con_eps[:, 2:3], LN_EPS).then_inc(*S("init", "pool").mark("epsln"))
        nc.gpsimd.memset(con_eps[:, 0:1], RMS_EPS).then_inc(*S("init", "pool").mark("eps"))
        nc.gpsimd.memset(con_eps[:, 1:2], L2_EPS * GD).then_inc(*S("init", "pool").mark("epsq"))
        pre_pool(pool, "pre0")
        gdn_pool(pool)
        post_pool(pool, "post0")
        pre_pool(pool, "pre1")
        ffn_pool(pool, 0, G["up0"])
        post_pool(pool, "post1")
        pre_pool(pool, "pre2")
        ml_pool(pool)
        post_pool(pool, "post2")
        pre_pool(pool, "pre3")
        ffn_pool(pool, 1, G["up1"])
        post_pool(pool, "post3")
        x_pool(pool, "b2")
        even_pool(pool)
        x_pool(pool, "ln0")
        ffn_pool(pool, 2, G["up2"])
        x_pool(pool, "ln1")
        odd_pool(pool)
        x_pool(pool, "ln2")
        ffn_pool(pool, 3, G["up3"])

    @block.scalar
    def _(act):
        act.wait_ge(hs_loaded, 16)
        act.wait_ge(*S("init", "pool").at("epsq"))
        nc.scalar.preload_act_table_set(LN_EXP)
        pre_act(act, "pre0", G["pre0"], lambda act, m: None, lambda: [split_hi(act, n) for n in range(AHEAD)])
        act.wait_ge(loaded, 32)
        gdn_gates_act(act)
        nc.scalar.preload_act_table_set(SILU)
        gdn_in_act(act)
        nc.scalar.preload_act_table_set(LN_EXP)
        gdn_act(act)
        mix_act(act, "gdn", lambda k: big[:, 32 + k, :], 16, lambda e: e.wait_ge(*S("gdn", "dve").at("o3")))
        split_all(act, split_hi, "gdn_out")
        nc.scalar.preload_act_table_set(LN_EXP)
        post_act(act, "post0", G["post0"])
        nc.scalar.preload_act_table_set(LN_EXP)
        pre_act(act, "pre1", G["pre1"], lambda act, m: act.wait_ge(*added("post0", m)))
        nc.scalar.preload_act_table_set(SILU)
        ffn_act(act, 0, G["up0"])
        split_all(act, split_hi, "down0")
        nc.scalar.preload_act_table_set(LN_EXP)
        post_act(act, "post1", G["post1"])
        nc.scalar.preload_act_table_set(LN_EXP)
        pre_act(act, "pre2", G["pre2"], lambda act, m: act.wait_ge(*added("post1", m)))
        ml_gates_act(act)
        ml_in_act(act)
        nc.scalar.preload_act_table_set(LN_EXP)
        ml_act(act)
        mix_act(act, "ml", mix1, 8, lambda e: e.wait_ge(*S("ml", "dve").at("o31")))
        split_all(act, split_hi, "ml_out")
        nc.scalar.preload_act_table_set(LN_EXP)
        post_act(act, "post2", G["post2"])
        nc.scalar.preload_act_table_set(LN_EXP)
        pre_act(act, "pre3", G["pre3"], lambda act, m: act.wait_ge(*added("post2", m)))
        nc.scalar.preload_act_table_set(SILU)
        ffn_act(act, 1, G["up1"])
        split_all(act, split_hi, "down1")
        nc.scalar.preload_act_table_set(LN_EXP)
        post_act(act, "post3", G["post3"])
        x_act(act, "b2")
        in_act(act, "ev_in", [(ACT.Copy, 1.0)] * 18)
        nc.scalar.preload_act_table_set(LN_EXP)
        even_act(act)
        mix_act(act, "ev", mix2, 8, even_done)
        split_all(act, split_hi, "ev_out")
        nc.scalar.preload_act_table_set(LN_EXP)
        ln_act(act, 0, "ln_mix", 0)
        nc.scalar.preload_act_table_set(SILU)
        ffn_act(act, 2, G["up2"])
        split_all(act, split_hi, "down2")
        nc.scalar.preload_act_table_set(LN_EXP)
        ln_act(act, 1, "ln_ffn", 0)
        act.wait_ge(block_used, used_after("down2"))
        act.dma_start(MLAW, mla).then_inc(mla_loaded, 16)
        odd_gate_act(act)
        nc.scalar.preload_act_table_set(SILU)
        in_act(act, "od_in", [(ACT.Copy, 0.125)] * 2 + [(ACT.Copy, 1.0)] * 6 + [(ACT.Silu, 1.0)] * 4 + [(ACT.Copy, 1.0)] * 5)
        nc.scalar.preload_act_table_set(LN_EXP)
        odd_act(act)
        mix_act(act, "od", mix2, 8, odd_done)
        split_all(act, split_hi, "od_out")
        nc.scalar.preload_act_table_set(LN_EXP)
        ln_act(act, 2, "ln_mix", 1)
        nc.scalar.preload_act_table_set(SILU)
        ffn_act(act, 3, G["up3"])
        split_all(act, split_hi, "down3")
        nc.scalar.preload_act_table_set(LN_EXP)
        ln_act(act, 3, "ln_ffn", 1)

    @block.vector
    def _(dve):
        nc.vector.memset(rs[:, 0, 0:1], 0.0).then_inc(bank_free, 8)
        nc.vector.memset(rs[:, 1, 0:1], 0.0).then_inc(conv_taken, 8)
        dve.wait_ge(loaded, 32)
        for n in range(AHEAD):
            split_lo(dve, n)
        pre_dve(dve, "pre0", 0)
        gdn_in_dve(dve)
        gdn_dve(dve)
        mix_dve(dve, "gdn", lambda k: big[:, 32 + k, :], 16, lambda e: e.wait_ge(*S("gdn", "dve").at("o3")))
        split_all(dve, split_lo, "gdn_out")
        post_dve(dve, "post0", G["post0"], 1, used_after("gdn_out"))
        pre_dve(dve, "pre1", 2, after="post0")
        ffn_dve(dve, 0, G["up0"])
        split_all(dve, split_lo, "down0")
        post_dve(dve, "post1", G["post1"], 3, used_after("down0"))
        pre_dve(dve, "pre2", 4, after="post1")
        split_all(dve, split_lo, "ml_in", 0, 4)
        ml_gates_dve(dve)
        split_all(dve, split_lo, "ml_in", 8)
        ml_dve(dve)
        mix_dve(dve, "ml", mix1, 8, lambda e: e.wait_ge(*S("ml", "dve").at("o31")))
        split_all(dve, split_lo, "ml_out")
        post_dve(dve, "post2", G["post2"], 5, used_after("ml_out"))
        pre_dve(dve, "pre3", 6, after="post2")
        ffn_dve(dve, 1, G["up1"])
        split_all(dve, split_lo, "down1")
        post_dve(dve, "post3", G["post3"], 7, used_after("down1"))
        x_dve(dve, "b2")
        split_all(dve, split_lo, "ev_in")
        even_dve(dve)
        mix_dve(dve, "ev", mix2, 8, even_done)
        split_all(dve, split_lo, "ev_out")
        ln_dve(dve, 0, "ln_mix", 0, used_after("ev_out"))
        ffn_dve(dve, 2, G["up2"])
        split_all(dve, split_lo, "down2")
        ln_dve(dve, 1, "ln_ffn", 0, used_after("down2"))
        split_all(dve, split_lo, "od_in")
        odd_dve(dve)
        mix_dve(dve, "od", mix2, 8, odd_done)
        split_all(dve, split_lo, "od_out")
        ln_dve(dve, 2, "ln_mix", 1, used_after("od_out"))
        ffn_dve(dve, 3, G["up3"])
        split_all(dve, split_lo, "down3")
        ln_dve(dve, 3, "ln_ffn", 1, used_after("down3"))

    @block.tensor
    def _(pe):
        pe.wait_ge(loaded, 32)
        pre_pe(pe, "pre0", G["pre0"])
        gates_pe(pe, "gdn", G["gdn_g"], ((0, 16), (16, 16)), "gdn_gates", 32, T1, xk, lambda k: S("norm", "dve").at(f"pre0_x{k}"))
        pe_tiles(pe, "gdn_in", G["gdn_in"], "pre0")
        gdn_pe(pe)
        pe_wide(pe, "gdn_out", G["gdn_out"], mix_ready("gdn"))
        post_pe(pe, "post0", G["post0"])
        pre_pe(pe, "pre1", G["pre1"])
        pe_tiles(pe, "up0", G["up0"], "pre1")
        pe_wide(pe, "down0", G["down0"], ffn_ready(0))
        post_pe(pe, "post1", G["post1"])
        pre_pe(pe, "pre2", G["pre2"])
        gates_pe(pe, "ml", G["ml_g"], ((0, 4), (4, 4)), "ml_gates", 8, T1, xk, lambda k: S("norm", "dve").at(f"pre2_x{k}"))
        pe_tiles(pe, "ml_in", G["ml_in"], "pre2")
        ml_pe(pe)
        pe_wide(pe, "ml_out", G["ml_out"], mix_ready("ml"))
        post_pe(pe, "post2", G["post2"])
        pre_pe(pe, "pre3", G["pre3"])
        pe_tiles(pe, "up1", G["up1"], "pre3")
        pe_wide(pe, "down1", G["down1"], ffn_ready(1))
        post_pe(pe, "post3", G["post3"])
        pe_tiles(pe, "ev_in", G["ev_in"], "b2")
        even_pe(pe)
        pe_wide(pe, "ev_out", G["ev_out"], mix_ready("ev"))
        ln_pe(pe, 0)
        pe_tiles(pe, "up2", G["up2"], "ln0")
        pe_wide(pe, "down2", G["down2"], ffn_ready(2))
        ln_pe(pe, 1)
        gates_pe(pe, "od", G["od_g"], ((0, 16),), "g_low", 16, T2, X, lambda k: S("norm", "act").at(f"ln1_x{k}"))
        pe_tiles(pe, "od_in", G["od_in"], "ln1")
        odd_pe(pe)
        pe_wide(pe, "od_out", G["od_out"], mix_ready("od"))
        ln_pe(pe, 2)
        pe_tiles(pe, "up3", G["up3"], "ln2")
        pe_wide(pe, "down3", G["down3"], ffn_ready(3))
        ln_pe(pe, 3)
    ctx.close()

INPUTS = ["stream", "params", "consts", "mla", "hs"]


def kernel(**inputs):
    import concourse.bacc as bacc
    from concourse.bass_utils import run_bass_kernel_spmd

    table = {}
    for build_number in range(2):
        table["counted"] = build_number == 1
        nc = bacc.Bacc("TRN2", target_bir_lowering=False, num_devices=1)
        aps = [nc.dram_tensor(name, SHAPES[name], F32, kind="ExternalInput").ap() for name in INPUTS]
        out = nc.dram_tensor("y_out", (P, KC * T2), F32, kind="ExternalOutput").ap()
        build(nc, *aps, out, table)
    arrays = lay_out({name: np.asarray(v) for name, v in inputs.items()})
    result = run_bass_kernel_spmd(nc, [arrays], core_ids=[0]).results[0]["y_out"]
    return np.ascontiguousarray(result.reshape(P, KC, T2).transpose(2, 1, 0).reshape(1, T2, D))
```
